# Optimizing a Trainium2 kernel written in Bass

```python
import math
import jax
import jax.numpy as jnp
from jax import lax
import numpy as np

D_MODEL = 1024
BATCH = 1
SEQ = 256
DEPTH = 1

CHUNK = 64
EPS = 1e-6
A_HEADS = 16
A_HEAD_DIM = 64
A_WIDTH = A_HEADS * A_HEAD_DIM
LEFT_CHUNKS = 8
BAND = (LEFT_CHUNKS + 1) * CHUNK
REL_CLIP = 128
SSM_INNER = 2 * D_MODEL
SSM_HEAD_DIM = 64
SSM_HEADS = SSM_INNER // SSM_HEAD_DIM
SSM_GROUPS = 4
SSM_HPG = SSM_HEADS // SSM_GROUPS
SSM_STATE = 128
CONV_WIDTH = 4
CONV_CH = SSM_INNER + 2 * SSM_GROUPS * SSM_STATE
DT_MIN = 0.001
DT_MAX = 0.1
MEM_LEN = 256
X_HEADS = 4
X_HEAD_DIM = 256
X_WIDTH = X_HEADS * X_HEAD_DIM
N_BRANCH = 3
IN_SPLITS = (
    A_WIDTH,
    2 * A_WIDTH,
    3 * A_WIDTH,
    3 * A_WIDTH + SSM_INNER,
    3 * A_WIDTH + SSM_INNER + CONV_CH,
    3 * A_WIDTH + SSM_INNER + CONV_CH + SSM_HEADS,
    3 * A_WIDTH + SSM_INNER + CONV_CH + SSM_HEADS + X_WIDTH,
)
IN_COLS = 3 * A_WIDTH + SSM_INNER + CONV_CH + SSM_HEADS + X_WIDTH + N_BRANCH * D_MODEL
N_EXPERTS = 32
TOP_K = 4
D_EXPERT = D_MODEL
SWIGLU_LIMIT = 7.0
SWIGLU_ALPHA = 1.702
MOE_BLOCK = 128

kernel_name = "hybrid_chunk_attn_ssd_memxattn_moe"

def rms_norm(x, gain):
    xf = x.astype(jnp.float32)
    y = xf * lax.rsqrt(jnp.mean(xf * xf, axis=-1, keepdims=True) + EPS)
    return (y * gain.astype(jnp.float32)).astype(x.dtype)

def chunk_attention(q, k, v, q_gain, k_gain, rel_bias):
    b, s = q.shape[0], q.shape[1]
    n_chunks = s // CHUNK
    left = LEFT_CHUNKS * CHUNK
    q = rms_norm(q.reshape(b, s, A_HEADS, A_HEAD_DIM), q_gain)
    k = rms_norm(k.reshape(b, s, A_HEADS, A_HEAD_DIM), k_gain)
    v = v.reshape(b, s, A_HEADS, A_HEAD_DIM)
    kp = jnp.pad(k, ((0, 0), (left, 0), (0, 0), (0, 0)))
    vp = jnp.pad(v, ((0, 0), (left, 0), (0, 0), (0, 0)))
    rel = jnp.arange(CHUNK)[:, None] + left - jnp.arange(BAND)[None, :]
    bias = rel_bias[:, jnp.clip(rel, -REL_CLIP, REL_CLIP) + REL_CLIP].astype(jnp.float32)
    qc = q.reshape(b, n_chunks, CHUNK, A_HEADS, A_HEAD_DIM).transpose(1, 0, 2, 3, 4)
    scale = A_HEAD_DIM ** -0.5

    def one_chunk(args):
        qb, c = args
        start = c * CHUNK
        kb = lax.dynamic_slice_in_dim(kp, start, BAND, axis=1)
        vb = lax.dynamic_slice_in_dim(vp, start, BAND, axis=1)
        sc = jnp.einsum("bqhd,bkhd->bhqk", qb, kb).astype(jnp.float32) * scale + bias
        valid = (start - left + jnp.arange(BAND)) >= 0
        sc = jnp.where(valid, sc, -jnp.inf)
        p = jax.nn.softmax(sc, axis=-1).astype(vb.dtype)
        return jnp.einsum("bhqk,bkhd->bqhd", p, vb)

    out = lax.map(one_chunk, (qc, jnp.arange(n_chunks)))
    return out.transpose(1, 0, 2, 3, 4).reshape(b, s, A_WIDTH)

def segsum(a):
    n = a.shape[-1]
    cs = jnp.cumsum(a, axis=-1)
    diff = cs[..., :, None] - cs[..., None, :]
    return jnp.where(jnp.tril(jnp.ones((n, n), dtype=bool)), diff, -jnp.inf)

def mamba2_branch(z, xbc, dt_raw, conv_w, conv_b, dt_bias, a_log, d_skip, norm_gain):
    f32 = jnp.float32
    b, s = xbc.shape[0], xbc.shape[1]
    n_chunks = s // CHUNK
    xpad = jnp.pad(xbc, ((0, 0), (CONV_WIDTH - 1, 0), (0, 0)))
    conv = conv_b + xpad[:, 0:s] * conv_w[0]
    for i in range(1, CONV_WIDTH):
        conv = conv + xpad[:, i:i + s] * conv_w[i]
    xbc = jax.nn.silu(conv)
    xs, bm, cm = jnp.split(xbc, [SSM_INNER, SSM_INNER + SSM_GROUPS * SSM_STATE], axis=-1)
    x6 = xs.astype(f32).reshape(b, n_chunks, CHUNK, SSM_GROUPS, SSM_HPG, SSM_HEAD_DIM)
    bc = bm.astype(f32).reshape(b, n_chunks, CHUNK, SSM_GROUPS, SSM_STATE)
    cc = cm.astype(f32).reshape(b, n_chunks, CHUNK, SSM_GROUPS, SSM_STATE)
    dt = jax.nn.softplus(dt_raw.astype(f32) + dt_bias.astype(f32))
    dt5 = dt.reshape(b, n_chunks, CHUNK, SSM_GROUPS, SSM_HPG)
    a_head = -jnp.exp(a_log.astype(f32)).reshape(SSM_GROUPS, SSM_HPG)
    a = (dt5 * a_head).transpose(0, 1, 3, 4, 2)
    a_cs = jnp.cumsum(a, axis=-1)
    xdt = x6 * dt5[..., None]
    decay_in = jnp.exp(segsum(a))
    cb = jnp.einsum("bclgn,bcsgn->bcgls", cc, bc)
    y_diag = jnp.einsum("bcgls,bcgrls,bcsgrp->bclgrp", cb, decay_in, xdt)
    decay_to_end = jnp.exp(a_cs[..., -1:] - a_cs)
    states = jnp.einsum("bclgn,bcgrl,bclgrp->bcgrpn", bc, decay_to_end, xdt)
    chunk_decay = jnp.exp(a_cs[..., -1])

    def step(state, inp):
        dec, st = inp
        return dec[..., None, None] * state + st, state

    init = jnp.zeros((b, SSM_GROUPS, SSM_HPG, SSM_HEAD_DIM, SSM_STATE), f32)
    _, prev = lax.scan(step, init, (jnp.moveaxis(chunk_decay, 1, 0), jnp.moveaxis(states, 1, 0)))
    prev = jnp.moveaxis(prev, 0, 1)
    y_off = jnp.einsum("bclgn,bcgrpn,bcgrl->bclgrp", cc, prev, jnp.exp(a_cs))
    y = (y_diag + y_off).reshape(b, s, SSM_HEADS, SSM_HEAD_DIM)
    y = y + d_skip.astype(f32)[:, None] * xs.astype(f32).reshape(b, s, SSM_HEADS, SSM_HEAD_DIM)
    yz = y.reshape(b, s, SSM_INNER) * jax.nn.silu(z.astype(f32))
    yz = rms_norm(yz.reshape(b, s, SSM_GROUPS, SSM_INNER // SSM_GROUPS),
                  norm_gain.reshape(SSM_GROUPS, SSM_INNER // SSM_GROUPS))
    return yz.reshape(b, s, SSM_INNER).astype(z.dtype)

def memory_attention(q, mem, mem_gain, w_mem_kv, q_gain, k_gain):
    b, s = q.shape[0], q.shape[1]
    m = mem.shape[1]
    kv = rms_norm(mem, mem_gain) @ w_mem_kv
    k, v = jnp.split(kv, 2, axis=-1)
    q = rms_norm(q.reshape(b, s, X_HEADS, X_HEAD_DIM), q_gain)
    k = rms_norm(k.reshape(b, m, X_HEADS, X_HEAD_DIM), k_gain)
    v = v.reshape(b, m, X_HEADS, X_HEAD_DIM)
    sc = jnp.einsum("bshd,bmhd->bhsm", q, k).astype(jnp.float32) * (X_HEAD_DIM ** -0.5)
    p = jax.nn.softmax(sc, axis=-1).astype(v.dtype)
    return jnp.einsum("bhsm,bmhd->bshd", p, v).reshape(b, s, X_WIDTH)

def moe_ffn(h, w_router, b_router, w_gate, b_gate, w_up, b_up, w_down, b_down):
    b, s, d = h.shape
    t = b * s
    xt = h.reshape(t, d)
    logits = (xt @ w_router + b_router).astype(jnp.float32)
    top_val, top_idx = lax.top_k(logits, TOP_K)
    wts = jax.nn.softmax(top_val, axis=-1)
    n_assign = t * TOP_K
    e_flat = top_idx.reshape(-1)
    tok_flat = jnp.arange(n_assign, dtype=jnp.int32) // TOP_K
    w_flat = wts.reshape(-1)
    order = jnp.argsort(e_flat)
    e_s, tok_s, w_s = e_flat[order], tok_flat[order], w_flat[order]
    counts = jnp.bincount(e_flat, length=N_EXPERTS)
    starts = jnp.cumsum(counts) - counts
    padded = (counts + MOE_BLOCK - 1) // MOE_BLOCK * MOE_BLOCK
    pad_ends = jnp.cumsum(padded)
    pad_starts = pad_ends - padded
    dest = pad_starts[e_s] + jnp.arange(n_assign, dtype=jnp.int32) - starts[e_s]
    n_rows = n_assign + N_EXPERTS * MOE_BLOCK
    row_tok = jnp.full((n_rows,), t, jnp.int32).at[dest].set(tok_s)
    row_w = jnp.zeros((n_rows,), jnp.float32).at[dest].set(w_s)
    n_blocks = n_rows // MOE_BLOCK
    block_start = jnp.arange(n_blocks, dtype=jnp.int32) * MOE_BLOCK
    block_exp = jnp.minimum(jnp.searchsorted(pad_ends, block_start, side="right"), N_EXPERTS - 1)
    x_pad = jnp.concatenate([xt, jnp.zeros((1, d), xt.dtype)], axis=0)
    xb = x_pad[row_tok].reshape(n_blocks, MOE_BLOCK, d)

    def expert_block(args):
        xblk, e = args
        g = xblk @ w_gate[e] + b_gate[e]
        u = xblk @ w_up[e] + b_up[e]
        g = jnp.minimum(g, SWIGLU_LIMIT)
        u = jnp.clip(u, -SWIGLU_LIMIT, SWIGLU_LIMIT)
        act = (u + 1.0) * g * jax.nn.sigmoid(SWIGLU_ALPHA * g)
        return act @ w_down[e] + b_down[e]

    yb = lax.map(expert_block, (xb, block_exp)).reshape(n_rows, d)
    y = jax.ops.segment_sum(yb * row_w[:, None].astype(yb.dtype), row_tok, num_segments=t + 1)[:t]
    return y.reshape(b, s, d)

def setup_inputs(seed: int = 0) -> dict:
    key = jax.random.key(seed)
    ks = jax.random.split(key, 32)
    f32 = jnp.float32
    L = DEPTH

    def normal(k, shape, scale):
        return jax.random.normal(k, shape, f32) * scale

    def gain(k, shape):
        return 1.0 + 0.05 * jax.random.normal(k, shape, f32)

    dt = jnp.exp(jax.random.uniform(ks[8], (L, SSM_HEADS), f32, math.log(DT_MIN), math.log(DT_MAX)))
    dt_bias = dt + jnp.log(-jnp.expm1(-dt))
    a_log = jnp.log(jax.random.uniform(ks[9], (L, SSM_HEADS), f32, 1.0, 16.0))
    return {
        "x": normal(ks[0], (BATCH, SEQ, D_MODEL), 1.0),
        "mem": normal(ks[1], (BATCH, MEM_LEN, D_MODEL), 1.0),
        "norm_mix": gain(ks[2], (L, D_MODEL)),
        "w_in": normal(ks[3], (L, D_MODEL, IN_COLS), D_MODEL ** -0.5),
        "a_q_gain": gain(ks[4], (L, A_HEAD_DIM)),
        "a_k_gain": gain(ks[5], (L, A_HEAD_DIM)),
        "a_rel_bias": normal(ks[6], (L, A_HEADS, 2 * REL_CLIP + 1), 0.1),
        "conv_w": normal(ks[7], (L, CONV_WIDTH, CONV_CH), CONV_WIDTH ** -0.5),
        "conv_b": normal(ks[10], (L, CONV_CH), 0.01),
        "dt_bias": dt_bias,
        "a_log": a_log,
        "d_skip": gain(ks[11], (L, SSM_HEADS)),
        "ssm_norm": gain(ks[12], (L, SSM_INNER)),
        "norm_mem": gain(ks[13], (L, D_MODEL)),
        "w_mem_kv": normal(ks[14], (L, D_MODEL, 2 * X_WIDTH), D_MODEL ** -0.5),
        "x_q_gain": gain(ks[15], (L, X_HEAD_DIM)),
        "x_k_gain": gain(ks[16], (L, X_HEAD_DIM)),
        "w_br_a": normal(ks[17], (L, A_WIDTH, D_MODEL), A_WIDTH ** -0.5),
        "w_br_b": normal(ks[18], (L, SSM_INNER, D_MODEL), SSM_INNER ** -0.5),
        "w_br_c": normal(ks[19], (L, X_WIDTH, D_MODEL), X_WIDTH ** -0.5),
        "w_out": normal(ks[20], (L, D_MODEL, D_MODEL), D_MODEL ** -0.5),
        "norm_ffn": gain(ks[21], (L, D_MODEL)),
        "w_router": normal(ks[22], (L, D_MODEL, N_EXPERTS), D_MODEL ** -0.5),
        "b_router": normal(ks[23], (L, N_EXPERTS), 0.01),
        "w_gate": normal(ks[24], (L, N_EXPERTS, D_MODEL, D_EXPERT), D_MODEL ** -0.5),
        "b_gate": normal(ks[25], (L, N_EXPERTS, D_EXPERT), 0.01),
        "w_up": normal(ks[26], (L, N_EXPERTS, D_MODEL, D_EXPERT), D_MODEL ** -0.5),
        "b_up": normal(ks[27], (L, N_EXPERTS, D_EXPERT), 0.01),
        "w_down": normal(ks[28], (L, N_EXPERTS, D_EXPERT, D_MODEL), D_EXPERT ** -0.5),
        "b_down": normal(ks[29], (L, N_EXPERTS, D_MODEL), 0.01),
    }

def reference(x, mem, norm_mix, w_in, a_q_gain, a_k_gain, a_rel_bias, conv_w, conv_b, dt_bias, a_log,
              d_skip, ssm_norm, norm_mem, w_mem_kv, x_q_gain, x_k_gain, w_br_a, w_br_b, w_br_c, w_out,
              norm_ffn, w_router, b_router, w_gate, b_gate, w_up, b_up, w_down, b_down):
    b, s, d = x.shape
    for l in range(DEPTH):
        h = rms_norm(x, norm_mix[l])
        proj = h @ w_in[l]
        q_a, k_a, v_a, z, xbc, dt_raw, q_x, gate_logits = jnp.split(proj, IN_SPLITS, axis=-1)
        y_a = chunk_attention(q_a, k_a, v_a, a_q_gain[l], a_k_gain[l], a_rel_bias[l])
        y_b = mamba2_branch(z, xbc, dt_raw, conv_w[l], conv_b[l], dt_bias[l], a_log[l], d_skip[l], ssm_norm[l])
        y_c = memory_attention(q_x, mem, norm_mem[l], w_mem_kv[l], x_q_gain[l], x_k_gain[l])
        gates = jax.nn.sigmoid(gate_logits.astype(jnp.float32)).astype(x.dtype).reshape(b, s, N_BRANCH, d)
        merged = (gates[:, :, 0] * (y_a @ w_br_a[l])
                  + gates[:, :, 1] * (y_b @ w_br_b[l])
                  + gates[:, :, 2] * (y_c @ w_br_c[l]))
        x = x + merged @ w_out[l]
        x = x + moe_ffn(rms_norm(x, norm_ffn[l]), w_router[l], b_router[l], w_gate[l], b_gate[l],
                        w_up[l], b_up[l], w_down[l], b_down[l])
    return x


_drawn_inputs = setup_inputs


def setup_inputs(seed=0):
    import zlib

    import numpy as np

    out = dict(_drawn_inputs(seed))
    spreads = {}
    factors = {'a_q_gain': 8.0,
     'a_k_gain': 4.436,
     'a_rel_bias': 12.823,
     'conv_b': 12.242,
     'norm_mem': 3.928,
     'x_q_gain': 8.0,
     'x_k_gain': 6.955,
     'b_router': 8.968,
     'b_gate': 27.382,
     'b_up': 39.954,
     'b_down': 26.252,
     'd_skip': 3.694,
     'ssm_norm': 3.211}
    for name, (base, spread) in spreads.items():
        noise = np.random.default_rng([zlib.crc32(name.encode()), seed]).standard_normal(out[name].shape)
        drawn = base * np.exp(spread * noise) if base else spread * noise
        out[name] = jnp.asarray(drawn.astype(out[name].dtype))
    for name, factor in factors.items():
        out[name] = (out[name] * factor).astype(out[name].dtype)
    return out
```

```python
from contextlib import ExitStack

import concourse.bass as bass
from concourse import mybir

P = 128
F32 = mybir.dt.float32
I32 = mybir.dt.int32
U32 = mybir.dt.uint32
ALU = mybir.AluOpType
ACT = mybir.ActivationFunctionType
AX = mybir.AxisListType.X

EPS = 1e-6
D = 1024
T = 256
TT = T // P
KC = D // P
NB = 512
A_HEADS, A_DIM = 16, 64
X_HEADS, X_DIM = 4, 256
MEM = 256
CHUNK = 64
REL_CLIP = 128
INNER = 2048
GROUPS, STATE, SSM_HEADS, SSM_DIM = 4, 128, 32, 64
GW = INNER // GROUPS
CONV_CH = INNER + 2 * GROUPS * STATE
CONV_T = CONV_CH // P
TAPS = 4
EXPERTS, TOP_K = 32, 4
BLK = 64
PASSES = T // BLK
LIMIT, ALPHA = 7.0, 1.702
MASKED = -1e30
SKEW = 384

Q0, K0, V0, Z0 = 0, D, 2 * D, 3 * D
XBC0 = Z0 + INNER
DT0 = XBC0 + CONV_CH
QX0 = DT0 + SSM_HEADS
GATE0 = QX0 + D

BLOCKS = ([("mk", i) for i in range(2)] + [("mv", i) for i in range(2)] + [("qx", i) for i in range(2)]
          + [("q", i) for i in range(2)] + [("k", i) for i in range(2)] + [("v", i) for i in range(2)]
          + [("xbc", i) for i in range(6)] + [("gc", i) for i in range(2)] + [("bc", i) for i in range(2)]
          + [("z", i) for i in range(4)]
          + [("ga", i) for i in range(2)] + [("ba", i) for i in range(2)]
          + [("gb", i) for i in range(2)] + [("bb", i) for i in range(4)] + [("wo", i) for i in range(2)])
BLOCK_AT = {b: n for n, b in enumerate(BLOCKS)}
RING = 4


def block_groups():
    out = []
    for name, i in BLOCKS:
        if name == "bb":
            if i % 2 == 1:
                out += [(name, i // 2, h) for h in range(2)]
        else:
            out += [(name, i, h) for h in range(2)]
    return out


GEMM = block_groups()
GEMM_AT = {g: n for n, g in enumerate(GEMM)}


def schedule():
    s = [("memT",), ("hT",)]

    def gemm(name, i, h):
        s.append(("gemm", name, i, h))

    def block(name, i):
        gemm(name, i, 0)
        gemm(name, i, 1)

    heads = [("x", h) for h in range(X_HEADS)] + [("a", h) for h in range(A_HEADS)]

    def attend(n):
        for stage, m in (("scores", n), ("probsT", n - 1), ("values", n - 2), ("soften", n)):
            if lo <= m < hi:
                s.append((stage, m) + heads[m])

    block("mk", 0), block("mk", 1)
    s.append(("square", "kx"))
    block("mv", 0)
    s.append(("headnorm", "kx"))
    block("mv", 1)
    s.append(("headT", "kx"))
    block("qx", 0), block("qx", 1)
    s.append(("square", "qx"))
    gemm("q", 0, 0)
    s.append(("headnorm", "qx"))
    gemm("q", 0, 1)
    s.append(("headT", "qx"))
    block("q", 1)
    s.append(("square", "q"))
    lo, hi = 0, X_HEADS
    slot = 0
    for name in ("k", "v"):
        for i in range(2):
            for h in range(2):
                gemm(name, i, h)
                if name == "k" and (i, h) == (0, 0):
                    s.append(("headnorm", "q"))
                if name == "v" and (i, h) == (0, 1):
                    s.append(("headT", "q"))
                attend(slot)
                slot += 1
        if name == "k":
            s.append(("square", "k"))
            s.append(("headnorm", "k"))
    s.append(("headT", "k"))
    lo, hi = X_HEADS, X_HEADS + A_HEADS
    slot = X_HEADS
    conv = 0
    for i in range(6):
        for h in range(2):
            gemm("xbc", i, h)
            if conv >= 1:
                s.append(("silu", conv - 1))
            if conv >= 2 and conv - 2 < INNER // P // 2:
                s.append(("xsT", conv - 2))
            s.append(("conv", conv))
            conv += 1
            attend(slot)
            slot += 1
    s.append(("silu", conv - 1))
    s.append(("dt",))
    for name in ("gc", "bc"):
        for i in range(2):
            for h in range(2):
                gemm(name, i, h)
                attend(slot)
                slot += 1
                if (name, i, h) == ("gc", 1, 0):
                    s.append(("decay",))
    s.append(("xdt",))
    for u in range(GROUPS * TT):
        g, t = u // TT, u % TT
        if t == 0:
            s.append(("cb", g))
        s.append(("spread", u, g, t))
        gemm("z", g, t)
        s.append(("weigh", u, g, t))
        s.append(("ssm", u, g, t))
    gemm("ga", 0, 0)
    s.append(("ynorm",))
    gemm("ga", 0, 1)
    s.append(("yT",))
    block("ga", 1), block("ba", 0), block("ba", 1)
    block("gb", 0), block("gb", 1)
    for i in range(4):
        s.append(("gemmb", i))
    s.append(("mergedT",))
    block("wo", 0), block("wo", 1)
    return s


SCHED = schedule()
MISC_GROUPS = {"memT": 4, "hT": 4, "headT": 4, "scores": 1, "probsT": 1, "values": 1, "xsT": 1, "dt": 1, "cb": 1,
               "yT": 8, "mergedT": 4}


def misc_index():
    at, n = {}, 0
    for step in SCHED:
        at[step] = n
        n += MISC_GROUPS.get(step[0], 0)
        if step[0] == "ssm":
            n += 1 + step[3]
    at["h2T"], at["logits"], at["wT"], at["places"], at["end"] = n, n + 4, n + 5, n + 6, n + 7
    return at


MISC_AT = misc_index()
N_UNITS = GROUPS * TT


def hybrid_block_kernel(nc, x, mem, g_mix, w_in, w_dt, a_gains, rel_rev, conv_w, conv_b, dt_bias, a_log, d_skip,
                        g_ssm, g_mem, w_mem_kv, x_gains, w_br_a, w_br_b, w_br_c, w_out, norm_ffn, w_router,
                        b_router, w_gate, b_gate, w_up, b_up, w_down, b_down, bias_dram, out):
    with ExitStack() as ctx:
        def sb(name, shape, dt=F32):
            return ctx.enter_context(nc.sbuf_tensor(name, shape, dt))

        sems = {}

        def sem(name):
            if name not in sems:
                sems[name] = ctx.enter_context(nc.semaphore(name))
            return sems[name]

        SLOT = KC * NB
        ring = sb("ring", [P, RING, SLOT])
        HALF = SLOT // 2
        S = sb("S", [P, 14, HALF])
        x_sb = S[:, 0].rearrange("p (t d) -> p t d", t=TT)
        hT = S[:, 1].rearrange("p (c t) -> p c t", c=KC)
        mem_sb = S[:, 2].rearrange("p (t d) -> p t d", t=TT)
        memT = S[:, 3].rearrange("p (c t) -> p c t", c=KC)
        kx_raw = S[:, 4].rearrange("p (t d) -> p t d", t=TT)
        squares = S[:, 5].rearrange("p (t d) -> p t d", t=TT)
        vx = S[:, 6].rearrange("p (t d) -> p t d", t=TT)
        xn = S[:, 7].rearrange("p (t d) -> p t d", t=TT)
        qx_raw = S[:, 7].rearrange("p (t d) -> p t d", t=TT)
        kxT = S[:, 2].rearrange("p (c t) -> p c t", c=KC)
        qxT = S[:, 3].rearrange("p (c t) -> p c t", c=KC)
        q_raw = S[:, 8].rearrange("p (t d) -> p t d", t=TT)
        k_raw = S[:, 9].rearrange("p (t d) -> p t d", t=TT)
        v_sb = S[:, 10].rearrange("p (t d) -> p t d", t=TT)
        ycT = S[:, 4].rearrange("p (c t) -> p c t", c=KC)
        kT = S[:, 7].rearrange("p (c t) -> p c t", c=KC)
        qz = S[:, 12:14].rearrange("p a (h t) -> p (a h) t", t=T)
        rel_sb = S[0:A_HEADS, 12, 0:512]
        bias = [S[:, 6].rearrange("p (h k) -> p h k", k=T), S[:, 11].rearrange("p (h k) -> p h k", k=T)]
        yaT = S[:, 9].rearrange("p (c t) -> p c t", c=KC)
        xs = [S[:, 2], S[:, 3]]
        bcT = S[:, 8].rearrange("p (c t) -> p c t", c=2 * GROUPS)
        conv_acc = S[:, 5, 0:1024].rearrange("p (b j t) -> p b j t", b=2, j=2)
        conv_out = S[:, 5, 1024:2048].rearrange("p (b j t) -> p b j t", b=2, j=2)
        zbuf = S[:, 12, 0:2 * NB].rearrange("p (b n) -> p b n", b=2)
        sq_junk, y_off = S[:, 12, 2 * NB:3 * NB], S[:, 12, 3 * NB:4 * NB]
        xdt = [S[:, 7], S[:, 10]]
        fx = S[:, 11]
        merged = S[:, 5].rearrange("p (t d) -> p t d", t=TT)
        sig = S[:, 6].rearrange("p (t d) -> p t d", t=TT)
        ybT = S[:, 12:14].rearrange("p a (c t) -> p (a c) t", t=T)
        mergedT = S[:, 1].rearrange("p (c t) -> p c t", c=KC)
        h2 = S[:, 8].rearrange("p (t d) -> p t d", t=TT)
        h2T = S[:, 9].rearrange("p (c t) -> p c t", c=KC)
        gain2 = S[:, 4, 0:D]
        sq2 = S[:, 7].rearrange("p (t d) -> p t d", t=TT)

        def expert_slot(k):
            if k < RING:
                flat = ring[:, (len(BLOCKS) + k) % RING]
            else:
                flat = S[:, (10, 2)[k - RING]:(12, 4)[k - RING]].rearrange("p a f -> p (a f)")
            return flat.rearrange("p (c n) -> p c n", c=KC // 2)

        eslots = [expert_slot(k) for k in range(6)]
        gate_w, up_w, down_w = [eslots[0], eslots[2]], [eslots[1], eslots[3]], [eslots[4], eslots[5]]

        xgT = S[:, 12, 0:512].rearrange("p (c j) -> p c j", c=KC)
        g_sb, u_sb = S[:, 12, 512:1024], S[:, 12, 1024:1536]
        sg_sb, gu_sb = S[:, 12, 1536:2048], S[:, 13, 0:512]
        act_sb, actT = S[:, 13, 512:1024], S[:, 13, 1024:1536].rearrange("p (c j) -> p c j", c=4)
        yb = S[:, 13, 1536:2048]
        bias_gu = S[:, 6]
        bias_d = S[:, 5, 0:D]
        pick = S[:, 5, 1024:1024 + BLK]
        hot = S[:, 5, 1088:1088 + TT * BLK].rearrange("p (t j) -> p t j", t=TT)
        hot_w = S[:, 5, 1216:1216 + TT * 2 * BLK].rearrange("p (t r j) -> p t r j", t=TT, r=2)
        hot_wT = S[:, 5, 1472:1472 + 512].rearrange("p (h t j) -> p h t j", h=2, t=TT)
        NPAD = PASSES * EXPERTS + 1
        place4 = S[:, 1, 0:TT * NPAD].rearrange("p (t i) -> p t i", t=TT)
        weight4 = S[:, 1, 320:320 + TT * PASSES * EXPERTS].rearrange("p (t i) -> p t i", t=TT)
        picks = S[:, 1, 640:640 + PASSES * EXPERTS]
        wT = S[:, 1, 800:800 + T]
        y_out = S[:, 9].rearrange("p (t d) -> p t d", t=TT)

        ident = sb("ident", [P, P])
        upto = sb("upto", [P, P])
        after = sb("after", [P, P])
        ones = sb("ones", [P, P])
        iota_i = sb("iota_i", [P, BLK], I32)
        iota_j = sb("iota_j", [P, BLK])
        iota2 = sb("iota2", [P, 2, BLK])
        steps_b = sb("steps_b", [P, PASSES])
        gm_sb = sb("gm_sb", [P, KC])
        gmem_sb = sb("gmem_sb", [P, KC])
        gssm_sb = sb("gssm_sb", [P, INNER // P])
        ag_sb = sb("ag_sb", [P, 2])
        xg_sb = sb("xg_sb", [P, 4])
        cw_sb = sb("cw_sb", [P, CONV_T, TAPS])
        cb_sb = sb("cb_sb", [P, CONV_T])
        head_rows = sb("head_rows", [P, 4, SSM_HEADS])
        wdt_sb = sb("wdt_sb", [P, KC, SSM_HEADS])
        wr_sb = sb("wr_sb", [P, KC, EXPERTS])
        craw = sb("craw", [P, 2, 2, T + TAPS])
        work = sb("work", [P, 4, NB])
        tmp = sb("tmp", [P, 2, NB])
        cbm = sb("cbm", [P, 2, 384])
        stat = sb("stat", [P, 256])
        ss_x, rs_x = stat[:, 0:4], stat[:, 4:8]
        ss_h = stat[:, 8:40]
        mx3, mx1 = stat[:, 40:43], stat[:, 43:45]
        sm1, rc1 = stat[:, 45:47], stat[:, 47:49]
        ss_y = stat[:, 49:57]
        ss_2 = stat[:, 57:59]
        rs_2 = stat[:, 59:61]
        npass_f, cmax = stat[:, 61:62], stat[:, 62:63]
        over = stat[:, 64:68]
        mx8 = stat[:, 72:88].rearrange("p (t k) -> p t k", t=TT)
        idxf = stat[:, 88:104].rearrange("p (t k) -> p t k", t=TT)
        e4 = stat[:, 104:112].rearrange("p (t k) -> p t k", t=TT)
        s4 = stat[:, 112:114]
        root_in, root_out = stat[:, 128:160], stat[:, 160:192]
        idx8 = sb("idx8", [P, TT, 8], U32)
        npass_i = sb("npass_i", [1, 1], I32)
        dtw = sb("dtw", [P, 6, TT * SSM_HEADS])
        dt_sb = dtw[:, 4].rearrange("p (t h) -> p t h", t=TT)
        a_sb = dtw[:, 5].rearrange("p (t h) -> p t h", t=TT)
        a_head = sb("a_head", [P, SSM_HEADS])
        decays = sb("decays", [P, 2, SSM_HEADS])
        rt = sb("rt", [P, 4, TT * EXPERTS])
        logits = rt[:, 0].rearrange("p (t e) -> p t e", t=TT)
        wts = rt[:, 1].rearrange("p (t e) -> p t e", t=TT)
        part = rt[:, 2].rearrange("p (t e) -> p t e", t=TT)
        chosen = rt[:, 3].rearrange("p (t e) -> p t e", t=TT)

        ps = ctx.enter_context(nc.psum_tensor("ps", [P, 8, NB], F32))
        GEMM_BANKS, EXP_BANKS, MISC_BANKS = (0, 1, 2), (3, 7), (4, 5, 6)
        ACC, G_BANK, U_BANK, X_BANK, D_BANK = (0, 1, 2, 3), 4, 5, 6, 7

        gemm_ready, gemm_taken = sem("gemm_ready"), sem("gemm_taken")
        misc_ready, misc_taken = sem("misc_ready"), sem("misc_taken")
        exp_ready, exp_taken = sem("exp_ready"), sem("exp_taken")
        landed = [sem(f"block_landed{k}") for k in range(RING)]
        e_landed = [sem(f"expert_landed{k}") for k in range(6)]
        e_used = [sem(f"{n}_used") for n in ("gate_up0", "gate_up1", "down0", "down1")]
        MISC_END = MISC_AT["end"]
        GEMM_END = len(GEMM)

        def weight_src(name, i):
            def rows(w, c0):
                return w.rearrange("(c p) n -> p c n", p=P)[:, :, c0:c0 + NB]
            if name in ("mk", "mv"):
                return rows(w_mem_kv, (0 if name == "mk" else D) + i * NB)
            if name in ("bc", "ba", "wo"):
                return rows({"bc": w_br_c, "ba": w_br_a, "wo": w_out}[name], i * NB)
            if name == "bb":
                return w_br_b[(i % 2) * D:(i % 2 + 1) * D].rearrange("(c p) n -> p c n", p=P)[
                    :, :, (i // 2) * NB:(i // 2 + 1) * NB]
            c0 = {"q": Q0, "k": K0, "v": V0, "z": Z0, "xbc": XBC0, "qx": QX0,
                  "ga": GATE0, "gb": GATE0 + D, "gc": GATE0 + 2 * D}[name]
            return rows(w_in, c0 + i * NB)

        def expert_src(k, e):
            w = (w_gate, w_up, w_gate, w_up, w_down, w_down)[k]
            half = (0, 0, 1, 1, 0, 1)[k]
            return w[e].rearrange("(h c p) n -> h p c n", h=2, p=P)[half]

        block = ctx.enter_context(nc.Block())

        @block.sync
        def _(sp):
            def block_used(n):
                name, i = BLOCKS[n]
                if name == "bb" and i % 2 == 0:
                    sp.wait_ge(sem("half_summed"), i // 2 + 1)
                elif name == "bb":
                    sp.wait_ge(gemm_ready, GEMM_AT[(name, i // 2, 1)] + 1)
                else:
                    sp.wait_ge(gemm_ready, GEMM_AT[(name, i, 1)] + 1)

            def load(n):
                name, i = BLOCKS[n]
                if n >= RING:
                    block_used(n - RING)
                dst = ring[:, n % RING].rearrange("p (c n) -> p c n", c=KC)
                sp.dma_start(dst, weight_src(name, i)).then_inc(landed[n % RING], 16)

            sp.dma_start(mem_sb, mem.rearrange("a (t p) d -> p (a t) d", p=P)).then_inc(sem("mem_landed"), 16)
            sp.dma_start(x_sb, x.rearrange("a (t p) d -> p (a t) d", p=P)).then_inc(sem("x_landed"), 16)
            load(0)
            load(1)
            sp.wait_ge(sem("rel_edge"), 2)
            skewed = bass.AP(tensor=bias_dram.tensor, offset=0, ap=[[P * (SKEW + 1), A_HEADS], [SKEW + 1, P], [1, SKEW]])
            sp.dma_start(skewed, rel_sb[:, 0:SKEW].unsqueeze(1).to_broadcast([A_HEADS, P, SKEW])).then_inc(sem("rel_stored"), 16)
            sp.wait_ge(sem("rel_stored"), 16)
            load(2)
            load(3)
            for n in range(RING, len(BLOCKS)):
                if BLOCKS[n] == ("xbc", 0):
                    sp.wait_ge(misc_ready, MISC_AT[("values", X_HEADS - 1, "x", X_HEADS - 1)] + 1)
                    for j in range(2):
                        src = bass.AP(tensor=bias_dram.tensor, offset=8 * j * P * (SKEW + 1) + 127,
                                      ap=[[SKEW, P], [P * (SKEW + 1), 8], [1, T]])
                        sp.dma_start(bias[j], src).then_inc(sem("bias_landed"), 16)
                if BLOCKS[n] == ("gb", 0):
                    sp.wait_ge(misc_ready, MISC_AT[("yT",)] + 8)
                    for k in (4, 5):
                        sp.dma_start(eslots[k], expert_src(k, 0)).then_inc(e_landed[k], 16)
                load(n)
            sp.wait_ge(gemm_ready, GEMM_AT[("bc", 1, 1)] + 1)
            sp.dma_start(gain2, norm_ffn.partition_broadcast(P)).then_inc(sem("gain2_landed"), 16)
            for k in range(4):
                block_used(len(BLOCKS) + k - RING)
                sp.dma_start(eslots[k], expert_src(k, 0)).then_inc(e_landed[k], 16)
            sp.wait_ge(sem("bias_rows_zero"), 2)
            sp.dma_start(bias_gu[0:EXPERTS, 0:D], b_gate).then_inc(sem("bias_rows_landed"), 16)
            sp.dma_start(bias_gu[0:EXPERTS, D:2 * D], b_up).then_inc(sem("bias_rows_landed"), 16)
            sp.dma_start(bias_d[0:EXPERTS, :], b_down).then_inc(sem("bias_rows_landed"), 16)

            def expert_loads(i, e):
                for k in range(6):
                    sp.wait_ge(e_used[(0, 0, 1, 1, 2, 3)[k]], i)
                    sp.dma_start(eslots[k], expert_src(k, e)).then_inc(e_landed[k], 16)

            with sp.Fori(1, EXPERTS) as e:
                expert_loads(e, e)
            sp.wait_ge(sem("passes_known"), 1)
            n_pass = sp.value_load(npass_i[0:1, 0:1], min_val=1, max_val=PASSES)
            with sp.If(n_pass > 1):
                with sp.Fori(1, n_pass) as b:
                    with sp.Fori(0, EXPERTS) as e:
                        expert_loads(b * EXPERTS + e, e)
            for t in range(TT):
                sp.wait_ge(sem("y_ready"), 2 * t + 2)
                sp.dma_start(out.rearrange("a (t p) d -> t p (a d)", p=P)[t], y_out[:, t]).then_inc(sem("y_stored"), 16)
            sp.wait_ge(sem("y_stored"), 16 * TT)

        @block.gpsimd
        def _(pool):
            small = sem("small_landed")
            pool.dma_start(gm_sb[:], g_mix).then_inc(small, 16)
            pool.dma_start(gmem_sb[:], g_mem).then_inc(small, 16)
            pool.dma_start(gssm_sb[:], g_ssm).then_inc(small, 16)
            pool.dma_start(ag_sb[:], a_gains).then_inc(small, 16)
            pool.dma_start(xg_sb[:], x_gains).then_inc(small, 16)
            pool.dma_start(cw_sb[:], conv_w).then_inc(small, 16)
            pool.dma_start(cb_sb[:], conv_b).then_inc(small, 16)
            pool.dma_start(wdt_sb[:], w_dt.rearrange("(c p) n -> p c n", p=P)).then_inc(small, 16)
            pool.dma_start(wr_sb[:], w_router.rearrange("(c p) n -> p c n", p=P)).then_inc(small, 16)
            for j, row in enumerate((dt_bias, a_log, d_skip, b_router)):
                pool.dma_start(head_rows[:, j], row.partition_broadcast(P)).then_inc(small, 16)
            pool.dma_start(rel_sb[:, 127:384], rel_rev).then_inc(sem("rel_landed"), 16)
            pool.memset(ones[:], 1.0).then_inc(sem("ones_set"), 1)
            pool.wait_ge(sem("ones_set"), 1)
            pool.affine_select(out=ident[:], in_=ones[:], compare_op=ALU.is_equal, fill=0.0, base=0,
                               pattern=[[-1, P]], channel_multiplier=1).then_inc(sem("masks"), 1)
            pool.affine_select(out=upto[:], in_=ones[:], compare_op=ALU.is_ge, fill=0.0, base=0,
                               pattern=[[1, P]], channel_multiplier=-1).then_inc(sem("masks"), 1)
            pool.affine_select(out=after[:], in_=ones[:], compare_op=ALU.is_ge, fill=0.0, base=-1,
                               pattern=[[-1, P]], channel_multiplier=1).then_inc(sem("masks"), 1)
            pool.iota(iota_i[:], pattern=[[1, BLK]], base=0, channel_multiplier=0).then_inc(sem("iota"), 1)
            pool.memset(craw[:], 0.0).then_inc(sem("craw_zero"), 1)
            pool.wait_ge(sem("a_ready"), 1)
            for n in range(2 * N_UNITS):
                u = n // 2
                g, t = u // TT, u % TT
                h0 = g * (SSM_HEADS // GROUPS) + 4 * (n % 2)
                if n == 0:
                    pool.wait_ge(misc_taken, MISC_AT[("values", 19, "a", 15)] + 1)
                if n >= 2:
                    pool.wait_ge(exp_ready, n)
                dst = work[:, 2 + n % 2].rearrange("p (h l) -> p h l", h=4)
                pool.tensor_tensor(dst, upto[:].unsqueeze(1).to_broadcast([P, 4, P]),
                                   a_sb[:, t, h0:h0 + 4].unsqueeze(2).to_broadcast([P, 4, P]),
                                   ALU.mult).then_inc(sem("steps_ready"), 1)
            pool.wait_ge(gemm_taken, GEMM_END)
            pool.wait_ge(sem("br_merged"), 16)
            pool.memset(bias_gu, 0.0).then_inc(sem("bias_rows_zero"), 1)
            pool.memset(S[:, 5], 0.0).then_inc(sem("bias_rows_zero"), 1)
            pool.wait_ge(sem("out_squares"), TT)
            pool.memset(S[:, 1, 0:1100], 0.0).then_inc(sem("tables_zero"), 1)

        @block.scalar
        def _(act):
            roots = [0]

            def root(width):
                roots[0] += 1
                act.wait_ge(sem("variance"), roots[0])
                act.activation(root_out[:, 0:width], root_in[:, 0:width], ACT.Sqrt).then_inc(sem("root_ready"), 1)

            def exp_group(i):
                act.wait_ge(exp_ready, i + 1)

            act.wait_ge(sem("rel_landed"), 16)
            act.activation(rel_sb[:, 0:127], rel_sb[:, 127:128].to_broadcast([A_HEADS, 127]), ACT.Copy)\
                .then_inc(sem("rel_edge"), 1)
            act.activation(rel_sb[:, 384:512], rel_sb[:, 383:384].to_broadcast([A_HEADS, 128]), ACT.Copy)\
                .then_inc(sem("rel_edge"), 1)
            for j, (src, landed_sem) in enumerate(((mem_sb, "mem_landed"), (x_sb, "x_landed"))):
                act.wait_ge(sem(landed_sem), 16)
                for t in range(TT):
                    dst = (squares, q_raw)[j]
                    act.activation(dst[:, t], src[:, t], ACT.Square,
                                   accum_out=ss_x[:, 2 * j + t:2 * j + t + 1]).then_inc(sem("row_squares"), 1)

            root(4)
            n = 0
            br = 0
            for step in SCHED:
                kind = step[0]
                if kind == "headnorm":
                    root(TT * (X_HEADS if step[1] in ("kx", "qx") else A_HEADS))
                elif kind == "ynorm":
                    root(N_UNITS)
                elif kind in ("gemm", "gemmb"):
                    if kind == "gemmb":
                        if step[1] % 2 == 0:
                            continue
                        todo = [("bb", step[1] // 2, h) for h in range(2)]
                    else:
                        todo = [step[1:]]
                    for name, i, h in todo:
                        act.wait_ge(gemm_ready, n + 1)
                        src = ps[:, GEMM_BANKS[n % 3], :]
                        cols = slice(i * NB, (i + 1) * NB)
                        func = ACT.Copy
                        if name == "mk":
                            dst = kx_raw[:, h, cols]
                        elif name == "mv":
                            dst = vx[:, h, cols]
                        elif name == "qx":
                            act.wait_ge(misc_ready, MISC_AT[("hT",)] + 4)
                            dst = qx_raw[:, h, cols]
                        elif name == "q":
                            dst = q_raw[:, h, cols]
                        elif name == "k":
                            dst = k_raw[:, h, cols]
                        elif name == "v":
                            dst = v_sb[:, h, cols]
                        elif name == "xbc":
                            j = 2 * i + h
                            if j == 0:
                                act.wait_ge(sem("craw_zero"), 1)
                            if j >= 2:
                                act.wait_ge(sem("conv_done"), j - 1)
                            dst = craw[:, j % 2, :, TAPS - 1:TAPS - 1 + T]
                            src = src.rearrange("p (j t) -> p j t", j=2)
                        elif name == "z":
                            u = 2 * i + h
                            if u >= 2:
                                act.wait_ge(sem("gated"), u - 1)
                            else:
                                act.wait_ge(misc_ready, MISC_AT[("values", 19, "a", 15)] + 1)
                            dst, func = zbuf[:, u % 2], ACT.Silu
                        elif name in ("gc", "ga", "gb"):
                            k = {"gc": 0, "ga": 1, "gb": 2}[name]
                            if k == 0 and (i, h) == (0, 0):
                                act.wait_ge(misc_taken, MISC_AT[("scores", 11, "a", 7)] + 1)
                            if k:
                                act.wait_ge(sem("br_merged"), 4 * k)
                            dst, func = sig[:, h, cols], ACT.Sigmoid
                        else:
                            if br >= 2:
                                act.wait_ge(sem("br_merged"), br - 1)
                            dst = tmp[:, br % 2]
                            br += 1
                        act.activation(dst, src, func).then_inc(gemm_taken, 1)
                        n += 1
                elif kind == "square":
                    name = step[1]
                    src, last, order = {"kx": (kx_raw, ("mk", 1, 1), 0), "qx": (qx_raw, ("qx", 1, 1), 1),
                                        "q": (q_raw, ("q", 1, 1), 2), "k": (k_raw, ("k", 1, 1), 3)}[name]
                    act.wait_ge(gemm_taken, GEMM_AT[last] + 1)
                    if order == 0:
                        act.wait_ge(sem("row_squares"), 4)
                    else:
                        act.wait_ge(sem("head_sums"), order)
                    act.activation(squares[:], src[:], ACT.Square).then_inc(sem("head_squares"), 1)
                elif kind == "scores":
                    m = step[1]
                    act.wait_ge(misc_taken, MISC_AT[step] + 1)
                    if step[2] == "a":
                        act.wait_ge(sem("scores_first"), step[3] + 1)
                    w = 512 if step[2] == "x" else 384
                    act.activation(work[:, m % 2, 0:w], work[:, m % 2, 0:w], ACT.Exp).then_inc(sem("exp_out"), 1)
                elif kind == "silu":
                    j = step[1]
                    act.wait_ge(sem("conv_done"), j + 1)
                    if 2 * j < INNER // P:
                        if j >= 2:
                            act.wait_ge(misc_ready, MISC_AT[("xsT", j - 2)] + 1)
                        dst = conv_out[:, j % 2]
                    else:
                        dst = bcT[:, 2 * j - INNER // P:2 * j - INNER // P + 2, :]
                    act.activation(dst, conv_acc[:, j % 2], ACT.Silu).then_inc(sem("silu_out"), 1)
                elif kind == "dt":
                    act.wait_ge(sem("dt_abs"), 1)
                    act.activation(dtw[:, 1], dtw[:, 1], ACT.Exp, scale=-1.0).then_inc(sem("dt_exp"), 1)
                    act.wait_ge(sem("dt_exp"), 1)
                    act.wait_ge(sem("dt_one"), 1)
                    act.activation(dtw[:, 3], dtw[:, 2], ACT.Ln).then_inc(sem("dt_ln"), 1)
                    act.activation(a_head[:], head_rows[:, 1], ACT.Exp).then_inc(sem("a_exp"), 1)
                elif kind == "decay":
                    exp_group(0)
                    act.activation(decays[:].rearrange("p a h -> p (a h)"), ps[:, EXP_BANKS[0], 0:2 * SSM_HEADS],
                                   ACT.Exp).then_inc(exp_taken, 1)
                elif kind == "spread":
                    u = step[1]
                    for d in range(2):
                        n_exp = 1 + 2 * u + d
                        exp_group(n_exp)
                        if u >= 1:
                            act.wait_ge(misc_ready, MISC_AT[("ssm", u - 1, step[2] if step[3] else step[2] - 1,
                                                             1 - step[3])] + 1 + (1 - step[3]))
                        elif d == 0:
                            act.wait_ge(misc_taken, MISC_AT[("values", 19, "a", 15)] + 1)
                        act.activation(work[:, d], ps[:, EXP_BANKS[n_exp % 2], :], ACT.Exp).then_inc(exp_taken, 1)
                elif kind == "ssm":
                    u, g, t = step[1:]
                    act.wait_ge(sem("gated"), u + 1)
                    if u:
                        act.wait_ge(sem("y_squares"), u)
                    act.activation(sq_junk, xs[t][:, g * GW:(g + 1) * GW], ACT.Square,
                                   accum_out=ss_y[:, t * GROUPS + g:t * GROUPS + g + 1]).then_inc(sem("y_squares"), 1)
            act.wait_ge(sem("br_merged"), 16)
            for t in range(TT):
                act.activation(sq2[:, t], x_sb[:, t], ACT.Square, accum_out=ss_2[:, t:t + 1])\
                    .then_inc(sem("out_squares"), 1)
            root(TT)
            act.wait_ge(sem("top_shifted"), 1)
            act.activation(e4, e4, ACT.Exp).then_inc(sem("top_exp"), 1)
            act.wait_ge(sem("gather_ready"), 1)
            act.activation(xgT.rearrange("p c j -> p (c j)"), ps[:, X_BANK, :], ACT.Copy).then_inc(sem("xg_ready"), 1)
            act.wait_ge(sem("passes_known"), 1)
            n_pass = act.value_load(npass_i[0:1, 0:1], min_val=1, max_val=PASSES)
            with act.Fori(0, n_pass) as b:
                with act.Fori(0, EXPERTS) as e:
                    i = b * EXPERTS + e
                    act.wait_ge(sem("g_ready"), i + 1)
                    act.activation(sg_sb, g_sb, ACT.Sigmoid, scale=ALPHA).then_inc(sem("sg_ready"), 1)
                    act.wait_ge(sem("hot_wT_ready"), i + 1)
                    for h in range(2):
                        act.activation(hot_wT[64 * h:64 * h + 64, h],
                                       ps[64 * h:64 * h + 64, D_BANK, 0:T].rearrange("p (t j) -> p t j", t=TT),
                                       ACT.Copy).then_inc(sem("scatter_ready"), 1)
                    act.wait_ge(sem("gather_ready"), i + 2)
                    act.activation(xgT.rearrange("p c j -> p (c j)"), ps[:, X_BANK, :], ACT.Copy)\
                        .then_inc(sem("xg_ready"), 1)
                    act.wait_ge(sem("actT_out"), i + 1)
                    act.activation(actT.rearrange("p c j -> p (c j)"), ps[:, G_BANK, :], ACT.Copy)\
                        .then_inc(sem("actT_ready"), 1)

        @block.vector
        def _(dve):
            chain = [0]

            def link(ins):
                chain[0] += 1
                ins.then_inc(sem("vector_chain"), 1)
                dve.wait_ge(sem("vector_chain"), chain[0])

            misc = [0]
            roots = [0]

            def group():
                misc[0] += 1
                dve.wait_ge(misc_ready, misc[0])
                return MISC_BANKS[(misc[0] - 1) % 3]

            def rstd(dst, src, width):
                roots[0] += 1
                n = dst.shape[1]
                v, r = root_in[:, 0:n], root_out[:, 0:n]
                dve.tensor_scalar(v, src, 1.0 / width, EPS, ALU.mult, ALU.add).then_inc(sem("variance"), 1)
                dve.wait_ge(sem("root_ready"), roots[0])
                link(dve.reciprocal(dst, r))
                link(dve.tensor_tensor(r, dst, v, ALU.mult))
                link(dve.tensor_tensor(r, r, dst, ALU.mult))
                link(dve.tensor_scalar(r, r, -0.5, 1.5, ALU.mult, ALU.add))
                link(dve.tensor_tensor(dst, dst, r, ALU.mult))

            dve.wait_ge(sem("small_landed"), 16 * 13)
            dve.wait_ge(sem("iota"), 1)
            link(dve.tensor_copy(iota_j[:], iota_i[:]))
            dve.tensor_copy(iota2[:], iota_j[:].unsqueeze(1).to_broadcast([P, 2, BLK])).then_inc(sem("vector_side"), 1)
            dve.tensor_scalar(steps_b[:], iota_j[:, 0:PASSES], float(BLK), None, ALU.mult).then_inc(sem("vector_side"), 1)
            dve.wait_ge(sem("row_squares"), 4)
            rstd(rs_x, ss_x, D)
            dve.wait_ge(sem("mem_landed"), 16)
            dve.wait_ge(sem("x_landed"), 16)
            for t in range(TT):
                dve.tensor_scalar(mem_sb[:, t], mem_sb[:, t], rs_x[:, t:t + 1], None, ALU.mult)\
                    .then_inc(sem("rows_scaled"), 1)
            for t in range(TT):
                dve.tensor_scalar(xn[:, t], x_sb[:, t], rs_x[:, 2 + t:3 + t], None, ALU.mult)\
                    .then_inc(sem("rows_scaled"), 1)

            br = 0
            norms = 0
            for step in SCHED:
                kind = step[0]
                if kind in ("memT", "hT"):
                    dst, gain = (memT, gmem_sb) if kind == "memT" else (hT, gm_sb)
                    for t in range(TT):
                        for q in range(2):
                            b = group()
                            dve.tensor_tensor(dst[:, 4 * q:4 * q + 4, t * P:(t + 1) * P],
                                              ps[:, b, :].rearrange("p (c t) -> p c t", c=4),
                                              gain[:, 4 * q:4 * q + 4].unsqueeze(2).to_broadcast([P, 4, P]),
                                              ALU.mult).then_inc(misc_taken, 1)
                elif kind == "headnorm":
                    raw, heads = {"kx": (kx_raw, X_HEADS), "qx": (qx_raw, X_HEADS),
                                  "q": (q_raw, A_HEADS), "k": (k_raw, A_HEADS)}[step[1]]
                    norms += 1
                    dve.wait_ge(sem("head_squares"), norms)
                    w = D // heads
                    ss = ss_h[:, 0:TT * heads]
                    dve.tensor_reduce(ss, squares[:].rearrange("p t (h d) -> p (t h) d", d=w), AX, ALU.add)\
                        .then_inc(sem("head_sums"), 1)
                    dve.wait_ge(sem("head_sums"), norms)
                    rstd(ss, ss, w)
                    view = raw[:].rearrange("p t (h d) -> p (t h) d", d=w)
                    dve.tensor_tensor(view, view, ss.unsqueeze(2).to_broadcast([P, TT * heads, w]), ALU.mult)\
                        .then_inc(sem("head_normed"), 1)
                elif kind == "headT":
                    name = step[1]
                    if name == "q":
                        dve.wait_ge(sem("rel_stored"), 16)
                        link(dve.memset(qz[:], 0.0))
                    for c2 in range(4):
                        b = group()
                        for j in range(2):
                            c = 2 * c2 + j
                            src = ps[:, b, j * T:(j + 1) * T]
                            if name == "kx":
                                last = dve.tensor_scalar(kxT[:, c], src, xg_sb[:, 2 + j:3 + j], None, ALU.mult)
                            elif name == "qx":
                                last = dve.tensor_scalar(qxT[:, c], src, xg_sb[:, j:j + 1], X_DIM ** -0.5,
                                                         ALU.mult, ALU.mult)
                            elif name == "k":
                                last = dve.tensor_scalar(kT[:, c], src, ag_sb[:, 1:2], None, ALU.mult)
                            else:
                                for r in range(2):
                                    rows = slice(64 * r, 64 * r + 64)
                                    last = dve.tensor_scalar(qz[rows, 2 * c + r], src[rows], ag_sb[rows, 0:1],
                                                             A_DIM ** -0.5, ALU.mult, ALU.mult)
                        last.then_inc(misc_taken, 1)
                elif kind == "scores":
                    m, br_name, h = step[1:]
                    b = group()
                    sc = work[:, m % 2]
                    if br_name == "x":
                        v = ps[:, b, :].rearrange("p (t k) -> p t k", t=TT)
                        link(dve.tensor_reduce(mx1, v, AX, ALU.max))
                        dve.tensor_tensor(sc.rearrange("p (t k) -> p t k", t=TT), v,
                                          mx1.unsqueeze(2).to_broadcast([P, TT, MEM]), ALU.subtract)\
                            .then_inc(misc_taken, 1)
                    else:
                        if h == 0:
                            dve.wait_ge(sem("bias_landed"), 32)
                            for j in range(2):
                                link(dve.memset(bias[j][0:CHUNK, :, T - CHUNK:T], MASKED))
                        bh = bias[h // 8][:, h % 8]
                        link(dve.tensor_tensor(sc[:, 0:P], ps[:, b, 0:P], bh[:, P:T], ALU.add))
                        chain[0] += 1
                        dve.tensor_tensor(sc[:, P:3 * P], ps[:, b, P:3 * P], bh[:, 0:T], ALU.add)\
                            .then_inc(sem("vector_chain"), 1)
                        dve.wait_ge(sem("vector_chain"), chain[0])
                        link(dve.tensor_reduce(mx3, sc[:, 0:3 * P].rearrange("p (j k) -> p j k", j=3), AX, ALU.max))
                        link(dve.tensor_tensor(mx3[:, 1:2], mx3[:, 1:2], mx3[:, 2:3], ALU.max))
                        dve.tensor_scalar(sc[:, 0:P], sc[:, 0:P], mx3[:, 0:1], None, ALU.subtract)\
                            .then_inc(sem("scores_first"), 1)
                        dve.tensor_scalar(sc[:, P:3 * P], sc[:, P:3 * P], mx3[:, 1:2], None, ALU.subtract)\
                            .then_inc(misc_taken, 1)
                elif kind == "soften":
                    m, br_name, h = step[1:]
                    dve.wait_ge(sem("exp_out"), m + 1)
                    sc = work[:, m % 2]
                    if br_name == "x":
                        v = sc.rearrange("p (t k) -> p t k", t=TT)
                        link(dve.tensor_reduce(sm1, v, AX, ALU.add))
                        link(dve.reciprocal(rc1, sm1))
                        dve.tensor_tensor(v, v, rc1.unsqueeze(2).to_broadcast([P, TT, MEM]), ALU.mult)\
                            .then_inc(sem("probs"), 2)
                    else:
                        link(dve.tensor_reduce(mx3, sc[:, 0:3 * P].rearrange("p (j k) -> p j k", j=3), AX, ALU.add))
                        link(dve.tensor_tensor(mx3[:, 1:2], mx3[:, 1:2], mx3[:, 2:3], ALU.add))
                        link(dve.reciprocal(rc1, mx3[:, 0:2]))
                        dve.tensor_scalar(sc[:, 0:P], sc[:, 0:P], rc1[:, 0:1], None, ALU.mult)\
                            .then_inc(sem("probs"), 1)
                        dve.tensor_scalar(sc[:, P:3 * P], sc[:, P:3 * P], rc1[:, 1:2], None, ALU.mult)\
                            .then_inc(sem("probs"), 1)
                elif kind == "probsT":
                    m, br_name, h = step[1:]
                    b = group()
                    w = 512 if br_name == "x" else 384
                    dve.tensor_copy(work[:, 2 + m % 2, 0:w], ps[:, b, 0:w]).then_inc(misc_taken, 1)
                elif kind == "values":
                    m, br_name, h = step[1:]
                    b = group()
                    if br_name == "x":
                        dve.tensor_copy(ycT[:, 2 * h:2 * h + 2], ps[:, b, :].rearrange("p (c t) -> p c t", c=2))\
                            .then_inc(misc_taken, 1)
                    else:
                        rows = slice(64 * (h % 2), 64 * (h % 2) + 64)
                        dve.tensor_copy(yaT[rows, h // 2], ps[rows, b, 0:T]).then_inc(misc_taken, 1)
                elif kind == "conv":
                    j = step[1]
                    dve.wait_ge(gemm_taken, GEMM_AT[("xbc", j // 2, j % 2)] + 1)
                    if j >= 2:
                        dve.wait_ge(sem("silu_out"), j - 1)
                    for tap in range(TAPS):
                        for i in range(2):
                            c = 2 * j + i
                            acc, src = conv_acc[:, j % 2, i], craw[:, j % 2, i, tap:tap + T]
                            if tap == 0:
                                ins = dve.tensor_scalar(acc, src, cw_sb[:, c, 0:1], cb_sb[:, c:c + 1], ALU.mult, ALU.add)
                            else:
                                ins = dve.scalar_tensor_tensor(out=acc, in0=src, scalar=cw_sb[:, c, tap:tap + 1],
                                                               in1=acc, op0=ALU.mult, op1=ALU.add)
                            if tap == TAPS - 1 and i == 1:
                                ins.then_inc(sem("conv_done"), 1)
                            else:
                                chain[0] += 1
                                ins.then_inc(sem("vector_chain"), 1)
                        dve.wait_ge(sem("vector_chain"), chain[0])
                elif kind == "xsT":
                    j = step[1]
                    b = group()
                    for t in range(TT):
                        last = dve.tensor_copy(xs[t][:, j * 256:(j + 1) * 256], ps[:, b, t * 256:(t + 1) * 256])
                        if t == 0:
                            last.then_inc(sem("xs_first"), 1)
                    last.then_inc(misc_taken, 1)
                elif kind == "dt":
                    b = group()
                    v = dtw[:, 0].rearrange("p (t h) -> p t h", t=TT)
                    dve.tensor_tensor(v, ps[:, b, 0:64].rearrange("p (t h) -> p t h", t=TT),
                                      head_rows[:, 0].unsqueeze(1).to_broadcast([P, TT, SSM_HEADS]), ALU.add)\
                        .then_inc(misc_taken, 1)
                    dve.wait_ge(misc_taken, misc[0])
                    dve.scalar_tensor_tensor(out=dtw[:, 1], in0=dtw[:, 0], scalar=-1.0, in1=dtw[:, 0],
                                             op0=ALU.mult, op1=ALU.max).then_inc(sem("dt_abs"), 1)
                    dve.wait_ge(sem("dt_exp"), 1)
                    dve.tensor_scalar(dtw[:, 2], dtw[:, 1], 1.0, None, ALU.add).then_inc(sem("dt_one"), 1)
                    dve.wait_ge(sem("dt_one"), 1)
                    link(dve.tensor_scalar(dtw[:, 4], dtw[:, 2], -1.0, 1e-30, ALU.add, ALU.max))
                    dve.wait_ge(sem("dt_ln"), 1)
                    link(dve.tensor_tensor(dtw[:, 3], dtw[:, 3], dtw[:, 1], ALU.mult))
                    link(dve.reciprocal(dtw[:, 5], dtw[:, 4]))
                    link(dve.tensor_tensor(dtw[:, 3], dtw[:, 3], dtw[:, 5], ALU.mult))
                    link(dve.tensor_scalar(dtw[:, 5], dtw[:, 4], 1e-20, None, ALU.is_lt))
                    link(dve.tensor_tensor(dtw[:, 5], dtw[:, 5], dtw[:, 1], ALU.mult))
                    link(dve.tensor_tensor(dtw[:, 3], dtw[:, 3], dtw[:, 5], ALU.add))
                    link(dve.scalar_tensor_tensor(out=dtw[:, 4], in0=dtw[:, 0], scalar=0.0, in1=dtw[:, 3],
                                                  op0=ALU.max, op1=ALU.add))
                    dve.wait_ge(sem("a_exp"), 1)
                    dve.scalar_tensor_tensor(out=a_sb, in0=dt_sb, scalar=-1.0,
                                             in1=a_head[:].unsqueeze(1).to_broadcast([P, TT, SSM_HEADS]),
                                             op0=ALU.mult, op1=ALU.mult).then_inc(sem("a_ready"), 1)
                elif kind == "xdt":
                    dve.wait_ge(misc_taken, misc[0])
                    dve.wait_ge(sem("xs_first"), INNER // P // 2)
                    dve.wait_ge(sem("a_ready"), 1)
                    dve.wait_ge(exp_taken, 1)
                    for t in range(TT):
                        v = xs[t].rearrange("p (h d) -> p h d", d=SSM_DIM)
                        link(dve.tensor_tensor(xdt[t].rearrange("p (h d) -> p h d", d=SSM_DIM), v,
                                               dt_sb[:, t].unsqueeze(2).to_broadcast([P, SSM_HEADS, SSM_DIM]), ALU.mult))
                        link(dve.tensor_tensor(v, v, head_rows[:, 2].unsqueeze(2)
                                               .to_broadcast([P, SSM_HEADS, SSM_DIM]), ALU.mult))
                    dve.tensor_tensor(fx.rearrange("p (h d) -> p h d", d=SSM_DIM),
                                      xdt[0].rearrange("p (h d) -> p h d", d=SSM_DIM),
                                      decays[:, 0].unsqueeze(2).to_broadcast([P, SSM_HEADS, SSM_DIM]), ALU.mult)\
                        .then_inc(sem("xdt_ready"), 1)
                elif kind == "cb":
                    g = step[1]
                    b = group()
                    chain[0] += 2
                    dve.tensor_tensor(cbm[:, g % 2, 0:P], ps[:, b, 0:P], upto[:], ALU.mult)\
                        .then_inc(sem("vector_chain"), 1)
                    dve.tensor_tensor(cbm[:, g % 2, P:2 * P], ps[:, b, 2 * P:3 * P], upto[:], ALU.mult)\
                        .then_inc(sem("vector_chain"), 1)
                    dve.tensor_copy(cbm[:, g % 2, 2 * P:3 * P], ps[:, b, P:2 * P]).then_inc(misc_taken, 1)
                    dve.wait_ge(sem("vector_chain"), chain[0])
                elif kind == "weigh":
                    u, g, t = step[1:]
                    for d in range(2):
                        dve.wait_ge(exp_taken, 1 + 2 * u + d + 1)
                        v = work[:, d].rearrange("p (h l) -> p h l", h=4)
                        dve.tensor_tensor(v, v, cbm[:, g % 2, t * P:(t + 1) * P].unsqueeze(1).to_broadcast([P, 4, P]),
                                          ALU.mult).then_inc(sem("weighed"), 1)
                elif kind == "ssm":
                    u, g, t = step[1:]
                    y = xs[t][:, g * GW:(g + 1) * GW]
                    if t == 1:
                        b = group()
                        dve.tensor_tensor(y_off.rearrange("p (h d) -> p h d", d=SSM_DIM),
                                          ps[:, b, :].rearrange("p (h d) -> p h d", d=SSM_DIM),
                                          decays[:, 1, 8 * g:8 * g + 8].unsqueeze(2).to_broadcast([P, 8, SSM_DIM]),
                                          ALU.mult).then_inc(misc_taken, 1)
                        dve.wait_ge(misc_taken, misc[0])
                    b = group()
                    dve.tensor_tensor(y, ps[:, b, :], y, ALU.add).then_inc(misc_taken, 1)
                    dve.wait_ge(misc_taken, misc[0])
                    if t == 1:
                        link(dve.tensor_tensor(y, y, y_off, ALU.add))
                    dve.wait_ge(gemm_taken, GEMM_AT[("z", g, t)] + 1)
                    dve.tensor_tensor(y, y, zbuf[:, u % 2], ALU.mult).then_inc(sem("gated"), 1)
                elif kind == "ynorm":
                    dve.wait_ge(sem("y_squares"), N_UNITS)
                    rstd(ss_y, ss_y, GW)
                    for t in range(TT):
                        v = xs[t].rearrange("p (g d) -> p g d", d=GW)
                        dve.tensor_tensor(v, v, ss_y[:, t * GROUPS:(t + 1) * GROUPS].unsqueeze(2)
                                          .to_broadcast([P, GROUPS, GW]), ALU.mult).then_inc(sem("y_normed"), 1)
                elif kind == "yT":
                    for c2 in range(8):
                        b = group()
                        for j in range(2):
                            c = 2 * c2 + j
                            last = dve.tensor_scalar(ybT[:, c], ps[:, b, j * T:(j + 1) * T], gssm_sb[:, c:c + 1], None,
                                                     ALU.mult)
                            if j == 0:
                                last.then_inc(sem("ybT_first"), 1)
                        last.then_inc(misc_taken, 1)
                elif kind in ("gemm", "gemmb"):
                    if kind == "gemm":
                        if step[1] not in ("bc", "ba", "wo"):
                            continue
                        todo = [step[1:]]
                    else:
                        if step[1] % 2 == 0:
                            continue
                        todo = [("bb", step[1] // 2, h) for h in range(2)]
                    for name, i, h in todo:
                        dve.wait_ge(gemm_taken, GEMM_AT[(name, i, h)] + 1)
                        cols = slice(i * NB, (i + 1) * NB)
                        src = tmp[:, br % 2]
                        if name == "wo":
                            dve.tensor_tensor(x_sb[:, h, cols], x_sb[:, h, cols], src, ALU.add)\
                                .then_inc(sem("br_merged"), 1)
                        elif name == "bc":
                            if (i, h) == (0, 0):
                                dve.wait_ge(sem("silu_out"), CONV_T // 2)
                            dve.tensor_tensor(merged[:, h, cols], src, sig[:, h, cols], ALU.mult)\
                                .then_inc(sem("br_merged"), 1)
                        else:
                            link(dve.tensor_tensor(src, src, sig[:, h, cols], ALU.mult))
                            dve.tensor_tensor(merged[:, h, cols], merged[:, h, cols], src, ALU.add)\
                                .then_inc(sem("br_merged"), 1)
                        br += 1
                elif kind == "mergedT":
                    for c2 in range(4):
                        b = group()
                        dve.tensor_copy(mergedT[:, 2 * c2:2 * c2 + 2], ps[:, b, :].rearrange("p (c t) -> p c t", c=2))\
                            .then_inc(misc_taken, 1)

            dve.wait_ge(sem("out_squares"), TT)
            rstd(rs_2, ss_2, D)
            dve.wait_ge(sem("gain2_landed"), 16)
            for t in range(TT):
                dve.scalar_tensor_tensor(out=h2[:, t], in0=x_sb[:, t], scalar=rs_2[:, t:t + 1], in1=gain2,
                                         op0=ALU.mult, op1=ALU.mult).then_inc(sem("h2_ready"), 1)
            for c2 in range(4):
                b = group()
                dve.tensor_copy(h2T[:, 2 * c2:2 * c2 + 2], ps[:, b, :].rearrange("p (c t) -> p c t", c=2))\
                    .then_inc(misc_taken, 1)
            b = group()
            dve.tensor_tensor(logits, ps[:, b, 0:TT * EXPERTS].rearrange("p (t e) -> p t e", t=TT),
                              head_rows[:, 3].unsqueeze(1).to_broadcast([P, TT, EXPERTS]), ALU.add)\
                .then_inc(misc_taken, 1)
            dve.wait_ge(misc_taken, misc[0])
            for t in range(TT):
                link(dve.max(mx8[:, t], logits[:, t]))
                link(dve.max_index(idx8[:, t], mx8[:, t], logits[:, t]))
            link(dve.tensor_copy(idxf, idx8[:]))
            dve.tensor_tensor(e4, mx8[:, :, 0:TOP_K], mx8[:, :, 0:1].to_broadcast([P, TT, TOP_K]), ALU.subtract)\
                .then_inc(sem("top_shifted"), 1)
            dve.wait_ge(sem("top_exp"), 1)
            link(dve.tensor_reduce(s4, e4, AX, ALU.add))
            link(dve.reciprocal(s4, s4))
            link(dve.tensor_tensor(e4, e4, s4.unsqueeze(2).to_broadcast([P, TT, TOP_K]), ALU.mult))
            iota_e = iota_j[:, 0:EXPERTS]
            for t in range(TT):
                for k in range(TOP_K):
                    dst = wts if k == 0 else part
                    link(dve.tensor_scalar(dst[:, t], iota_e, idxf[:, t, k:k + 1], e4[:, t, k:k + 1],
                                           ALU.is_equal, ALU.mult))
                    if k:
                        link(dve.tensor_tensor(wts[:, t], wts[:, t], part[:, t], ALU.add))
            dve.tensor_scalar(chosen, wts, 0.0, None, ALU.is_gt).then_inc(sem("chosen_ready"), 1)
            dve.wait_ge(sem("tables_zero"), 1)
            b = group()
            dve.tensor_copy(wT[0:EXPERTS, :], ps[0:EXPERTS, b, 0:T]).then_inc(misc_taken, 1)
            b = group()
            link(dve.tensor_tensor(part, ps[:, b, 0:64].rearrange("p (t e) -> p t e", t=TT), chosen, ALU.mult))
            dve.tensor_reduce(cmax, ps[:, b, 64:64 + EXPERTS], AX, ALU.max).then_inc(misc_taken, 1)
            dve.wait_ge(misc_taken, misc[0])
            link(dve.tensor_scalar(over, steps_b[:], cmax, None, ALU.is_lt))
            link(dve.tensor_reduce(npass_f, over, AX, ALU.add))
            dve.tensor_copy(npass_i[:], npass_f[0:1, :]).then_inc(sem("passes_known"), 1)
            link(dve.memset(place4[:, :, PASSES * EXPERTS:NPAD], -1.0))
            for p in range(PASSES):
                cols = slice(p * EXPERTS, (p + 1) * EXPERTS)
                link(dve.tensor_scalar(place4[:, :, cols], part, -1.0 - BLK * p, None, ALU.add))
                link(dve.tensor_copy(weight4[:, :, cols], wts))
                link(dve.tensor_copy(picks[:, cols], ident[:, 0:EXPERTS]))
            dve.wait_ge(sem("bias_rows_zero"), 2)

            def find(i):
                for t in range(TT):
                    dve.tensor_scalar(hot[:, t], iota_j[:], place4[:, t, bass.ds(i, 1)], None, ALU.is_equal)\
                        .then_inc(sem("hot_ready"), 1)

            find(0)
            dve.wait_ge(sem("passes_known"), 1)
            n_pass = dve.value_load(npass_i[0:1, 0:1], min_val=1, max_val=PASSES)
            with dve.Fori(0, n_pass) as b_:
                with dve.Fori(0, EXPERTS) as e:
                    i = b_ * EXPERTS + e
                    dve.wait_ge(e_used[1], i)
                    dve.wait_ge(sem("hot_wT_ready"), i)
                    dve.tensor_copy(pick, picks[:, bass.ds(i, 1)].to_broadcast([P, BLK])).then_inc(sem("pick_ready"), 1)
                    for t in range(TT):
                        dve.tensor_scalar(hot_w[:, t], iota2[:], place4[:, t, bass.ds(i, 1)],
                                          weight4[:, t, bass.ds(i, 1)], ALU.is_equal, ALU.mult)\
                            .then_inc(sem("hot_w_ready"), 1)
                    dve.wait_ge(sem("gather_ready"), i + 1)
                    find(i + 1)
                    dve.wait_ge(e_used[1], i + 1)
                    dve.tensor_scalar(g_sb, ps[:, G_BANK, :], LIMIT, None, ALU.min).then_inc(sem("g_ready"), 1)
                    dve.tensor_scalar(u_sb, ps[:, U_BANK, :], LIMIT, -LIMIT, ALU.min, ALU.max)\
                        .then_inc(sem("u_ready"), 1)
                    dve.wait_ge(sem("u_ready"), i + 1)
                    dve.wait_ge(sem("g_ready"), i + 1)
                    dve.scalar_tensor_tensor(out=gu_sb, in0=u_sb, scalar=1.0, in1=g_sb, op0=ALU.add, op1=ALU.mult)\
                        .then_inc(sem("gu_ready"), 1)
                    dve.wait_ge(sem("gu_ready"), i + 1)
                    dve.wait_ge(sem("sg_ready"), i + 1)
                    dve.wait_ge(sem("actT_out"), i)
                    dve.tensor_tensor(act_sb, gu_sb, sg_sb, ALU.mult).then_inc(sem("act_ready"), 1)
                    dve.wait_ge(e_used[3], i + 1)
                    dve.wait_ge(sem("scattered"), i)
                    dve.tensor_copy(yb, ps[:, D_BANK, :]).then_inc(sem("yb_ready"), 1)
            dve.wait_ge(sem("experts_done"), 1)
            for t in range(TT):
                for h in range(2):
                    cols = slice(h * NB, (h + 1) * NB)
                    dve.tensor_tensor(y_out[:, t, cols], ps[:, ACC[2 * t + h], :], x_sb[:, t, cols], ALU.add)\
                        .then_inc(sem("y_ready"), 1)

        @block.tensor
        def _(pe):
            misc = [0]

            def group():
                n = misc[0]
                misc[0] += 1
                if n >= 3:
                    pe.wait_ge(misc_taken, n - 2)
                return MISC_BANKS[n % 3]

            def exp_bank(n):
                if n >= 2:
                    pe.wait_ge(exp_taken, n - 1)
                return EXP_BANKS[n % 2]

            def turn(dst, src):
                return pe.transpose(dst, src, ident[:])

            def by_columns(src, c2, width=P):
                b = group()
                for j in range(2):
                    for t in range(TT):
                        last = turn(ps[:, b, j * T + t * P:j * T + (t + 1) * P],
                                    src(t)[:, (2 * c2 + j) * P:(2 * c2 + j + 1) * P])
                last.then_inc(misc_ready, 1)

            pe.wait_ge(sem("masks"), 3)
            pe.wait_ge(sem("small_landed"), 16 * 13)
            n = 0
            blk = 0
            for step in SCHED:
                kind = step[0]
                if kind in ("memT", "hT"):
                    src = mem_sb if kind == "memT" else xn
                    pe.wait_ge(sem("rows_scaled"), 2 if kind == "memT" else 4)
                    for t in range(TT):
                        for q in range(2):
                            b = group()
                            for j in range(4):
                                c = 4 * q + j
                                last = turn(ps[:, b, j * P:(j + 1) * P], src[:, t, c * P:(c + 1) * P])
                            last.then_inc(misc_ready, 1)
                elif kind == "gemm":
                    name, i, h = step[1:]
                    slot = ring[:, blk % RING].rearrange("p (c n) -> p c n", c=KC)
                    if h == 0:
                        pe.wait_ge(landed[blk % RING], 16 * (blk // RING + 1))
                    if n >= 3:
                        pe.wait_ge(gemm_taken, n - 2)
                    lhs = {"mk": memT, "mv": memT, "bc": ycT, "ba": yaT, "wo": mergedT}.get(name, hT)
                    needs = {("mk", 0, 0): ("memT",), ("qx", 0, 0): ("hT",),
                             ("bc", 0, 0): ("values", 3, "x", 3), ("ba", 0, 0): ("values", 19, "a", 15),
                             ("wo", 0, 0): ("mergedT",)}.get((name, i, h))
                    if needs:
                        pe.wait_ge(misc_taken, MISC_AT[needs] + MISC_GROUPS[needs[0]])
                    b = GEMM_BANKS[n % 3]
                    if name == "xbc":
                        for j in range(2):
                            cols = slice((2 * h + j) * P, (2 * h + j + 1) * P)
                            for c in range(KC):
                                last = pe.matmul(ps[:, b, j * T:(j + 1) * T], slot[:, c, cols], hT[:, c],
                                                 start=(c == 0), stop=(c == KC - 1))
                    else:
                        for c in range(KC):
                            last = pe.matmul(ps[:, b, :], lhs[:, c, h * P:(h + 1) * P], slot[:, c],
                                             start=(c == 0), stop=(c == KC - 1))
                    last.then_inc(gemm_ready, 1)
                    n += 1
                    if h == 1:
                        blk += 1
                elif kind == "gemmb":
                    i = step[1]
                    slot = ring[:, blk % RING].rearrange("p (c n) -> p c n", c=KC)
                    pe.wait_ge(landed[blk % RING], 16 * (blk // RING + 1))
                    if i == 0:
                        pe.wait_ge(misc_taken, MISC_AT[("yT",)] + 8)
                    for h in range(2):
                        g = n + h
                        if i % 2 == 0:
                            pe.wait_ge(gemm_taken, g - 2)
                        b = GEMM_BANKS[g % 3]
                        for c in range(KC):
                            last = pe.matmul(ps[:, b, :], ybT[:, (i % 2) * KC + c, h * P:(h + 1) * P], slot[:, c],
                                             start=(i % 2 == 0 and c == 0), stop=(i % 2 == 1 and c == KC - 1))
                        if i % 2 == 1:
                            last.then_inc(gemm_ready, 1)
                        elif h == 1:
                            last.then_inc(sem("half_summed"), 1)
                    if i % 2 == 1:
                        n += 2
                    blk += 1
                elif kind == "headT":
                    name = step[1]
                    raw, order = {"kx": (kx_raw, 1), "qx": (qx_raw, 2), "q": (q_raw, 3), "k": (k_raw, 4)}[name]
                    pe.wait_ge(sem("head_normed"), order)
                    for c2 in range(4):
                        by_columns(lambda t: raw[:, t], c2)
                elif kind == "scores":
                    m, br, h = step[1:]
                    b = group()
                    if h == 0:
                        first = MISC_AT[("headT", "qx" if br == "x" else "k")] + 4
                        pe.wait_ge(misc_taken, first)
                    for t in range(TT):
                        if br == "x":
                            for j in range(2):
                                last = pe.matmul(ps[:, b, t * MEM:(t + 1) * MEM], qxT[:, 2 * h + j, t * P:(t + 1) * P],
                                                 kxT[:, 2 * h + j], start=(j == 0), stop=(j == 1))
                        else:
                            last = pe.matmul(ps[:, b, t * P:t * P + (t + 1) * P], qz[:, h, t * P:(t + 1) * P],
                                             kT[:, h // 2, 0:(t + 1) * P], start=True, stop=True)
                    last.then_inc(misc_ready, 1)
                elif kind == "probsT":
                    m, br, h = step[1:]
                    b = group()
                    pe.wait_ge(sem("probs"), 2 * m + 2)
                    pr = work[:, m % 2]
                    if br == "x":
                        for k in range(2):
                            for t in range(TT):
                                last = turn(ps[:, b, k * T + t * P:k * T + (t + 1) * P],
                                            pr[:, t * MEM + k * P:t * MEM + (k + 1) * P])
                    else:
                        for j in range(3):
                            last = turn(ps[:, b, j * P:(j + 1) * P], pr[:, j * P:(j + 1) * P])
                    last.then_inc(misc_ready, 1)
                elif kind == "values":
                    m, br, h = step[1:]
                    b = group()
                    pe.wait_ge(misc_taken, MISC_AT[("probsT", m, br, h)] + 1)
                    pT = work[:, 2 + m % 2]
                    if br == "x":
                        pe.wait_ge(gemm_taken, GEMM_AT[("mv", 1, 1)] + 1)
                        for c in range(2):
                            for k in range(2):
                                last = pe.matmul(ps[:, b, c * T:(c + 1) * T],
                                                 vx[:, k, h * X_DIM + c * P:h * X_DIM + (c + 1) * P],
                                                 pT[:, k * T:(k + 1) * T], start=(k == 0), stop=(k == 1))
                    else:
                        pe.wait_ge(gemm_taken, GEMM_AT[("v", 1, 1)] + 1)
                        rows = slice(64 * (h % 2), 64 * (h % 2) + 64)
                        hc = slice(h * A_DIM, (h + 1) * A_DIM)
                        pe.matmul(ps[rows, b, 0:T], v_sb[:, 0, hc], pT[:, 0:T], start=True, stop=False)
                        last = pe.matmul(ps[rows, b, P:T], v_sb[:, 1, hc], pT[:, T:T + P], start=False, stop=True)
                    last.then_inc(misc_ready, 1)
                elif kind == "xsT":
                    j = step[1]
                    b = group()
                    pe.wait_ge(sem("silu_out"), j + 1)
                    for t in range(TT):
                        for c in range(2):
                            last = turn(ps[:, b, (2 * t + c) * P:(2 * t + c + 1) * P],
                                        conv_out[:, j % 2, c, t * P:(t + 1) * P])
                    last.then_inc(misc_ready, 1)
                elif kind == "dt":
                    b = group()
                    for t in range(TT):
                        for c in range(KC):
                            last = pe.matmul(ps[:, b, t * SSM_HEADS:(t + 1) * SSM_HEADS], hT[:, c, t * P:(t + 1) * P],
                                             wdt_sb[:, c], start=(c == 0), stop=(c == KC - 1))
                    last.then_inc(misc_ready, 1)
                elif kind == "decay":
                    b = exp_bank(0)
                    pe.wait_ge(sem("a_ready"), 1)
                    pe.matmul(ps[:, b, 0:SSM_HEADS], after[:], a_sb[:, 0], start=True, stop=True)
                    pe.matmul(ps[:, b, SSM_HEADS:2 * SSM_HEADS], upto[:], a_sb[:, 1], start=True, stop=True)\
                        .then_inc(exp_ready, 1)
                elif kind == "cb":
                    g = step[1]
                    b = group()
                    pe.wait_ge(sem("silu_out"), CONV_T // 2)
                    pe.matmul(ps[:, b, 0:T], bcT[:, g, 0:P], bcT[:, GROUPS + g], start=True, stop=True)
                    pe.matmul(ps[:, b, T:T + P], bcT[:, g, P:T], bcT[:, GROUPS + g, P:T], start=True, stop=True)\
                        .then_inc(misc_ready, 1)
                elif kind == "spread":
                    u, g, t = step[1:]
                    for d in range(2):
                        n_exp = 1 + 2 * u + d
                        b = exp_bank(n_exp)
                        pe.wait_ge(sem("steps_ready"), n_exp)
                        pe.matmul(ps[:, b, :], after[:], work[:, 2 + d], start=True, stop=True).then_inc(exp_ready, 1)
                elif kind == "ssm":
                    u, g, t = step[1:]
                    if t == 1:
                        b = group()
                        pe.matmul(ps[:, b, :], cbm[:, g % 2, 2 * P:3 * P], fx[:, g * GW:(g + 1) * GW],
                                  start=True, stop=True).then_inc(misc_ready, 1)
                    b = group()
                    pe.wait_ge(sem("weighed"), 2 * u + 2)
                    pe.wait_ge(sem("xdt_ready"), 1)
                    for r in range(8):
                        hc = slice(g * GW + r * SSM_DIM, g * GW + (r + 1) * SSM_DIM)
                        last = pe.matmul(ps[:, b, r * SSM_DIM:(r + 1) * SSM_DIM],
                                         work[:, r // 4, (r % 4) * P:(r % 4 + 1) * P], xdt[t][:, hc],
                                         start=True, stop=True)
                    last.then_inc(misc_ready, 1)
                elif kind == "yT":
                    pe.wait_ge(sem("y_normed"), TT)
                    for c2 in range(8):
                        by_columns(lambda t: xs[t], c2)
                elif kind == "mergedT":
                    pe.wait_ge(sem("br_merged"), 12)
                    for c2 in range(4):
                        by_columns(lambda t: merged[:, t], c2)

            pe.wait_ge(sem("h2_ready"), TT)
            for c2 in range(4):
                by_columns(lambda t: h2[:, t], c2)
            b = group()
            pe.wait_ge(misc_taken, MISC_AT["logits"])
            for t in range(TT):
                for c in range(KC):
                    last = pe.matmul(ps[:, b, t * EXPERTS:(t + 1) * EXPERTS], h2T[:, c, t * P:(t + 1) * P], wr_sb[:, c],
                                     start=(c == 0), stop=(c == KC - 1))
            last.then_inc(misc_ready, 1)
            pe.wait_ge(sem("chosen_ready"), 1)
            b = group()
            for t in range(TT):
                last = turn(ps[0:EXPERTS, b, t * P:(t + 1) * P], wts[:, t])
            last.then_inc(misc_ready, 1)
            b = group()
            pe.matmul(ps[:, b, 0:EXPERTS], upto[:], chosen[:, 0], start=True, stop=True)
            pe.matmul(ps[:, b, EXPERTS:2 * EXPERTS], upto[:], chosen[:, 1], start=True, stop=False)
            pe.matmul(ps[:, b, EXPERTS:2 * EXPERTS], ones[:], chosen[:, 0], start=False, stop=True)
            for t in range(TT):
                last = pe.matmul(ps[:, b, 64:64 + EXPERTS], ones[:], chosen[:, t], start=(t == 0), stop=(t == 1))
            last.then_inc(misc_ready, 1)
            pe.wait_ge(misc_taken, MISC_END)
            pe.wait_ge(gemm_taken, GEMM_END)
            pe.wait_ge(sem("bias_rows_landed"), 48)
            pe.wait_ge(exp_taken, 1 + 2 * N_UNITS)
            for t in range(TT):
                for h in range(2):
                    pe.matmul(ps[:, ACC[2 * t + h], :], wT[:, t * P:(t + 1) * P], bias_d[:, h * NB:(h + 1) * NB],
                              start=True, stop=False, skip_group_check=True)

            def gather():
                for c in range(KC):
                    for t in range(TT):
                        last = pe.matmul(ps[:, X_BANK, c * BLK:(c + 1) * BLK], h2[:, t, c * P:(c + 1) * P], hot[:, t],
                                         start=(t == 0), stop=(t == TT - 1))
                last.then_inc(sem("gather_ready"), 1)

            pe.wait_ge(sem("hot_ready"), TT)
            gather()
            pe.wait_ge(sem("passes_known"), 1)
            n_pass = pe.value_load(npass_i[0:1, 0:1], min_val=1, max_val=PASSES)
            with pe.Fori(0, n_pass) as b_:
                with pe.Fori(0, EXPERTS) as e:
                    i = b_ * EXPERTS + e
                    pe.wait_ge(sem("pick_ready"), i + 1)
                    pe.wait_ge(sem("xg_ready"), i + 1)
                    pe.wait_ge(sem("actT_ready"), i)
                    for bank, c0 in ((G_BANK, 0), (U_BANK, D)):
                        for h in range(2):
                            pe.matmul(ps[64 * h:64 * h + 64, bank, :], pick, bias_gu[:, c0 + h * NB:c0 + (h + 1) * NB],
                                      start=True, stop=False, skip_group_check=True)
                    for k in range(2):
                        for bank, w, sl in ((G_BANK, gate_w, 2 * k), (U_BANK, up_w, 2 * k + 1)):
                            pe.wait_ge(e_landed[sl], i * 16 + 16)
                            for c in range(KC // 2):
                                for h in range(2):
                                    last = pe.matmul(ps[64 * h:64 * h + 64, bank, :], xgT[:, k * 4 + c],
                                                     w[k][:, c, h * NB:(h + 1) * NB], start=False,
                                                     stop=(k == 1 and c == 3), skip_group_check=True)
                        last.then_inc(e_used[k], 1)
                    pe.wait_ge(sem("hot_w_ready"), i * TT + TT)
                    pe.wait_ge(sem("yb_ready"), i)
                    for t in range(TT):
                        last = turn(ps[:, D_BANK, t * P:(t + 1) * P], hot_w[:, t].rearrange("p r j -> p (r j)"))
                    last.then_inc(sem("hot_wT_ready"), 1)
                    pe.wait_ge(sem("hot_ready"), i * TT + 2 * TT)
                    gather()
                    pe.wait_ge(sem("act_ready"), i + 1)
                    for c in range(4):
                        last = turn(ps[:, G_BANK, c * P:(c + 1) * P], act_sb[:, c * P:(c + 1) * P])
                    last.then_inc(sem("actT_out"), 1)
                    pe.wait_ge(sem("actT_ready"), i + 1)
                    pe.wait_ge(sem("scatter_ready"), i * 2 + 2)
                    for k in range(2):
                        pe.wait_ge(e_landed[4 + k], i * 16 + 16)
                        for c in range(4):
                            for h in range(2):
                                last = pe.matmul(ps[64 * h:64 * h + 64, D_BANK, :], actT[:, c, 64 * k:64 * k + 64],
                                                 down_w[k][:, c, h * NB:(h + 1) * NB], start=(k == 0 and c == 0),
                                                 stop=(k == 1 and c == 3))
                        last.then_inc(e_used[2 + k], 1)
                    pe.wait_ge(sem("yb_ready"), i + 1)
                    for t in range(TT):
                        for h in range(2):
                            last = pe.matmul(ps[:, ACC[2 * t + h], :], hot_wT[:, h, t], yb, start=False, stop=False,
                                             skip_group_check=True)
                    last.then_inc(sem("scattered"), 1)
            pe.matmul(ps[:, D_BANK, 0:EXPERTS], ident[:], chosen[:, 0], start=True, stop=True)\
                .then_inc(sem("experts_done"), 1)


def kernel(**inputs):
    import numpy as np
    import concourse.bacc as bacc
    from concourse.bass_utils import run_bass_kernel_spmd

    src = {k: np.asarray(v) for k, v in inputs.items()}
    one = {k: v[0] for k, v in src.items() if k not in ("x", "mem")}

    def columns(v):
        return np.ascontiguousarray(v.reshape(-1, P).T)

    args = {
        "x": src["x"], "mem": src["mem"], "g_mix": columns(one["norm_mix"]), "w_in": one["w_in"],
        "w_dt": np.ascontiguousarray(one["w_in"][:, DT0:DT0 + SSM_HEADS]),
        "a_gains": np.stack([np.concatenate([one["a_q_gain"]] * 2), np.concatenate([one["a_k_gain"]] * 2)], 1),
        "rel_rev": np.ascontiguousarray(one["a_rel_bias"][:, ::-1]),
        "conv_w": np.ascontiguousarray(one["conv_w"].reshape(TAPS, CONV_T, P).transpose(2, 1, 0)),
        "conv_b": columns(one["conv_b"]), "dt_bias": one["dt_bias"], "a_log": one["a_log"], "d_skip": one["d_skip"],
        "g_ssm": columns(one["ssm_norm"]), "g_mem": columns(one["norm_mem"]), "w_mem_kv": one["w_mem_kv"],
        "x_gains": np.concatenate([columns(one["x_q_gain"]), columns(one["x_k_gain"])], 1),
        "w_br_a": one["w_br_a"], "w_br_b": one["w_br_b"], "w_br_c": one["w_br_c"], "w_out": one["w_out"],
        "norm_ffn": one["norm_ffn"], "w_router": one["w_router"], "b_router": one["b_router"],
        "w_gate": one["w_gate"], "b_gate": one["b_gate"], "w_up": one["w_up"], "b_up": one["b_up"],
        "w_down": one["w_down"], "b_down": one["b_down"],
    }
    nc = bacc.Bacc("TRN2", target_bir_lowering=False, num_devices=1)
    arrays, aps = {}, []
    for name, a in args.items():
        a = np.ascontiguousarray(a)
        arrays["in_" + name] = a
        aps.append(nc.dram_tensor("in_" + name, a.shape, mybir.dt.from_np(a.dtype), kind="ExternalInput").ap())
    aps.append(nc.dram_tensor("bias_rows", (A_HEADS, P * (SKEW + 1)), F32).ap())
    aps.append(nc.dram_tensor("out_0", (1, T, D), F32, kind="ExternalOutput").ap())
    hybrid_block_kernel(nc, *aps)
    r = run_bass_kernel_spmd(nc, [arrays], core_ids=[0])
    return r.results[0]["out_0"]
```

```python
from contextlib import ExitStack

import concourse.bass as bass
from concourse import mybir

P = 128
F32 = mybir.dt.float32
F32R = mybir.dt.float32r
I32 = mybir.dt.int32
U32 = mybir.dt.uint32
ALU = mybir.AluOpType
ACT = mybir.ActivationFunctionType
AX = mybir.AxisListType.X

EPS = 1e-6
D = 1024
T = 256
TT = T // P
KC = D // P
NB = 512
A_HEADS, A_DIM = 16, 64
X_HEADS, X_DIM = 4, 256
MEM = 256
CHUNK = 64
REL_CLIP = 128
INNER = 2048
GROUPS, STATE, SSM_HEADS, SSM_DIM = 4, 128, 32, 64
GW = INNER // GROUPS
CONV_CH = INNER + 2 * GROUPS * STATE
CONV_T = CONV_CH // P
TAPS = 4
EXPERTS, TOP_K = 32, 4
BLK = 64
PASSES = T // BLK
LIMIT, ALPHA = 7.0, 1.702
MASKED = -1e30
SKEW = 384

Q0, K0, V0, Z0 = 0, D, 2 * D, 3 * D
XBC0 = Z0 + INNER
DT0 = XBC0 + CONV_CH
QX0 = DT0 + SSM_HEADS
GATE0 = QX0 + D

BLOCKS = ([("xbc", i) for i in range(6)] + [("z", i) for i in range(4)] + [("q", i) for i in range(2)]
          + [("k", i) for i in range(2)] + [("v", i) for i in range(2)]
          + [("gb", 0), ("bb", 0), ("bb", 1), ("gb", 1), ("bb", 2), ("bb", 3)]
          + [("qx", i) for i in range(2)] + [("mk", i) for i in range(2)] + [("mv", i) for i in range(2)]
          + [("ga", 0), ("ba", 0), ("ga", 1), ("ba", 1), ("gc", 0), ("bc", 0), ("gc", 1), ("bc", 1)]
          + [("wo", i) for i in range(2)])
BLOCK_AT = {b: n for n, b in enumerate(BLOCKS)}
QUARTERS = 4
UNITS = QUARTERS * len(BLOCKS)
HALVES = 3
SPLITS = 4
GATES = ("gb", "ga", "gc")


def block_groups():
    out = []
    for name, i in BLOCKS:
        if name == "bb":
            if i % 2 == 1:
                out += [(name, i // 2, h) for h in range(2)]
        else:
            out += [(name, i, h) for h in range(2)]
    return out


GEMM = block_groups()
GEMM_AT = {g: n for n, g in enumerate(GEMM)}
HEADS = [("a", h) for h in range(A_HEADS)] + [("x", h) for h in range(X_HEADS)]


def first(name, i=0):
    return QUARTERS * BLOCK_AT[(name, i)]


def block_end(name, i):
    return first(name, 2 * i + 1 if name == "bb" else i) + QUARTERS


def schedule():
    extra = [[] for _ in range(UNITS + 2)]

    def at(w, *step):
        extra[w].append(step)

    for n, (name, i) in enumerate(BLOCKS):
        if name == "bb":
            if i % 2 == 0:
                continue
            i = i // 2
        at(4 * n + 4, "take", name, i)
        if name in ("bb", "ba", "bc"):
            at(4 * n + 5, "merge", name, i)
    for i in range(6):
        w = first("xbc", i)
        at(w + 5, "conv", 2 * i)
        at(w + 6, "silu", 2 * i)
        at(w + 6, "conv", 2 * i + 1)
        at(w + 7, "silu", 2 * i + 1)
        if i < INNER // P // 4:
            at(w + 7, "xsT", 2 * i)
            at(w + 8, "xsT", 2 * i + 1)
    at(first("xbc", 1) + 3, "dt")
    at(first("xbc", 2) + 1, "decay")
    at(first("xbc", 5) + 1, "xdt")
    k0 = first("z", 1)
    for k in range(2 * GROUPS * TT + 1):
        u, d = k // 2, k % 2
        if k >= 2 and d == 0:
            at(k0 + k, "weigh", u - 1, (u - 1) // TT, (u - 1) % TT)
            at(k0 + k, "ssm", u - 1, (u - 1) // TT, (u - 1) % TT)
        if u < GROUPS * TT:
            if k % 4 == 0:
                at(k0 + k, "cb", u // TT)
            at(k0 + k, "spread", u, u // TT, u % TT, d)
    at(first("q", 1) + 2, "ynorm")
    for p in range(4):
        at(first("k", 0) + p, "yT", p)
    at(first("k", 0) + 1, "square", "q")
    at(first("k", 0) + 3, "headnorm", "q")
    at(first("k", 1) + 2, "headT", "q")
    at(first("v", 0) + 1, "square", "k")
    at(first("v", 0) + 3, "headnorm", "k")
    at(first("v", 1) + 1, "headT", "k")

    def attend(w0, lo, hi):
        for slot in range(hi - lo + 2):
            for stage, m in (("scores", lo + slot), ("probsT", lo + slot - 1), ("values", lo + slot - 2),
                             ("soften", lo + slot)):
                if lo <= m < hi:
                    at(w0 + 2 * slot, stage, m, *HEADS[m])

    attend(first("v", 1) + 3, 0, A_HEADS)
    at(first("bb", 2), "memsquare")
    at(first("bb", 2) + 2, "memnorm")
    at(first("qx", 0) + 1, "memT")
    at(first("mk", 0) + 1, "square", "qx")
    at(first("mk", 0) + 3, "headnorm", "qx")
    at(first("mk", 1) + 2, "headT", "qx")
    at(first("mv", 0) + 1, "square", "kx")
    at(first("mv", 0) + 3, "headnorm", "kx")
    at(first("mv", 1) + 1, "headT", "kx")
    attend(first("ga", 0), A_HEADS, A_HEADS + X_HEADS)
    at(first("bc", 1), "mergedT", 0)
    at(first("wo", 0) + 1, "mergedT", 1)
    s = [("hT",)] + [("split", w) for w in range(SPLITS - 1)]
    for w in range(UNITS):
        name, i = BLOCKS[w // QUARTERS]
        s.append(("gemm", name, i, w % QUARTERS, w))
        if w + SPLITS - 1 < UNITS:
            s.append(("split", w + SPLITS - 1))
        s += extra[w]
    return s + extra[UNITS]


SCHED = schedule()
MISC_GROUPS = {"memT": 4, "hT": 4, "headT": 4, "scores": 1, "probsT": 1, "values": 1, "xsT": 1, "dt": 1, "cb": 1,
               "yT": 2, "mergedT": 2}


def misc_index():
    at, n = {}, 0
    for step in SCHED:
        at[step] = n
        n += MISC_GROUPS.get(step[0], 0)
        if step[0] == "ssm":
            n += 1 + step[3]
    at["h2T"], at["logits"], at["wT"], at["places"], at["end"] = n, n + 4, n + 5, n + 6, n + 7
    return at


MISC_AT = misc_index()
N_UNITS = GROUPS * TT


def values_end(m):
    return MISC_AT[("values", m) + HEADS[m]] + 1


def ssm_end(u):
    return MISC_AT[("ssm", u, u // TT, u % TT)] + 1 + u % TT


def hybrid_block_kernel(nc, x, mem, g_mix, w_in, w_dt, a_gains, rel_rev, conv_w, conv_b, dt_bias, a_log, d_skip,
                        g_ssm, g_mem, w_mem_kv, x_gains, w_br_a, w_br_b, w_br_c, w_out, norm_ffn, w_router,
                        b_router, w_gate, b_gate, w_up, b_up, w_down, b_down, bias_dram, out):
    with ExitStack() as ctx:
        def sb(name, shape, dt=F32):
            return ctx.enter_context(nc.sbuf_tensor(name, shape, dt))

        sems = {}

        def sem(name):
            if name not in sems:
                sems[name] = ctx.enter_context(nc.semaphore(name))
            return sems[name]

        REGION = 2048
        N_REGIONS = 14
        PART = 2 * NB
        ARENA = N_REGIONS * REGION + HALVES * REGION + SPLITS * 2 * PART
        base = (nc.sbuf_base + 31) // 32 * 32
        sb("arena", [P, ARENA + 8])

        def placed(name, shape, dt, offset):
            return nc.alloc_sbuf_tensor_at(name, shape, dt, offset=base + 4 * offset)

        S = placed("regions", [P, N_REGIONS, REGION], F32, 0)
        SR = placed("regions_r", [P, N_REGIONS, REGION], F32R, 0)
        halves = placed("halves", [P, HALVES, 4, NB], F32, N_REGIONS * REGION)
        splits = placed("splits", [P, SPLITS, 2, 2, NB], F32R, (N_REGIONS + HALVES) * REGION)
        expert_ring = placed("expert_ring", [P, 3, 2 * REGION], F32, N_REGIONS * REGION)

        def by_token(i):
            return S[:, i].rearrange("p (t d) -> p t d", t=TT)

        def by_channel(i):
            return S[:, i].rearrange("p (c t) -> p c t", c=KC)

        def split_pair(hi, lo):
            return [SR[:, r].rearrange("p (c t) -> p c t", c=KC) for r in (hi, lo)]

        x_sb, xn = by_token(0), by_token(7)
        hT = split_pair(1, 0)
        conv_acc = S[:, 5, 0:1024].rearrange("p (b j t) -> p b j t", b=2, j=2)
        conv_out = S[:, 5, 1024:2048].rearrange("p (b j t) -> p b j t", b=2, j=2)
        xs = [S[:, 2], S[:, 3]]
        bcT = by_channel(8)
        xdt = [S[:, 7], S[:, 10]]
        fx = S[:, 11]
        sq_junk, y_off = S[:, 12, 0:NB], S[:, 12, NB:2 * NB]
        zbuf = S[:, 13].rearrange("p (b t n) -> p b t n", b=2, t=TT)
        ybT = [SR[:, 12:14].rearrange("p a (c t) -> p (a c) t", t=T), SR[:, 10:12].rearrange("p a (c t) -> p (a c) t", t=T)]
        q_raw, k_raw, v_sb = by_token(4), by_token(9), by_token(6)
        squares = {"q": S[:, 5], "k": S[:, 5], "qx": S[:, 8], "kx": S[:, 8]}
        qz = S[:, 2:4].rearrange("p a (h t) -> p (a h) t", t=T)
        kT = by_channel(7)
        yaT = split_pair(4, 9)
        rel_sb = S[0:A_HEADS, 12, 0:512]
        mem_sb = by_token(8)
        memT = split_pair(10, 11)
        qx_raw, kx_raw, vx = by_token(12), by_token(13), by_token(2)
        kxT, qxT = by_channel(3), by_channel(6)
        ycT = split_pair(7, 12)
        merged = by_token(5)
        mergedT = split_pair(1, 6)
        h2, h2T = by_token(12), by_channel(13)
        gain2 = S[:, 4, 0:D]
        sq2 = by_token(7)

        eslots = ([S[:, r:r + 2].rearrange("p a (c n) -> p (a c) n", n=D) for r in (10, 2, 8)]
                  + [expert_ring[:, k].rearrange("p (c n) -> p c n", n=D) for k in range(3)])
        gate_w, up_w, down_w = [eslots[0], eslots[2]], [eslots[1], eslots[3]], [eslots[4], eslots[5]]

        xgT = S[:, 4, 0:512].rearrange("p (c j) -> p c j", c=KC)
        g_sb, u_sb = S[:, 4, 512:1024], S[:, 4, 1024:1536]
        sg_sb, gu_sb = S[:, 4, 1536:2048], S[:, 7, 0:512]
        act_sb, actT = S[:, 7, 512:1024], S[:, 7, 1024:1536].rearrange("p (c j) -> p c j", c=4)
        yb = S[:, 7, 1536:2048]
        bias_gu = S[:, 6]
        bias_d = S[:, 5, 0:D]
        pick = S[:, 5, 1024:1024 + BLK]
        hot = S[:, 5, 1088:1088 + TT * BLK].rearrange("p (t j) -> p t j", t=TT)
        hot_w = S[:, 5, 1216:1216 + TT * 2 * BLK].rearrange("p (t r j) -> p t r j", t=TT, r=2)
        hot_wT = S[:, 5, 1472:1472 + 512].rearrange("p (h t j) -> p h t j", h=2, t=TT)
        NPAD = PASSES * EXPERTS + 1
        place4 = S[:, 1, 0:TT * NPAD].rearrange("p (t i) -> p t i", t=TT)
        weight4 = S[:, 1, 320:320 + TT * PASSES * EXPERTS].rearrange("p (t i) -> p t i", t=TT)
        picks = S[:, 1, 640:640 + PASSES * EXPERTS]
        wT = S[:, 1, 800:800 + T]
        y_out = by_token(13)

        bias4 = sb("bias4", [P, 4, T])
        sig = sb("sig", [P, TT, NB])
        wdt_r = sb("wdt_r", [P, 2, KC, SSM_HEADS], F32R)
        ident = sb("ident", [P, P])
        upto = sb("upto", [P, P])
        after = sb("after", [P, P])
        ones = sb("ones", [P, P])
        iota_i = sb("iota_i", [P, BLK], I32)
        iota_j = sb("iota_j", [P, BLK])
        iota2 = sb("iota2", [P, 2, BLK])
        steps_b = sb("steps_b", [P, PASSES])
        gm_sb = sb("gm_sb", [P, KC])
        gmem_sb = sb("gmem_sb", [P, KC])
        gssm_sb = sb("gssm_sb", [P, INNER // P])
        ag_sb = sb("ag_sb", [P, 2])
        xg_sb = sb("xg_sb", [P, 4])
        cw_sb = sb("cw_sb", [P, CONV_T, TAPS])
        cb_sb = sb("cb_sb", [P, CONV_T])
        head_rows = sb("head_rows", [P, 4, SSM_HEADS])
        wdt_sb = sb("wdt_sb", [P, KC, SSM_HEADS])
        wr_sb = sb("wr_sb", [P, KC, EXPERTS])
        craw = sb("craw", [P, 2, 2, T + TAPS])
        work = sb("work", [P, 4, NB])
        tmp = sb("tmp", [P, 2, NB])
        cbm = sb("cbm", [P, 2, 384])
        stat = sb("stat", [P, 256])
        ss_x, rs_x = stat[:, 0:2], stat[:, 4:6]
        ss_h = stat[:, 8:40]
        mx, rc = stat[:, 40:42], stat[:, 42:44]
        nmx = stat[:, 192:196].rearrange("p (b t) -> p b t", b=2)
        sums = stat[:, 196:200].rearrange("p (b t) -> p b t", b=2)
        ss_m, rs_m = stat[:, 200:202], stat[:, 202:204]
        ss_y = stat[:, 49:57]
        ss_2 = stat[:, 57:59]
        rs_2 = stat[:, 59:61]
        npass_f, cmax = stat[:, 61:62], stat[:, 62:63]
        over = stat[:, 64:68]
        mx8 = stat[:, 72:88].rearrange("p (t k) -> p t k", t=TT)
        idxf = stat[:, 88:104].rearrange("p (t k) -> p t k", t=TT)
        e4 = stat[:, 104:112].rearrange("p (t k) -> p t k", t=TT)
        s4 = stat[:, 112:114]
        root_in, root_out = stat[:, 128:160], stat[:, 160:192]
        idx8 = sb("idx8", [P, TT, 8], U32)
        npass_i = sb("npass_i", [1, 1], I32)
        dtw = sb("dtw", [P, 6, TT * SSM_HEADS])
        dt_sb = dtw[:, 4].rearrange("p (t h) -> p t h", t=TT)
        a_sb = dtw[:, 5].rearrange("p (t h) -> p t h", t=TT)
        a_head = sb("a_head", [P, SSM_HEADS])
        decays = sb("decays", [P, 2, SSM_HEADS])
        rt = sb("rt", [P, 4, TT * EXPERTS])
        logits = rt[:, 0].rearrange("p (t e) -> p t e", t=TT)
        wts = rt[:, 1].rearrange("p (t e) -> p t e", t=TT)
        part = rt[:, 2].rearrange("p (t e) -> p t e", t=TT)
        chosen = rt[:, 3].rearrange("p (t e) -> p t e", t=TT)

        ps = ctx.enter_context(nc.psum_tensor("ps", [P, 8, NB], F32))
        GEMM_BANKS, EXP_BANK, MISC_BANKS = (0, 1, 2, 3), 7, (4, 5, 6)
        ACC, G_BANK, U_BANK, X_BANK, D_BANK = (0, 1, 2, 3), 4, 5, 6, 7

        gemm_taken = sem("gemm_taken")
        misc_ready, misc_taken = sem("misc_ready"), sem("misc_taken")
        exp_ready, exp_taken = sem("exp_ready"), sem("exp_taken")
        landed = [sem(f"half_landed{k}") for k in range(HALVES)]
        bias_landed = [sem(f"bias_landed{k}") for k in range(4)]
        hi_ready, lo_ready, lo_ready_pool = sem("rounded"), sem("rest_by_vector"), sem("rest_by_pool")
        unit_used = sem("quarter_used")
        e_landed = [sem(f"expert_landed{k}") for k in range(6)]
        e_used = [sem(f"{n}_used") for n in ("gate_up0", "gate_up1", "down0", "down1")]
        MISC_END = MISC_AT["end"]
        GEMM_END = len(GEMM)

        def pool_rests(n):
            return n // QUARTERS

        def quarter(w):
            m = w // 2
            return halves[:, m % HALVES, 2 * (w % 2):2 * (w % 2) + 2], splits[:, w % SPLITS, 0], splits[:, w % SPLITS, 1]

        def weight_src(name, i):
            def rows(w, c0):
                return w.rearrange("(c p) n -> p c n", p=P)[:, :, c0:c0 + NB]
            if name in ("mk", "mv"):
                return rows(w_mem_kv, (0 if name == "mk" else D) + i * NB)
            if name in ("bc", "ba", "wo"):
                return rows({"bc": w_br_c, "ba": w_br_a, "wo": w_out}[name], i * NB)
            if name == "bb":
                return w_br_b[(i % 2) * D:(i % 2 + 1) * D].rearrange("(c p) n -> p c n", p=P)[
                    :, :, (i // 2) * NB:(i // 2 + 1) * NB]
            c0 = {"q": Q0, "k": K0, "v": V0, "z": Z0, "xbc": XBC0, "qx": QX0,
                  "ga": GATE0, "gb": GATE0 + D, "gc": GATE0 + 2 * D}[name]
            return rows(w_in, c0 + i * NB)

        def expert_src(k, e):
            w = (w_gate, w_up, w_gate, w_up, w_down, w_down)[k]
            half = (0, 0, 1, 1, 0, 1)[k]
            return w[e].rearrange("(h c p) n -> h p c n", h=2, p=P)[half]

        block = ctx.enter_context(nc.Block())

        @block.sync
        def _(sp):
            def load(m):
                name, i = BLOCKS[m // 2]
                if m >= HALVES:
                    done = 2 * (m - HALVES) + 2
                    sp.wait_ge(lo_ready, done - pool_rests(done))
                    if pool_rests(done):
                        sp.wait_ge(lo_ready_pool, pool_rests(done))
                sp.dma_start(halves[:, m % HALVES], weight_src(name, i)[:, 4 * (m % 2):4 * (m % 2) + 4])\
                    .then_inc(landed[m % HALVES], 16)

            sp.dma_start(x_sb, x.rearrange("a (t p) d -> p (a t) d", p=P)).then_inc(sem("x_landed"), 16)
            sp.dma_start(gm_sb[:], g_mix).then_inc(sem("gain_landed"), 16)
            for m in range(HALVES):
                load(m)
            sp.wait_ge(sem("rel_edge"), 2)
            skewed = bass.AP(tensor=bias_dram.tensor, offset=0, ap=[[P * (SKEW + 1), A_HEADS], [SKEW + 1, P], [1, SKEW]])
            sp.dma_start(skewed, rel_sb[:, 0:SKEW].unsqueeze(1).to_broadcast([A_HEADS, P, SKEW]))\
                .then_inc(sem("rel_stored"), 16)
            for m in range(HALVES, 2 * len(BLOCKS)):
                if m == 2 * BLOCK_AT[("gb", 0)]:
                    sp.wait_ge(misc_ready, ssm_end(N_UNITS - 1))
                    sp.dma_start(mem_sb, mem.rearrange("a (t p) d -> p (a t) d", p=P)).then_inc(sem("mem_landed"), 16)
                if m == 2 * BLOCK_AT[("gc", 0)]:
                    sp.wait_ge(unit_used, first("mv", 1) + 4)
                    sp.dma_start(eslots[0], expert_src(0, 0)).then_inc(e_landed[0], 16)
                if m == 2 * BLOCK_AT[("bc", 0)]:
                    sp.wait_ge(misc_ready, values_end(A_HEADS + X_HEADS - 1))
                    sp.dma_start(eslots[1], expert_src(1, 0)).then_inc(e_landed[1], 16)
                if m == 2 * BLOCK_AT[("bc", 1)]:
                    sp.wait_ge(unit_used, first("ba", 1) + 4)
                    sp.dma_start(eslots[2], expert_src(2, 0)).then_inc(e_landed[2], 16)
                if m == 2 * BLOCK_AT[("wo", 1)]:
                    sp.wait_ge(unit_used, first("gc", 1) + 4)
                    sp.dma_start(x_sb, x.rearrange("a (t p) d -> p (a t) d", p=P)).then_inc(sem("x_again"), 16)
                    sp.dma_start(gain2, norm_ffn.partition_broadcast(P)).then_inc(sem("gain2_landed"), 16)
                load(m)
            sp.wait_ge(lo_ready, UNITS - pool_rests(UNITS))
            sp.wait_ge(lo_ready_pool, pool_rests(UNITS))
            sp.dma_start(eslots[3], expert_src(3, 0)).then_inc(e_landed[3], 16)
            sp.wait_ge(unit_used, UNITS)
            for k in (4, 5):
                sp.dma_start(eslots[k], expert_src(k, 0)).then_inc(e_landed[k], 16)
            sp.wait_ge(sem("bias_rows_zero"), 2)
            sp.dma_start(bias_gu[0:EXPERTS, 0:D], b_gate).then_inc(sem("bias_rows_landed"), 16)
            sp.dma_start(bias_gu[0:EXPERTS, D:2 * D], b_up).then_inc(sem("bias_rows_landed"), 16)
            sp.dma_start(bias_d[0:EXPERTS, :], b_down).then_inc(sem("bias_rows_landed"), 16)

            def expert_loads(i, e):
                for k in range(6):
                    sp.wait_ge(e_used[(0, 0, 1, 1, 2, 3)[k]], i)
                    sp.dma_start(eslots[k], expert_src(k, e)).then_inc(e_landed[k], 16)

            with sp.Fori(1, EXPERTS) as e:
                expert_loads(e, e)
            sp.wait_ge(sem("passes_known"), 1)
            n_pass = sp.value_load(npass_i[0:1, 0:1], min_val=1, max_val=PASSES)
            with sp.If(n_pass > 1):
                with sp.Fori(1, n_pass) as b:
                    with sp.Fori(0, EXPERTS) as e:
                        expert_loads(b * EXPERTS + e, e)
            for t in range(TT):
                sp.wait_ge(sem("y_ready"), 2 * t + 2)
                sp.dma_start(out.rearrange("a (t p) d -> t p (a d)", p=P)[t], y_out[:, t]).then_inc(sem("y_stored"), 16)
            sp.wait_ge(sem("y_stored"), 16 * TT)

        @block.gpsimd
        def _(pool):
 
            pool.memset(ones[:], 1.0).then_inc(sem("ones_set"), 1)
            pool.wait_ge(sem("ones_set"), 1)
            pool.affine_select(out=ident[:], in_=ones[:], compare_op=ALU.is_equal, fill=0.0, base=0,
                               pattern=[[-1, P]], channel_multiplier=1).then_inc(sem("masks"), 1)
            pool.affine_select(out=upto[:], in_=ones[:], compare_op=ALU.is_ge, fill=0.0, base=0,
                               pattern=[[1, P]], channel_multiplier=-1).then_inc(sem("masks"), 1)
            pool.affine_select(out=after[:], in_=ones[:], compare_op=ALU.is_ge, fill=0.0, base=-1,
                               pattern=[[-1, P]], channel_multiplier=1).then_inc(sem("masks"), 1)
            pool.iota(iota_i[:], pattern=[[1, BLK]], base=0, channel_multiplier=0).then_inc(sem("iota"), 1)
            pool.memset(craw[:], 0.0).then_inc(sem("craw_zero"), 1)
            small = sem("small_landed")
            pool.dma_start(cw_sb[:], conv_w).then_inc(small, 16)
            pool.dma_start(cb_sb[:], conv_b).then_inc(small, 16)
            pool.dma_start(wdt_sb[:], w_dt.rearrange("(c p) n -> p c n", p=P)).then_inc(small, 16)
            pool.dma_start(gmem_sb[:], g_mem).then_inc(small, 16)
            pool.dma_start(gssm_sb[:], g_ssm).then_inc(small, 16)
            pool.dma_start(ag_sb[:], a_gains).then_inc(small, 16)
            pool.dma_start(xg_sb[:], x_gains).then_inc(small, 16)
            pool.dma_start(wr_sb[:], w_router.rearrange("(c p) n -> p c n", p=P)).then_inc(small, 16)
            for j, row in enumerate((dt_bias, a_log, d_skip, b_router)):
                pool.dma_start(head_rows[:, j], row.partition_broadcast(P)).then_inc(small, 16)
            pool.dma_start(rel_sb[:, 127:384], rel_rev).then_inc(sem("rel_landed"), 16)

            def heads(v):
                return v.rearrange("p (h d) -> p h d", d=SSM_DIM)

            def by_head(v):
                return v.unsqueeze(2).to_broadcast([P, SSM_HEADS, SSM_DIM])

            for step in SCHED:
                kind = step[0]
                if kind == "split" and step[1] % QUARTERS == QUARTERS - 1:
                    w = step[1]
                    raw, hi, lo = quarter(w)
                    pool.wait_ge(hi_ready, w + 1)
                    pool.tensor_tensor(lo, raw, hi.bitcast(F32), ALU.subtract).then_inc(lo_ready_pool, 1)
                elif kind == "xdt":
                    pool.wait_ge(misc_taken, MISC_AT[("xsT", INNER // P // 2 - 1)] + 1)
                    pool.wait_ge(sem("xs_first"), INNER // P // 2)
                    pool.wait_ge(sem("a_ready"), 1)
                    pool.wait_ge(exp_taken, 1)
                    for t in range(TT):
                        pool.tensor_tensor(heads(xdt[t]), heads(xs[t]), by_head(dt_sb[:, t]), ALU.mult)\
                            .then_inc(sem("xdt_ready"), 1)
                        pool.wait_ge(sem("xdt_ready"), 2 * t + 1)
                        pool.tensor_tensor(heads(xs[t]), heads(xs[t]), by_head(head_rows[:, 2]), ALU.mult)\
                            .then_inc(sem("xdt_ready"), 1)
                    pool.tensor_tensor(heads(fx), heads(xdt[0]), by_head(decays[:, 0]), ALU.mult)\
                        .then_inc(sem("xdt_ready"), 1)
                elif kind == "spread":
                    u, g, t, d = step[1:]
                    n = 2 * u + d
                    h0 = g * (SSM_HEADS // GROUPS) + 4 * d
                    if n >= 2:
                        pool.wait_ge(exp_ready, n)
                    pool.tensor_tensor(work[:, 2 + d].rearrange("p (h l) -> p h l", h=4),
                                       upto[:].unsqueeze(1).to_broadcast([P, 4, P]),
                                       a_sb[:, t, h0:h0 + 4].unsqueeze(2).to_broadcast([P, 4, P]),
                                       ALU.mult).then_inc(sem("steps_ready"), 1)
                elif kind == "headnorm" and step[1] == "q":
                    pool.wait_ge(misc_ready, MISC_AT[("yT", 3)] + 2)
                    pool.memset(qz, 0.0).then_inc(sem("qz_zero"), 1)
            pool.wait_ge(gemm_taken, GEMM_END)
            pool.wait_ge(sem("br_merged"), 16)
            pool.memset(bias_gu, 0.0).then_inc(sem("bias_rows_zero"), 1)
            pool.memset(S[:, 5], 0.0).then_inc(sem("bias_rows_zero"), 1)
            pool.wait_ge(sem("out_squares"), TT)
            pool.memset(S[:, 1, 0:1100], 0.0).then_inc(sem("tables_zero"), 1)

        @block.scalar
        def _(act):
            roots = [0]

            def root(width):
                roots[0] += 1
                act.wait_ge(sem("variance"), roots[0])
                act.activation(root_out[:, 0:width], root_in[:, 0:width], ACT.Sqrt).then_inc(sem("root_ready"), 1)

            def exp_group(i):
                act.wait_ge(exp_ready, i + 1)

            def load_bias(h):
                src = bass.AP(tensor=bias_dram.tensor, offset=h * P * (SKEW + 1) + 127, ap=[[SKEW, P], [1, T]])
                act.dma_start(bias4[:, h % 4], src).then_inc(bias_landed[h % 4], 16)

            act.wait_ge(sem("rel_landed"), 16)
            act.activation(rel_sb[:, 0:127], rel_sb[:, 127:128].to_broadcast([A_HEADS, 127]), ACT.Copy)\
                .then_inc(sem("rel_edge"), 1)
            act.activation(rel_sb[:, 384:512], rel_sb[:, 383:384].to_broadcast([A_HEADS, 128]), ACT.Copy)\
                .then_inc(sem("rel_edge"), 1)
            act.wait_ge(sem("x_landed"), 16)
            for t in range(TT):
                act.activation(q_raw[:, t], x_sb[:, t], ACT.Square, accum_out=ss_x[:, t:t + 1])\
                    .then_inc(sem("row_squares"), 1)
            root(TT)
            n = 0
            br = 0
            n_gates = 0
            for step in SCHED:
                kind = step[0]
                if kind == "headnorm":
                    root(TT * (X_HEADS if step[1] in ("kx", "qx") else A_HEADS))
                elif kind == "ynorm":
                    root(N_UNITS)
                elif kind == "memnorm":
                    root(TT)
                elif kind == "split":
                    w = step[1]
                    raw, hi, lo = quarter(w)
                    if w % 2 == 0:
                        act.wait_ge(landed[w // 2 % HALVES], 16 * (w // 2 // HALVES + 1))
                    if w >= SPLITS:
                        act.wait_ge(unit_used, w - SPLITS + 1)
                    act.activation(hi, raw, ACT.Copy).then_inc(hi_ready, 1)
                elif kind == "take":
                    name, i = step[1:]
                    cols = slice(i * NB, (i + 1) * NB)
                    if name in GATES and n_gates:
                        act.wait_ge(sem("br_merged"), 2 * n_gates)
                    n_gates += name in GATES
                    for h in range(2):
                        act.wait_ge(unit_used, block_end(name, i))
                        src = ps[:, GEMM_BANKS[n % 4], :]
                        func = ACT.Copy
                        if name in ("q", "k", "v", "qx", "mk", "mv"):
                            dst = {"q": q_raw, "k": k_raw, "v": v_sb, "qx": qx_raw, "mk": kx_raw, "mv": vx}[name][:, h, cols]
                            if h == 0 and name == "mv" and i == 0:
                                act.wait_ge(misc_ready, values_end(A_HEADS - 1))
                        elif name == "xbc":
                            j = 2 * i + h
                            if j == 0:
                                act.wait_ge(sem("craw_zero"), 1)
                            if j >= 2:
                                act.wait_ge(sem("conv_done"), j - 1)
                            dst = craw[:, j % 2, :, TAPS - 1:TAPS - 1 + T]
                            src = src.rearrange("p (j t) -> p j t", j=2)
                        elif name == "z":
                            if i >= 2:
                                act.wait_ge(sem("gated"), 2 * (i - 2) + h + 1)
                            dst, func = zbuf[:, i % 2, h], ACT.Silu
                        elif name in GATES:
                            dst, func = sig[:, h], ACT.Sigmoid
                        else:
                            if br >= 2:
                                act.wait_ge(sem("br_merged"), br - 1)
                            dst = tmp[:, br % 2]
                            br += 1
                        act.activation(dst, src, func).then_inc(gemm_taken, 1)
                        n += 1
                elif kind == "square":
                    name = step[1]
                    src, last, order = {"q": (4, ("q", 1, 1), 0), "k": (9, ("k", 1, 1), 1), "qx": (12, ("qx", 1, 1), 2),
                                        "kx": (13, ("mk", 1, 1), 3)}[name]
                    act.wait_ge(gemm_taken, GEMM_AT[last] + 1)
                    if order:
                        act.wait_ge(sem("head_sums"), order)
                    if name == "q":
                        act.wait_ge(misc_ready, MISC_AT[("xsT", INNER // P // 2 - 1)] + 1)
                        act.wait_ge(sem("silu_out"), CONV_T // 2)
                    if name == "qx":
                        act.wait_ge(misc_ready, MISC_AT[("memT",)] + 4)
                    act.activation(squares[name], S[:, src], ACT.Square).then_inc(sem("head_squares"), 1)
                elif kind == "memsquare":
                    act.wait_ge(sem("mem_landed"), 16)
                    for t in range(TT):
                        act.wait_ge(sem("br_merged"), br)
                        act.activation(tmp[:].rearrange("p a n -> p (a n)"), mem_sb[:, t], ACT.Square,
                                       accum_out=ss_m[:, t:t + 1]).then_inc(sem("mem_squares"), 1)
                        act.wait_ge(sem("mem_squares"), t + 1)
                elif kind == "scores":
                    m, br_name, h = step[1:]
                    act.wait_ge(misc_taken, MISC_AT[step] + 1)
                    act.wait_ge(sem("maxima"), m + 1)
                    bounds = ((0, MEM), (MEM, 2 * MEM)) if br_name == "x" else ((0, P), (P, 3 * P))
                    for t, (lo, hi) in enumerate(bounds):
                        act.activation(work[:, m % 2, lo:hi], work[:, m % 2, lo:hi], ACT.Exp, bias=nmx[:, m % 2, t:t + 1],
                                       accum_out=sums[:, m % 2, t:t + 1]).then_inc(sem("exp_out"), 1)
                    if br_name == "a" and h + 4 < A_HEADS:
                        load_bias(h + 4)
                elif kind == "silu":
                    j = step[1]
                    act.wait_ge(sem("conv_done"), j + 1)
                    if 2 * j < INNER // P:
                        if j >= 2:
                            act.wait_ge(misc_ready, MISC_AT[("xsT", j - 2)] + 1)
                        dst = conv_out[:, j % 2]
                    else:
                        dst = bcT[:, 2 * j - INNER // P:2 * j - INNER // P + 2, :]
                    act.activation(dst, conv_acc[:, j % 2], ACT.Silu).then_inc(sem("silu_out"), 1)
                elif kind == "dt":
                    act.wait_ge(sem("dt_abs"), 1)
                    act.activation(dtw[:, 1], dtw[:, 1], ACT.Exp, scale=-1.0).then_inc(sem("dt_exp"), 1)
                    act.wait_ge(sem("dt_exp"), 1)
                    act.wait_ge(sem("dt_one"), 1)
                    act.activation(dtw[:, 3], dtw[:, 2], ACT.Ln).then_inc(sem("dt_ln"), 1)
                    act.activation(a_head[:], head_rows[:, 1], ACT.Exp).then_inc(sem("a_exp"), 1)
                elif kind == "decay":
                    exp_group(0)
                    act.activation(decays[:].rearrange("p a h -> p (a h)"), ps[:, EXP_BANK, 0:2 * SSM_HEADS],
                                   ACT.Exp).then_inc(exp_taken, 1)
                    act.wait_ge(sem("rel_stored"), 16)
                    for h in range(4):
                        load_bias(h)
                elif kind == "spread":
                    u, d = step[1], step[4]
                    exp_group(1 + 2 * u + d)
                    if u:
                        act.wait_ge(misc_ready, ssm_end(u - 1))
                    act.activation(work[:, d], ps[:, EXP_BANK, :], ACT.Exp).then_inc(exp_taken, 1)
                elif kind == "ssm":
                    u, g, t = step[1:]
                    act.wait_ge(sem("gated"), u + 1)
                    if u:
                        act.wait_ge(sem("y_squares"), u)
                    act.activation(sq_junk, xs[t][:, g * GW:(g + 1) * GW], ACT.Square,
                                   accum_out=ss_y[:, t * GROUPS + g:t * GROUPS + g + 1]).then_inc(sem("y_squares"), 1)
            act.wait_ge(sem("br_merged"), 16)
            for t in range(TT):
                act.activation(sq2[:, t], x_sb[:, t], ACT.Square, accum_out=ss_2[:, t:t + 1])\
                    .then_inc(sem("out_squares"), 1)
            root(TT)
            act.wait_ge(sem("top_shifted"), 1)
            act.activation(e4, e4, ACT.Exp).then_inc(sem("top_exp"), 1)
            act.wait_ge(sem("gather_ready"), 1)
            act.activation(xgT.rearrange("p c j -> p (c j)"), ps[:, X_BANK, :], ACT.Copy).then_inc(sem("xg_ready"), 1)
            act.wait_ge(sem("passes_known"), 1)
            n_pass = act.value_load(npass_i[0:1, 0:1], min_val=1, max_val=PASSES)
            with act.Fori(0, n_pass) as b:
                with act.Fori(0, EXPERTS) as e:
                    i = b * EXPERTS + e
                    act.wait_ge(sem("g_ready"), i + 1)
                    act.activation(sg_sb, g_sb, ACT.Sigmoid, scale=ALPHA).then_inc(sem("sg_ready"), 1)
                    act.wait_ge(sem("hot_wT_ready"), i + 1)
                    for h in range(2):
                        act.activation(hot_wT[64 * h:64 * h + 64, h],
                                       ps[64 * h:64 * h + 64, D_BANK, 0:T].rearrange("p (t j) -> p t j", t=TT),
                                       ACT.Copy).then_inc(sem("scatter_ready"), 1)
                    act.wait_ge(sem("gather_ready"), i + 2)
                    act.activation(xgT.rearrange("p c j -> p (c j)"), ps[:, X_BANK, :], ACT.Copy)\
                        .then_inc(sem("xg_ready"), 1)
                    act.wait_ge(sem("actT_out"), i + 1)
                    act.activation(actT.rearrange("p c j -> p (c j)"), ps[:, G_BANK, :], ACT.Copy)\
                        .then_inc(sem("actT_ready"), 1)

        @block.vector
        def _(dve):
            chain = [0]

            def link(ins):
                chain[0] += 1
                ins.then_inc(sem("vector_chain"), 1)
                dve.wait_ge(sem("vector_chain"), chain[0])

            misc = [0]
            roots = [0]

            def group():
                misc[0] += 1
                dve.wait_ge(misc_ready, misc[0])
                return MISC_BANKS[(misc[0] - 1) % 3]

            def rstd(dst, src, width):
                roots[0] += 1
                n = dst.shape[1]
                v, r = root_in[:, 0:n], root_out[:, 0:n]
                dve.tensor_scalar(v, src, 1.0 / width, EPS, ALU.mult, ALU.add).then_inc(sem("variance"), 1)
                dve.wait_ge(sem("root_ready"), roots[0])
                link(dve.reciprocal(dst, r))
                link(dve.tensor_tensor(r, dst, v, ALU.mult))
                link(dve.tensor_tensor(r, r, dst, ALU.mult))
                link(dve.tensor_scalar(r, r, -0.5, 1.5, ALU.mult, ALU.add))
                link(dve.tensor_tensor(dst, dst, r, ALU.mult))

            dve.wait_ge(sem("iota"), 1)
            link(dve.tensor_copy(iota_j[:], iota_i[:]))
            dve.tensor_copy(iota2[:], iota_j[:].unsqueeze(1).to_broadcast([P, 2, BLK])).then_inc(sem("vector_side"), 1)
            dve.tensor_scalar(steps_b[:], iota_j[:, 0:PASSES], float(BLK), None, ALU.mult).then_inc(sem("vector_side"), 1)
            dve.wait_ge(sem("row_squares"), 2)
            rstd(rs_x, ss_x, D)
            for t in range(TT):
                dve.tensor_scalar(xn[:, t], x_sb[:, t], rs_x[:, t:t + 1], None, ALU.mult).then_inc(sem("rows_scaled"), 1)

            def split_out(pair, c, src, gain, signal):
                hi, lo = pair[0][:, c], pair[1][:, c]
                g = 1.0 if gain is None else gain
                link(dve.tensor_scalar(hi, src, g, None, ALU.mult))
                ins = dve.scalar_tensor_tensor(out=lo, in0=src, scalar=g, in1=hi.bitcast(F32), op0=ALU.mult,
                                               op1=ALU.subtract)
                if signal:
                    ins.then_inc(misc_taken, 1)
                else:
                    chain[0] += 1
                    ins.then_inc(sem("vector_chain"), 1)

            br = 0
            norms = 0
            for step in SCHED:
                kind = step[0]
                if kind in ("memT", "hT"):
                    pair, gain = (memT, gmem_sb) if kind == "memT" else (hT, gm_sb)
                    if kind == "hT":
                        dve.wait_ge(sem("gain_landed"), 16)
                        dve.wait_ge(sem("rows_scaled"), 2)
                    for c2 in range(4):
                        b = group()
                        for j in range(2):
                            c = 2 * c2 + j
                            split_out(pair, c, ps[:, b, j * T:(j + 1) * T], gain[:, c:c + 1], j == 1)
                        dve.wait_ge(sem("vector_chain"), chain[0])
                    if kind == "hT":
                        dve.wait_ge(sem("small_landed"), 16 * 12)
                        link(dve.tensor_copy(wdt_r[:, 0], wdt_sb[:]))
                        dve.tensor_tensor(wdt_r[:, 1], wdt_sb[:], wdt_r[:, 0].bitcast(F32), ALU.subtract)\
                            .then_inc(sem("wdt_ready"), 1)
                elif kind == "split":
                    w = step[1]
                    if w % QUARTERS != QUARTERS - 1:
                        raw, hi, lo = quarter(w)
                        dve.wait_ge(hi_ready, w + 1)
                        dve.tensor_tensor(lo, raw, hi.bitcast(F32), ALU.subtract).then_inc(lo_ready, 1)
                elif kind == "memnorm":
                    dve.wait_ge(sem("mem_squares"), TT)
                    rstd(rs_m, ss_m, D)
                    for t in range(TT):
                        dve.tensor_scalar(mem_sb[:, t], mem_sb[:, t], rs_m[:, t:t + 1], None, ALU.mult)\
                            .then_inc(sem("mem_scaled"), 1)
                elif kind == "headnorm":
                    raw, heads = {"kx": (kx_raw, X_HEADS), "qx": (qx_raw, X_HEADS),
                                  "q": (q_raw, A_HEADS), "k": (k_raw, A_HEADS)}[step[1]]
                    norms += 1
                    dve.wait_ge(sem("head_squares"), norms)
                    w = D // heads
                    ss = ss_h[:, 0:TT * heads]
                    dve.tensor_reduce(ss, squares[step[1]].rearrange("p (th d) -> p th d", d=w), AX, ALU.add)\
                        .then_inc(sem("head_sums"), 1)
                    dve.wait_ge(sem("head_sums"), norms)
                    rstd(ss, ss, w)
                    view = raw[:].rearrange("p t (h d) -> p (t h) d", d=w)
                    dve.tensor_tensor(view, view, ss.unsqueeze(2).to_broadcast([P, TT * heads, w]), ALU.mult)\
                        .then_inc(sem("head_normed"), 1)
                elif kind == "headT":
                    name = step[1]
                    if name == "q":
                        dve.wait_ge(sem("qz_zero"), 1)
                    for c2 in range(4):
                        b = group()
                        for j in range(2):
                            c = 2 * c2 + j
                            src = ps[:, b, j * T:(j + 1) * T]
                            if name == "kx":
                                last = dve.tensor_scalar(kxT[:, c], src, xg_sb[:, 2 + j:3 + j], None, ALU.mult)
                            elif name == "qx":
                                last = dve.tensor_scalar(qxT[:, c], src, xg_sb[:, j:j + 1], X_DIM ** -0.5,
                                                         ALU.mult, ALU.mult)
                            elif name == "k":
                                last = dve.tensor_scalar(kT[:, c], src, ag_sb[:, 1:2], None, ALU.mult)
                            else:
                                for r in range(2):
                                    rows = slice(64 * r, 64 * r + 64)
                                    last = dve.tensor_scalar(qz[rows, 2 * c + r], src[rows], ag_sb[rows, 0:1],
                                                             A_DIM ** -0.5, ALU.mult, ALU.mult)
                        last.then_inc(misc_taken, 1)
                elif kind == "scores":
                    m, br_name, h = step[1:]
                    b = group()
                    sc = work[:, m % 2]
                    if br_name == "x":
                        dve.tensor_copy(sc, ps[:, b, :]).then_inc(misc_taken, 1)
                        bounds = ((0, MEM), (MEM, 2 * MEM))
                    else:
                        bh = bias4[:, h % 4]
                        dve.wait_ge(bias_landed[h % 4], 16 * (h // 4 + 1))
                        link(dve.memset(bh[0:CHUNK, T - CHUNK:T], MASKED))
                        link(dve.tensor_tensor(sc[:, 0:P], ps[:, b, 0:P], bh[:, P:T], ALU.add))
                        dve.tensor_tensor(sc[:, P:3 * P], ps[:, b, P:3 * P], bh, ALU.add).then_inc(misc_taken, 1)
                        bounds = ((0, P), (P, 3 * P))
                    dve.wait_ge(misc_taken, misc[0])
                    for t, (lo, hi) in enumerate(bounds):
                        chain[0] += 1
                        dve.tensor_reduce(mx[:, t:t + 1], sc[:, lo:hi], AX, ALU.max).then_inc(sem("vector_chain"), 1)
                    dve.wait_ge(sem("vector_chain"), chain[0])
                    if m >= 2:
                        dve.wait_ge(sem("exp_out"), 2 * m - 2)
                    dve.tensor_scalar(nmx[:, m % 2], mx, -1.0, None, ALU.mult).then_inc(sem("maxima"), 1)
                elif kind == "soften":
                    m, br_name, h = step[1:]
                    dve.wait_ge(sem("exp_out"), 2 * m + 2)
                    sc = work[:, m % 2]
                    link(dve.reciprocal(rc, sums[:, m % 2]))
                    bounds = ((0, MEM), (MEM, 2 * MEM)) if br_name == "x" else ((0, P), (P, 3 * P))
                    for t, (lo, hi) in enumerate(bounds):
                        dve.tensor_scalar(sc[:, lo:hi], sc[:, lo:hi], rc[:, t:t + 1], None, ALU.mult)\
                            .then_inc(sem("probs"), 1)
                elif kind == "probsT":
                    m, br_name, h = step[1:]
                    b = group()
                    w = 512 if br_name == "x" else 384
                    dve.tensor_copy(work[:, 2 + m % 2, 0:w], ps[:, b, 0:w]).then_inc(misc_taken, 1)
                elif kind == "values":
                    m, br_name, h = step[1:]
                    b = group()
                    if br_name == "x":
                        src = ps[:, b, :].rearrange("p (c t) -> p c t", c=2)
                        hi, lo = ycT[0][:, 2 * h:2 * h + 2], ycT[1][:, 2 * h:2 * h + 2]
                    else:
                        rows = slice(64 * (h % 2), 64 * (h % 2) + 64)
                        src, hi, lo = ps[rows, b, 0:T], yaT[0][rows, h // 2], yaT[1][rows, h // 2]
                    link(dve.tensor_copy(hi, src))
                    dve.tensor_tensor(lo, src, hi.bitcast(F32), ALU.subtract).then_inc(misc_taken, 1)
                elif kind == "conv":
                    j = step[1]
                    dve.wait_ge(gemm_taken, GEMM_AT[("xbc", j // 2, j % 2)] + 1)
                    if j >= 2:
                        dve.wait_ge(sem("silu_out"), j - 1)
                    for tap in range(TAPS):
                        for i in range(2):
                            c = 2 * j + i
                            acc, src = conv_acc[:, j % 2, i], craw[:, j % 2, i, tap:tap + T]
                            if tap == 0:
                                ins = dve.tensor_scalar(acc, src, cw_sb[:, c, 0:1], cb_sb[:, c:c + 1], ALU.mult, ALU.add)
                            else:
                                ins = dve.scalar_tensor_tensor(out=acc, in0=src, scalar=cw_sb[:, c, tap:tap + 1],
                                                               in1=acc, op0=ALU.mult, op1=ALU.add)
                            if tap == TAPS - 1 and i == 1:
                                ins.then_inc(sem("conv_done"), 1)
                            else:
                                chain[0] += 1
                                ins.then_inc(sem("vector_chain"), 1)
                        dve.wait_ge(sem("vector_chain"), chain[0])
                elif kind == "xsT":
                    j = step[1]
                    b = group()
                    for t in range(TT):
                        last = dve.tensor_copy(xs[t][:, j * 256:(j + 1) * 256], ps[:, b, t * 256:(t + 1) * 256])
                        if t == 0:
                            last.then_inc(sem("xs_first"), 1)
                    last.then_inc(misc_taken, 1)
                elif kind == "dt":
                    b = group()
                    v = dtw[:, 0].rearrange("p (t h) -> p t h", t=TT)
                    dve.tensor_tensor(v, ps[:, b, 0:64].rearrange("p (t h) -> p t h", t=TT),
                                      head_rows[:, 0].unsqueeze(1).to_broadcast([P, TT, SSM_HEADS]), ALU.add)\
                        .then_inc(misc_taken, 1)
                    dve.wait_ge(misc_taken, misc[0])
                    dve.scalar_tensor_tensor(out=dtw[:, 1], in0=dtw[:, 0], scalar=-1.0, in1=dtw[:, 0],
                                             op0=ALU.mult, op1=ALU.max).then_inc(sem("dt_abs"), 1)
                    dve.wait_ge(sem("dt_exp"), 1)
                    dve.tensor_scalar(dtw[:, 2], dtw[:, 1], 1.0, None, ALU.add).then_inc(sem("dt_one"), 1)
                    dve.wait_ge(sem("dt_one"), 1)
                    link(dve.tensor_scalar(dtw[:, 4], dtw[:, 2], -1.0, 1e-30, ALU.add, ALU.max))
                    dve.wait_ge(sem("dt_ln"), 1)
                    link(dve.tensor_tensor(dtw[:, 3], dtw[:, 3], dtw[:, 1], ALU.mult))
                    link(dve.reciprocal(dtw[:, 5], dtw[:, 4]))
                    link(dve.tensor_tensor(dtw[:, 3], dtw[:, 3], dtw[:, 5], ALU.mult))
                    link(dve.tensor_scalar(dtw[:, 5], dtw[:, 4], 1e-20, None, ALU.is_lt))
                    link(dve.tensor_tensor(dtw[:, 5], dtw[:, 5], dtw[:, 1], ALU.mult))
                    link(dve.tensor_tensor(dtw[:, 3], dtw[:, 3], dtw[:, 5], ALU.add))
                    link(dve.scalar_tensor_tensor(out=dtw[:, 4], in0=dtw[:, 0], scalar=0.0, in1=dtw[:, 3],
                                                  op0=ALU.max, op1=ALU.add))
                    dve.wait_ge(sem("a_exp"), 1)
                    dve.scalar_tensor_tensor(out=a_sb, in0=dt_sb, scalar=-1.0,
                                             in1=a_head[:].unsqueeze(1).to_broadcast([P, TT, SSM_HEADS]),
                                             op0=ALU.mult, op1=ALU.mult).then_inc(sem("a_ready"), 1)
                elif kind == "cb":
                    g = step[1]
                    b = group()
                    chain[0] += 2
                    dve.tensor_tensor(cbm[:, g % 2, 0:P], ps[:, b, 0:P], upto[:], ALU.mult)\
                        .then_inc(sem("vector_chain"), 1)
                    dve.tensor_tensor(cbm[:, g % 2, P:2 * P], ps[:, b, 2 * P:3 * P], upto[:], ALU.mult)\
                        .then_inc(sem("vector_chain"), 1)
                    dve.tensor_copy(cbm[:, g % 2, 2 * P:3 * P], ps[:, b, P:2 * P]).then_inc(misc_taken, 1)
                    dve.wait_ge(sem("vector_chain"), chain[0])
                elif kind == "weigh":
                    u, g, t = step[1:]
                    for d in range(2):
                        dve.wait_ge(exp_taken, 1 + 2 * u + d + 1)
                        v = work[:, d].rearrange("p (h l) -> p h l", h=4)
                        dve.tensor_tensor(v, v, cbm[:, g % 2, t * P:(t + 1) * P].unsqueeze(1).to_broadcast([P, 4, P]),
                                          ALU.mult).then_inc(sem("weighed"), 1)
                elif kind == "ssm":
                    u, g, t = step[1:]
                    y = xs[t][:, g * GW:(g + 1) * GW]
                    if u == 0:
                        dve.wait_ge(sem("xdt_ready"), 5)
                    if t == 1:
                        b = group()
                        dve.tensor_tensor(y_off.rearrange("p (h d) -> p h d", d=SSM_DIM),
                                          ps[:, b, :].rearrange("p (h d) -> p h d", d=SSM_DIM),
                                          decays[:, 1, 8 * g:8 * g + 8].unsqueeze(2).to_broadcast([P, 8, SSM_DIM]),
                                          ALU.mult).then_inc(misc_taken, 1)
                        dve.wait_ge(misc_taken, misc[0])
                    b = group()
                    dve.tensor_tensor(y, ps[:, b, :], y, ALU.add).then_inc(misc_taken, 1)
                    dve.wait_ge(misc_taken, misc[0])
                    if t == 1:
                        link(dve.tensor_tensor(y, y, y_off, ALU.add))
                    dve.wait_ge(gemm_taken, GEMM_AT[("z", g, t)] + 1)
                    dve.tensor_tensor(y, y, zbuf[:, g % 2, t], ALU.mult).then_inc(sem("gated"), 1)
                elif kind == "ynorm":
                    dve.wait_ge(sem("y_squares"), N_UNITS)
                    rstd(ss_y, ss_y, GW)
                    for t in range(TT):
                        v = xs[t].rearrange("p (g d) -> p g d", d=GW)
                        dve.tensor_tensor(v, v, ss_y[:, t * GROUPS:(t + 1) * GROUPS].unsqueeze(2)
                                          .to_broadcast([P, GROUPS, GW]), ALU.mult).then_inc(sem("y_normed"), 1)
                elif kind == "yT":
                    for c2 in range(2 * step[1], 2 * step[1] + 2):
                        b = group()
                        for j in range(2):
                            c = 2 * c2 + j
                            split_out(ybT, c, ps[:, b, j * T:(j + 1) * T], gssm_sb[:, c:c + 1], j == 1)
                        dve.wait_ge(sem("vector_chain"), chain[0])
                elif kind in ("merge", "take") and (kind == "merge" or step[1] == "wo"):
                    name, i = step[1:]
                    for h in range(2):
                        dve.wait_ge(gemm_taken, GEMM_AT[(name, i, h)] + 1)
                        cols = slice(i * NB, (i + 1) * NB)
                        src = tmp[:, br % 2]
                        if name == "wo":
                            dve.wait_ge(sem("x_again"), 16)
                            dve.tensor_tensor(x_sb[:, h, cols], x_sb[:, h, cols], src, ALU.add)\
                                .then_inc(sem("br_merged"), 1)
                        elif name == "bb":
                            dve.tensor_tensor(merged[:, h, cols], src, sig[:, h], ALU.mult)\
                                .then_inc(sem("br_merged"), 1)
                        else:
                            link(dve.tensor_tensor(src, src, sig[:, h], ALU.mult))
                            dve.tensor_tensor(merged[:, h, cols], merged[:, h, cols], src, ALU.add)\
                                .then_inc(sem("br_merged"), 1)
                        br += 1
                elif kind == "mergedT":
                    for c2 in range(2 * step[1], 2 * step[1] + 2):
                        b = group()
                        for j in range(2):
                            split_out(mergedT, 2 * c2 + j, ps[:, b, j * T:(j + 1) * T], None, j == 1)
                        dve.wait_ge(sem("vector_chain"), chain[0])

            dve.wait_ge(sem("out_squares"), TT)
            rstd(rs_2, ss_2, D)
            dve.wait_ge(sem("gain2_landed"), 16)
            for t in range(TT):
                dve.scalar_tensor_tensor(out=h2[:, t], in0=x_sb[:, t], scalar=rs_2[:, t:t + 1], in1=gain2,
                                         op0=ALU.mult, op1=ALU.mult).then_inc(sem("h2_ready"), 1)
            for c2 in range(4):
                b = group()
                dve.tensor_copy(h2T[:, 2 * c2:2 * c2 + 2], ps[:, b, :].rearrange("p (c t) -> p c t", c=2))\
                    .then_inc(misc_taken, 1)
            b = group()
            dve.tensor_tensor(logits, ps[:, b, 0:TT * EXPERTS].rearrange("p (t e) -> p t e", t=TT),
                              head_rows[:, 3].unsqueeze(1).to_broadcast([P, TT, EXPERTS]), ALU.add)\
                .then_inc(misc_taken, 1)
            dve.wait_ge(misc_taken, misc[0])
            for t in range(TT):
                link(dve.max(mx8[:, t], logits[:, t]))
                link(dve.max_index(idx8[:, t], mx8[:, t], logits[:, t]))
            link(dve.tensor_copy(idxf, idx8[:]))
            dve.tensor_tensor(e4, mx8[:, :, 0:TOP_K], mx8[:, :, 0:1].to_broadcast([P, TT, TOP_K]), ALU.subtract)\
                .then_inc(sem("top_shifted"), 1)
            dve.wait_ge(sem("top_exp"), 1)
            link(dve.tensor_reduce(s4, e4, AX, ALU.add))
            link(dve.reciprocal(s4, s4))
            link(dve.tensor_tensor(e4, e4, s4.unsqueeze(2).to_broadcast([P, TT, TOP_K]), ALU.mult))
            iota_e = iota_j[:, 0:EXPERTS]
            for t in range(TT):
                for k in range(TOP_K):
                    dst = wts if k == 0 else part
                    link(dve.tensor_scalar(dst[:, t], iota_e, idxf[:, t, k:k + 1], e4[:, t, k:k + 1],
                                           ALU.is_equal, ALU.mult))
                    if k:
                        link(dve.tensor_tensor(wts[:, t], wts[:, t], part[:, t], ALU.add))
            dve.tensor_scalar(chosen, wts, 0.0, None, ALU.is_gt).then_inc(sem("chosen_ready"), 1)
            dve.wait_ge(sem("tables_zero"), 1)
            b = group()
            dve.tensor_copy(wT[0:EXPERTS, :], ps[0:EXPERTS, b, 0:T]).then_inc(misc_taken, 1)
            b = group()
            link(dve.tensor_tensor(part, ps[:, b, 0:64].rearrange("p (t e) -> p t e", t=TT), chosen, ALU.mult))
            dve.tensor_reduce(cmax, ps[:, b, 64:64 + EXPERTS], AX, ALU.max).then_inc(misc_taken, 1)
            dve.wait_ge(misc_taken, misc[0])
            link(dve.tensor_scalar(over, steps_b[:], cmax, None, ALU.is_lt))
            link(dve.tensor_reduce(npass_f, over, AX, ALU.add))
            dve.tensor_copy(npass_i[:], npass_f[0:1, :]).then_inc(sem("passes_known"), 1)
            link(dve.memset(place4[:, :, PASSES * EXPERTS:NPAD], -1.0))
            for p in range(PASSES):
                cols = slice(p * EXPERTS, (p + 1) * EXPERTS)
                link(dve.tensor_scalar(place4[:, :, cols], part, -1.0 - BLK * p, None, ALU.add))
                link(dve.tensor_copy(weight4[:, :, cols], wts))
                link(dve.tensor_copy(picks[:, cols], ident[:, 0:EXPERTS]))
            dve.wait_ge(sem("bias_rows_zero"), 2)

            def find(i):
                for t in range(TT):
                    dve.tensor_scalar(hot[:, t], iota_j[:], place4[:, t, bass.ds(i, 1)], None, ALU.is_equal)\
                        .then_inc(sem("hot_ready"), 1)

            find(0)
            dve.wait_ge(sem("passes_known"), 1)
            n_pass = dve.value_load(npass_i[0:1, 0:1], min_val=1, max_val=PASSES)
            with dve.Fori(0, n_pass) as b_:
                with dve.Fori(0, EXPERTS) as e:
                    i = b_ * EXPERTS + e
                    dve.wait_ge(e_used[1], i)
                    dve.wait_ge(sem("hot_wT_ready"), i)
                    dve.tensor_copy(pick, picks[:, bass.ds(i, 1)].to_broadcast([P, BLK])).then_inc(sem("pick_ready"), 1)
                    for t in range(TT):
                        dve.tensor_scalar(hot_w[:, t], iota2[:], place4[:, t, bass.ds(i, 1)],
                                          weight4[:, t, bass.ds(i, 1)], ALU.is_equal, ALU.mult)\
                            .then_inc(sem("hot_w_ready"), 1)
                    dve.wait_ge(sem("gather_ready"), i + 1)
                    find(i + 1)
                    dve.wait_ge(e_used[1], i + 1)
                    dve.tensor_scalar(g_sb, ps[:, G_BANK, :], LIMIT, None, ALU.min).then_inc(sem("g_ready"), 1)
                    dve.tensor_scalar(u_sb, ps[:, U_BANK, :], LIMIT, -LIMIT, ALU.min, ALU.max)\
                        .then_inc(sem("u_ready"), 1)
                    dve.wait_ge(sem("u_ready"), i + 1)
                    dve.wait_ge(sem("g_ready"), i + 1)
                    dve.scalar_tensor_tensor(out=gu_sb, in0=u_sb, scalar=1.0, in1=g_sb, op0=ALU.add, op1=ALU.mult)\
                        .then_inc(sem("gu_ready"), 1)
                    dve.wait_ge(sem("gu_ready"), i + 1)
                    dve.wait_ge(sem("sg_ready"), i + 1)
                    dve.wait_ge(sem("actT_out"), i)
                    dve.tensor_tensor(act_sb, gu_sb, sg_sb, ALU.mult).then_inc(sem("act_ready"), 1)
                    dve.wait_ge(e_used[3], i + 1)
                    dve.wait_ge(sem("scattered"), i)
                    dve.tensor_copy(yb, ps[:, D_BANK, :]).then_inc(sem("yb_ready"), 1)
            dve.wait_ge(sem("experts_done"), 1)
            for t in range(TT):
                for h in range(2):
                    cols = slice(h * NB, (h + 1) * NB)
                    dve.tensor_tensor(y_out[:, t, cols], ps[:, ACC[2 * t + h], :], x_sb[:, t, cols], ALU.add)\
                        .then_inc(sem("y_ready"), 1)

        @block.tensor
        def _(pe):
            misc = [0]

            def group():
                n = misc[0]
                misc[0] += 1
                if n >= 3:
                    pe.wait_ge(misc_taken, n - 2)
                return MISC_BANKS[n % 3]

            def exp_bank(n):
                if n >= 1:
                    pe.wait_ge(exp_taken, n)
                return EXP_BANK

            def turn(dst, src):
                return pe.transpose(dst, src, ident[:])

            def by_columns(src, c2, width=P):
                b = group()
                for j in range(2):
                    for t in range(TT):
                        last = turn(ps[:, b, j * T + t * P:j * T + (t + 1) * P],
                                    src(t)[:, (2 * c2 + j) * P:(2 * c2 + j + 1) * P])
                last.then_inc(misc_ready, 1)

            def three_passes(out, lhs, rhs, start, stop):
                pe.matmul(out, lhs[0], rhs[0], start=start, stop=False, skip_group_check=True)
                pe.matmul(out, lhs[1], rhs[0], start=False, stop=False, skip_group_check=True)
                return pe.matmul(out, lhs[0], rhs[1], start=False, stop=stop, skip_group_check=True)

            pe.wait_ge(sem("masks"), 3)
            n = 0
            for step in SCHED:
                kind = step[0]
                if kind in ("memT", "hT"):
                    pe.wait_ge(sem("mem_scaled" if kind == "memT" else "rows_scaled"), 2)
                    src = mem_sb if kind == "memT" else xn
                    for c2 in range(4):
                        by_columns(lambda t: src[:, t], c2)
                elif kind == "gemm":
                    name, i, q, w = step[1:]
                    raw, hi, lo = quarter(w)
                    pe.wait_ge(lo_ready_pool if q == QUARTERS - 1 else lo_ready, w // QUARTERS + 1
                               if q == QUARTERS - 1 else w + 1 - pool_rests(w))
                    opens = q == 0 and not (name == "bb" and i % 2)
                    closes = q == QUARTERS - 1 and not (name == "bb" and i % 2 == 0)
                    lhs = {"mk": memT, "mv": memT, "bc": ycT, "ba": yaT, "bb": ybT, "wo": mergedT}.get(name, hT)
                    needs = {("mk", 0, 0): ("memT",), ("xbc", 0, 0): ("hT",), ("bb", 0, 0): ("yT", 3),
                             ("bc", 0, 0): ("values", 19, "x", 3), ("ba", 0, 0): ("values", 15, "a", 15),
                             ("wo", 0, 0): ("mergedT", 0), ("wo", 0, 2): ("mergedT", 1)}.get((name, i, q))
                    if needs:
                        pe.wait_ge(misc_taken, MISC_AT[needs] + MISC_GROUPS[needs[0]])
                    if opens and n >= 4:
                        pe.wait_ge(gemm_taken, n - 2)
                    for h in range(2):
                        b = GEMM_BANKS[(n + h) % 4]
                        for c in range(2):
                            k = 2 * q + c
                            if name == "xbc":
                                for j in range(2):
                                    cols = slice((2 * h + j) * P, (2 * h + j + 1) * P)
                                    last = three_passes(ps[:, b, j * T:(j + 1) * T], (hi[:, c, cols], lo[:, c, cols]),
                                                        (hT[0][:, k], hT[1][:, k]), opens and c == 0 and j == 0,
                                                        closes and c == 1)
                            else:
                                kk = k + KC * (i % 2) if name == "bb" else k
                                tok = slice(h * P, (h + 1) * P)
                                last = three_passes(ps[:, b, :], (lhs[0][:, kk, tok], lhs[1][:, kk, tok]),
                                                    (hi[:, c], lo[:, c]), opens and c == 0, closes and c == 1)
                    last.then_inc(unit_used, 1)
                    if closes:
                        n += 2
                elif kind == "headT":
                    name = step[1]
                    raw, order = {"q": (q_raw, 1), "k": (k_raw, 2), "qx": (qx_raw, 3), "kx": (kx_raw, 4)}[name]
                    pe.wait_ge(sem("head_normed"), order)
                    for c2 in range(4):
                        by_columns(lambda t: raw[:, t], c2)
                elif kind == "scores":
                    m, br, h = step[1:]
                    b = group()
                    if h == 0:
                        pe.wait_ge(misc_taken, MISC_AT[("headT", "kx" if br == "x" else "k")] + 4)
                        pe.wait_ge(misc_taken, MISC_AT[("headT", "qx" if br == "x" else "q")] + 4)
                    for t in range(TT):
                        if br == "x":
                            for j in range(2):
                                last = pe.matmul(ps[:, b, t * MEM:(t + 1) * MEM], qxT[:, 2 * h + j, t * P:(t + 1) * P],
                                                 kxT[:, 2 * h + j], start=(j == 0), stop=(j == 1))
                        else:
                            last = pe.matmul(ps[:, b, t * P:t * P + (t + 1) * P], qz[:, h, t * P:(t + 1) * P],
                                             kT[:, h // 2, 0:(t + 1) * P], start=True, stop=True)
                    last.then_inc(misc_ready, 1)
                elif kind == "probsT":
                    m, br, h = step[1:]
                    b = group()
                    pe.wait_ge(sem("probs"), 2 * m + 2)
                    pr = work[:, m % 2]
                    if br == "x":
                        for k in range(2):
                            for t in range(TT):
                                last = turn(ps[:, b, k * T + t * P:k * T + (t + 1) * P],
                                            pr[:, t * MEM + k * P:t * MEM + (k + 1) * P])
                    else:
                        for j in range(3):
                            last = turn(ps[:, b, j * P:(j + 1) * P], pr[:, j * P:(j + 1) * P])
                    last.then_inc(misc_ready, 1)
                elif kind == "values":
                    m, br, h = step[1:]
                    b = group()
                    pe.wait_ge(misc_taken, MISC_AT[("probsT", m, br, h)] + 1)
                    pT = work[:, 2 + m % 2]
                    if br == "x":
                        pe.wait_ge(gemm_taken, GEMM_AT[("mv", 1, 1)] + 1)
                        for c in range(2):
                            for k in range(2):
                                last = pe.matmul(ps[:, b, c * T:(c + 1) * T],
                                                 vx[:, k, h * X_DIM + c * P:h * X_DIM + (c + 1) * P],
                                                 pT[:, k * T:(k + 1) * T], start=(k == 0), stop=(k == 1))
                    else:
                        pe.wait_ge(gemm_taken, GEMM_AT[("v", 1, 1)] + 1)
                        rows = slice(64 * (h % 2), 64 * (h % 2) + 64)
                        hc = slice(h * A_DIM, (h + 1) * A_DIM)
                        pe.matmul(ps[rows, b, 0:T], v_sb[:, 0, hc], pT[:, 0:T], start=True, stop=False)
                        last = pe.matmul(ps[rows, b, P:T], v_sb[:, 1, hc], pT[:, T:T + P], start=False, stop=True)
                    last.then_inc(misc_ready, 1)
                elif kind == "xsT":
                    j = step[1]
                    b = group()
                    pe.wait_ge(sem("silu_out"), j + 1)
                    for t in range(TT):
                        for c in range(2):
                            last = turn(ps[:, b, (2 * t + c) * P:(2 * t + c + 1) * P],
                                        conv_out[:, j % 2, c, t * P:(t + 1) * P])
                    last.then_inc(misc_ready, 1)
                elif kind == "dt":
                    b = group()
                    pe.wait_ge(sem("wdt_ready"), 1)
                    for t in range(TT):
                        for c in range(KC):
                            tok = slice(t * P, (t + 1) * P)
                            last = three_passes(ps[:, b, t * SSM_HEADS:(t + 1) * SSM_HEADS],
                                                (hT[0][:, c, tok], hT[1][:, c, tok]), (wdt_r[:, 0, c], wdt_r[:, 1, c]),
                                                c == 0, c == KC - 1)
                    last.then_inc(misc_ready, 1)
                elif kind == "decay":
                    b = exp_bank(0)
                    pe.wait_ge(sem("a_ready"), 1)
                    pe.matmul(ps[:, b, 0:SSM_HEADS], after[:], a_sb[:, 0], start=True, stop=True)
                    pe.matmul(ps[:, b, SSM_HEADS:2 * SSM_HEADS], upto[:], a_sb[:, 1], start=True, stop=True)\
                        .then_inc(exp_ready, 1)
                elif kind == "cb":
                    g = step[1]
                    b = group()
                    pe.wait_ge(sem("silu_out"), CONV_T // 2)
                    pe.matmul(ps[:, b, 0:T], bcT[:, g, 0:P], bcT[:, GROUPS + g], start=True, stop=True)
                    pe.matmul(ps[:, b, T:T + P], bcT[:, g, P:T], bcT[:, GROUPS + g, P:T], start=True, stop=True)\
                        .then_inc(misc_ready, 1)
                elif kind == "spread":
                    u, g, t, d = step[1:]
                    n_exp = 1 + 2 * u + d
                    b = exp_bank(n_exp)
                    pe.wait_ge(sem("steps_ready"), n_exp)
                    pe.matmul(ps[:, b, :], after[:], work[:, 2 + d], start=True, stop=True).then_inc(exp_ready, 1)
                elif kind == "ssm":
                    u, g, t = step[1:]
                    if t == 1:
                        b = group()
                        pe.matmul(ps[:, b, :], cbm[:, g % 2, 2 * P:3 * P], fx[:, g * GW:(g + 1) * GW],
                                  start=True, stop=True).then_inc(misc_ready, 1)
                    b = group()
                    pe.wait_ge(sem("weighed"), 2 * u + 2)
                    pe.wait_ge(sem("xdt_ready"), 5)
                    for r in range(8):
                        hc = slice(g * GW + r * SSM_DIM, g * GW + (r + 1) * SSM_DIM)
                        last = pe.matmul(ps[:, b, r * SSM_DIM:(r + 1) * SSM_DIM],
                                         work[:, r // 4, (r % 4) * P:(r % 4 + 1) * P], xdt[t][:, hc],
                                         start=True, stop=True)
                    last.then_inc(misc_ready, 1)
                elif kind == "yT":
                    pe.wait_ge(sem("y_normed"), TT)
                    for c2 in range(2 * step[1], 2 * step[1] + 2):
                        by_columns(lambda t: xs[t], c2)
                elif kind == "mergedT":
                    pe.wait_ge(sem("br_merged"), 10 + 2 * step[1])
                    for c2 in range(2 * step[1], 2 * step[1] + 2):
                        by_columns(lambda t: merged[:, t], c2)

            pe.wait_ge(sem("h2_ready"), TT)
            for c2 in range(4):
                by_columns(lambda t: h2[:, t], c2)
            b = group()
            pe.wait_ge(misc_taken, MISC_AT["logits"])
            for t in range(TT):
                for c in range(KC):
                    last = pe.matmul(ps[:, b, t * EXPERTS:(t + 1) * EXPERTS], h2T[:, c, t * P:(t + 1) * P], wr_sb[:, c],
                                     start=(c == 0), stop=(c == KC - 1))
            last.then_inc(misc_ready, 1)
            pe.wait_ge(sem("chosen_ready"), 1)
            b = group()
            for t in range(TT):
                last = turn(ps[0:EXPERTS, b, t * P:(t + 1) * P], wts[:, t])
            last.then_inc(misc_ready, 1)
            b = group()
            pe.matmul(ps[:, b, 0:EXPERTS], upto[:], chosen[:, 0], start=True, stop=True)
            pe.matmul(ps[:, b, EXPERTS:2 * EXPERTS], upto[:], chosen[:, 1], start=True, stop=False)
            pe.matmul(ps[:, b, EXPERTS:2 * EXPERTS], ones[:], chosen[:, 0], start=False, stop=True)
            for t in range(TT):
                last = pe.matmul(ps[:, b, 64:64 + EXPERTS], ones[:], chosen[:, t], start=(t == 0), stop=(t == 1))
            last.then_inc(misc_ready, 1)
            pe.wait_ge(misc_taken, MISC_END)
            pe.wait_ge(gemm_taken, GEMM_END)
            pe.wait_ge(sem("bias_rows_landed"), 48)
            pe.wait_ge(exp_taken, 1 + 2 * N_UNITS)
            for t in range(TT):
                for h in range(2):
                    pe.matmul(ps[:, ACC[2 * t + h], :], wT[:, t * P:(t + 1) * P], bias_d[:, h * NB:(h + 1) * NB],
                              start=True, stop=False, skip_group_check=True)

            def gather():
                for c in range(KC):
                    for t in range(TT):
                        last = pe.matmul(ps[:, X_BANK, c * BLK:(c + 1) * BLK], h2[:, t, c * P:(c + 1) * P], hot[:, t],
                                         start=(t == 0), stop=(t == TT - 1))
                last.then_inc(sem("gather_ready"), 1)

            pe.wait_ge(sem("hot_ready"), TT)
            gather()
            pe.wait_ge(sem("passes_known"), 1)
            n_pass = pe.value_load(npass_i[0:1, 0:1], min_val=1, max_val=PASSES)
            with pe.Fori(0, n_pass) as b_:
                with pe.Fori(0, EXPERTS) as e:
                    i = b_ * EXPERTS + e
                    pe.wait_ge(sem("pick_ready"), i + 1)
                    pe.wait_ge(sem("xg_ready"), i + 1)
                    pe.wait_ge(sem("actT_ready"), i)
                    for bank, c0 in ((G_BANK, 0), (U_BANK, D)):
                        for h in range(2):
                            pe.matmul(ps[64 * h:64 * h + 64, bank, :], pick, bias_gu[:, c0 + h * NB:c0 + (h + 1) * NB],
                                      start=True, stop=False, skip_group_check=True)
                    for k in range(2):
                        for bank, w, sl in ((G_BANK, gate_w, 2 * k), (U_BANK, up_w, 2 * k + 1)):
                            pe.wait_ge(e_landed[sl], i * 16 + 16)
                            for c in range(KC // 2):
                                for h in range(2):
                                    last = pe.matmul(ps[64 * h:64 * h + 64, bank, :], xgT[:, k * 4 + c],
                                                     w[k][:, c, h * NB:(h + 1) * NB], start=False,
                                                     stop=(k == 1 and c == 3), skip_group_check=True)
                        last.then_inc(e_used[k], 1)
                    pe.wait_ge(sem("hot_w_ready"), i * TT + TT)
                    pe.wait_ge(sem("yb_ready"), i)
                    for t in range(TT):
                        last = turn(ps[:, D_BANK, t * P:(t + 1) * P], hot_w[:, t].rearrange("p r j -> p (r j)"))
                    last.then_inc(sem("hot_wT_ready"), 1)
                    pe.wait_ge(sem("hot_ready"), i * TT + 2 * TT)
                    gather()
                    pe.wait_ge(sem("act_ready"), i + 1)
                    for c in range(4):
                        last = turn(ps[:, G_BANK, c * P:(c + 1) * P], act_sb[:, c * P:(c + 1) * P])
                    last.then_inc(sem("actT_out"), 1)
                    pe.wait_ge(sem("actT_ready"), i + 1)
                    pe.wait_ge(sem("scatter_ready"), i * 2 + 2)
                    for k in range(2):
                        pe.wait_ge(e_landed[4 + k], i * 16 + 16)
                        for c in range(4):
                            for h in range(2):
                                last = pe.matmul(ps[64 * h:64 * h + 64, D_BANK, :], actT[:, c, 64 * k:64 * k + 64],
                                                 down_w[k][:, c, h * NB:(h + 1) * NB], start=(k == 0 and c == 0),
                                                 stop=(k == 1 and c == 3))
                        last.then_inc(e_used[2 + k], 1)
                    pe.wait_ge(sem("yb_ready"), i + 1)
                    for t in range(TT):
                        for h in range(2):
                            last = pe.matmul(ps[:, ACC[2 * t + h], :], hot_wT[:, h, t], yb, start=False, stop=False,
                                             skip_group_check=True)
                    last.then_inc(sem("scattered"), 1)
            pe.matmul(ps[:, D_BANK, 0:EXPERTS], ident[:], chosen[:, 0], start=True, stop=True)\
                .then_inc(sem("experts_done"), 1)


def kernel(**inputs):
    import numpy as np
    import concourse.bacc as bacc
    from concourse.bass_utils import run_bass_kernel_spmd

    src = {k: np.asarray(v) for k, v in inputs.items()}
    one = {k: v[0] for k, v in src.items() if k not in ("x", "mem")}

    def columns(v):
        return np.ascontiguousarray(v.reshape(-1, P).T)

    args = {
        "x": src["x"], "mem": src["mem"], "g_mix": columns(one["norm_mix"]), "w_in": one["w_in"],
        "w_dt": np.ascontiguousarray(one["w_in"][:, DT0:DT0 + SSM_HEADS]),
        "a_gains": np.stack([np.concatenate([one["a_q_gain"]] * 2), np.concatenate([one["a_k_gain"]] * 2)], 1),
        "rel_rev": np.ascontiguousarray(one["a_rel_bias"][:, ::-1]),
        "conv_w": np.ascontiguousarray(one["conv_w"].reshape(TAPS, CONV_T, P).transpose(2, 1, 0)),
        "conv_b": columns(one["conv_b"]), "dt_bias": one["dt_bias"], "a_log": one["a_log"], "d_skip": one["d_skip"],
        "g_ssm": columns(one["ssm_norm"]), "g_mem": columns(one["norm_mem"]), "w_mem_kv": one["w_mem_kv"],
        "x_gains": np.concatenate([columns(one["x_q_gain"]), columns(one["x_k_gain"])], 1),
        "w_br_a": one["w_br_a"], "w_br_b": one["w_br_b"], "w_br_c": one["w_br_c"], "w_out": one["w_out"],
        "norm_ffn": one["norm_ffn"], "w_router": one["w_router"], "b_router": one["b_router"],
        "w_gate": one["w_gate"], "b_gate": one["b_gate"], "w_up": one["w_up"], "b_up": one["b_up"],
        "w_down": one["w_down"], "b_down": one["b_down"],
    }
    nc = bacc.Bacc("TRN2", target_bir_lowering=False, num_devices=1)
    arrays, aps = {}, []
    for name, a in args.items():
        a = np.ascontiguousarray(a)
        arrays["in_" + name] = a
        aps.append(nc.dram_tensor("in_" + name, a.shape, mybir.dt.from_np(a.dtype), kind="ExternalInput").ap())
    aps.append(nc.dram_tensor("bias_rows", (A_HEADS, P * (SKEW + 1)), F32).ap())
    aps.append(nc.dram_tensor("out_0", (1, T, D), F32, kind="ExternalOutput").ap())
    hybrid_block_kernel(nc, *aps)
    r = run_bass_kernel_spmd(nc, [arrays], core_ids=[0])
    return r.results[0]["out_0"]
```

```python
from contextlib import ExitStack

import concourse.bass as bass
from concourse import mybir

P = 128
F32 = mybir.dt.float32
F32R = mybir.dt.float32r
I32 = mybir.dt.int32
U32 = mybir.dt.uint32
ALU = mybir.AluOpType
ACT = mybir.ActivationFunctionType
AX = mybir.AxisListType.X

EPS = 1e-6
D = 1024
T = 256
TT = T // P
KC = D // P
NB = 512
A_HEADS, A_DIM = 16, 64
X_HEADS, X_DIM = 4, 256
MEM = 256
CHUNK = 64
REL_CLIP = 128
INNER = 2048
GROUPS, STATE, SSM_HEADS, SSM_DIM = 4, 128, 32, 64
GW = INNER // GROUPS
CONV_CH = INNER + 2 * GROUPS * STATE
CONV_T = CONV_CH // P
TAPS = 4
EXPERTS, TOP_K = 32, 4
BLK = 64
PASSES = T // BLK
LIMIT, ALPHA = 7.0, 1.702
MASKED = -1e30
SKEW = 384

Q0, K0, V0, Z0 = 0, D, 2 * D, 3 * D
XBC0 = Z0 + INNER
DT0 = XBC0 + CONV_CH
QX0 = DT0 + SSM_HEADS
GATE0 = QX0 + D

BLOCKS = ([("xbc", i) for i in range(6)] + [("z", i) for i in range(4)] + [("q", i) for i in range(2)]
          + [("k", i) for i in range(2)] + [("v", i) for i in range(2)]
          + [("gb", 0), ("bb", 0), ("bb", 1), ("gb", 1), ("bb", 2), ("bb", 3)]
          + [("qx", i) for i in range(2)] + [("mk", i) for i in range(2)] + [("mv", i) for i in range(2)]
          + [("ga", 0), ("ba", 0), ("ga", 1), ("ba", 1), ("gc", 0), ("bc", 0), ("gc", 1), ("bc", 1)]
          + [("wo", i) for i in range(2)])
BLOCK_AT = {b: n for n, b in enumerate(BLOCKS)}
QUARTERS = 4
UNITS = QUARTERS * len(BLOCKS)
HALVES = 3
SPLITS = 4
GATES = ("gb", "ga", "gc")


def block_groups():
    out = []
    for name, i in BLOCKS:
        if name == "bb":
            if i % 2 == 1:
                out += [(name, i // 2, h) for h in range(2)]
        else:
            out += [(name, i, h) for h in range(2)]
    return out


GEMM = block_groups()
GEMM_AT = {g: n for n, g in enumerate(GEMM)}
HEADS = [("a", h) for h in range(A_HEADS)] + [("x", h) for h in range(X_HEADS)]


def first(name, i=0):
    return QUARTERS * BLOCK_AT[(name, i)]


def block_end(name, i):
    return first(name, 2 * i + 1 if name == "bb" else i) + QUARTERS


def schedule():
    extra = [[] for _ in range(UNITS + 2)]

    def at(w, *step):
        extra[w].append(step)

    for n, (name, i) in enumerate(BLOCKS):
        if name == "bb":
            if i % 2 == 0:
                continue
            i = i // 2
        at(4 * n + 4, "take", name, i)
        if name in ("bb", "ba", "bc"):
            at(4 * n + (4 if (name, i) == ("bc", 1) else 5), "merge", name, i)
    for i in range(6):
        w = first("xbc", i)
        at(w + 5, "conv", 2 * i)
        at(w + 6, "silu", 2 * i)
        at(w + 6, "conv", 2 * i + 1)
        at(w + 7, "silu", 2 * i + 1)
        if i < INNER // P // 4:
            at(w + 7, "xsT", 2 * i)
            at(w + 8, "xsT", 2 * i + 1)
    at(first("xbc", 1) + 3, "dt")
    at(first("xbc", 2) + 1, "decay")
    for part in range(5):
        at(first("xbc", 3) + 2 + part, "xdt", 0, part)
        at(first("xbc", 5) + 1 + part, "xdt", 1, part)
    k0 = first("z", 1) + 2
    for k in range(2 * GROUPS * TT + 1):
        u, d = k // 2, k % 2
        if k >= 2 and d == 0:
            at(k0 + k, "ssm", u - 1, (u - 1) // TT, (u - 1) % TT)
        if u < GROUPS * TT:
            if k % 4 == 0:
                at(k0 + k, "cb", u // TT)
            at(k0 + k, "spread", u, u // TT, u % TT, d)
            if d == 1:
                at(k0 + k, "weigh", u, u // TT, u % TT)
    at(first("q", 1) + 3, "ynorm")
    for p in range(4):
        at(first("k", 0) + 2 + p, "yT", p)
    at(first("k", 1) + 2, "clear")
    at(first("k", 0) + 1, "square", "q")
    at(first("k", 1), "headnorm", "q")
    at(first("v", 0), "headT", "q")
    at(first("v", 0) + 1, "square", "k")
    at(first("v", 0) + 3, "headnorm", "k")
    at(first("v", 1) + 2, "headT", "k")

    def attend(w0, lo, hi):
        for slot in range(hi - lo + 2):
            for stage, m in (("scores", lo + slot), ("probsT", lo + slot - 1), ("values", lo + slot - 2),
                             ("soften", lo + slot)):
                if lo <= m < hi:
                    at(w0 + 2 * slot, stage, m, *HEADS[m])

    attend(first("v", 1) + 4, 0, A_HEADS)
    at(first("v", 0) + 2, "memsquare")
    at(first("gb", 0) + 1, "memnorm")
    for c2 in range(4):
        at(first("qx", 0) + 3 + c2, "memT", c2)
    at(first("mk", 0) + 1, "square", "qx")
    at(first("mk", 0) + 3, "headnorm", "qx")
    at(first("mk", 1) + 2, "headT", "qx")
    at(first("mv", 0) + 1, "square", "kx")
    at(first("mv", 0) + 3, "headnorm", "kx")
    at(first("mv", 1) + 1, "headT", "kx")
    attend(first("ga", 0), A_HEADS, A_HEADS + X_HEADS)
    at(first("bc", 1), "mergedT", 0)
    at(first("wo", 0) + 1, "mergedT", 1)
    for i in range(2):
        w = first("wo", i) + QUARTERS + (1 if i == 0 else 0)
        at(w, "outT", i)
        at(w + 1, "logits", i)
    s = [("hT",)] + [("split", w) for w in range(SPLITS - 1)]
    for w in range(UNITS):
        name, i = BLOCKS[w // QUARTERS]
        s.append(("gemm", name, i, w % QUARTERS, w))
        if w + SPLITS - 1 < UNITS:
            s.append(("split", w + SPLITS - 1))
        s += extra[w]
    return s + extra[UNITS] + extra[UNITS + 1]


SCHED = schedule()
MISC_GROUPS = {"memT": 1, "hT": 4, "headT": 4, "scores": 1, "probsT": 1, "values": 1, "xsT": 1, "dt": 1, "cb": 1,
               "yT": 2, "mergedT": 2, "outT": 2}


def misc_index():
    at, n = {}, 0
    for step in SCHED:
        at[step] = n
        n += MISC_GROUPS.get(step[0], 0)
        if step[0] == "ssm":
            n += 1 + step[3]
    at["places"], at["end"] = n, n + 1
    return at


MISC_AT = misc_index()
N_UNITS = GROUPS * TT


def values_end(m):
    return MISC_AT[("values", m) + HEADS[m]] + 1


def ssm_end(u):
    return MISC_AT[("ssm", u, u // TT, u % TT)] + 1 + u % TT


def hybrid_block_kernel(nc, x, mem, g_mix, w_in, w_dt, a_gains, rel_rev, conv_w, conv_b, dt_bias, a_log, d_skip,
                        g_ssm, g_mem, w_mem_kv, x_gains, w_br_a, w_br_b, w_br_c, w_out, norm_ffn, w_router,
                        b_router, w_gate, b_gate, w_up, b_up, w_down, b_down, bias_dram, out):
    with ExitStack() as ctx:
        def sb(name, shape, dt=F32):
            return ctx.enter_context(nc.sbuf_tensor(name, shape, dt))

        sems = {}

        def sem(name):
            if name not in sems:
                sems[name] = ctx.enter_context(nc.semaphore(name))
            return sems[name]

        REGION = 2048
        N_REGIONS = 14
        PART = 2 * NB
        ARENA = N_REGIONS * REGION + HALVES * REGION + SPLITS * 2 * PART
        base = (nc.sbuf_base + 31) // 32 * 32
        sb("arena", [P, ARENA + 8])

        def placed(name, shape, dt, offset):
            return nc.alloc_sbuf_tensor_at(name, shape, dt, offset=base + 4 * offset)

        S = placed("regions", [P, N_REGIONS + 7, REGION], F32, 0)
        SR = placed("regions_r", [P, N_REGIONS, REGION], F32R, 0)
        halves = placed("halves", [P, HALVES, 4, NB], F32, N_REGIONS * REGION)
        splits = placed("splits", [P, SPLITS, 2, 2, NB], F32R, (N_REGIONS + HALVES) * REGION)

        def by_token(i):
            return S[:, i].rearrange("p (t d) -> p t d", t=TT)

        def by_channel(i):
            return S[:, i].rearrange("p (c t) -> p c t", c=KC)

        def split_pair(hi, lo):
            return [SR[:, r].rearrange("p (c t) -> p c t", c=KC) for r in (hi, lo)]

        x_sb, xn = by_token(0), by_token(7)
        gain1 = S[:, 6, 0:D]
        hT = split_pair(1, 0)
        conv_acc = S[:, 5, 0:1024].rearrange("p (b j t) -> p b j t", b=2, j=2)
        conv_out = S[:, 5, 1024:2048].rearrange("p (b j t) -> p b j t", b=2, j=2)
        xs = [S[:, 2], S[:, 3]]
        bcT = by_channel(8)
        xdt = [S[:, 7], S[:, 10]]
        fx = S[:, 11]
        sq_junk, y_off = S[:, 12, 0:NB], S[:, 12, NB:2 * NB]
        zbuf = S[:, 13].rearrange("p (b t n) -> p b t n", b=2, t=TT)
        ybT = [SR[:, 12:14].rearrange("p a (c t) -> p (a c) t", t=T), SR[:, 10:12].rearrange("p a (c t) -> p (a c) t", t=T)]
        q_raw, k_raw, v_sb = by_token(4), by_token(9), by_token(6)
        squares = {"q": S[:, 5], "k": S[:, 5], "qx": S[:, 8], "kx": S[:, 8]}
        qz = S[:, 2:4].rearrange("p a (h t) -> p (a h) t", t=T)
        kT = by_channel(7)
        yaT = split_pair(4, 9)
        rel_sb = S[0:A_HEADS, 12, 0:512]
        mem_sb = by_token(8)
        memT = split_pair(10, 11)
        qx_raw, kx_raw, vx = by_token(12), by_token(13), by_token(2)
        kxT, qxT = by_channel(3), by_channel(6)
        ycT = split_pair(7, 12)
        merged = by_token(5)
        mergedT = split_pair(1, 6)
        h2, h2T = by_token(12), by_channel(5)
        gain2, bias_d = S[:, 4, 0:D], S[:, 4, D:2 * D]
        bias_gu = S[:, 1]

        eslots = [S[:, a:a + 2].rearrange("p a (c n) -> p (a c) n", n=D) for a in (10, 2, 8, 13, 15, 17, 19, 6)]

        bias4 = sb("bias4", [P, 4, T])
        sig = sb("sig", [P, TT, NB])
        wdt_r = sb("wdt_r", [P, 2, KC, SSM_HEADS], F32R)
        ident = sb("ident", [P, P])
        upto = sb("upto", [P, P])
        after = sb("after", [P, P])
        ones = S[:, 13, 0:P]
        iota_i = sb("iota_i", [P, BLK], I32)
        iota_j = sb("iota_j", [P, BLK])
        iota2 = sb("iota2", [P, 2, BLK])
        steps_b = sb("steps_b", [P, PASSES])
        gmem_sb = sb("gmem_sb", [P, KC])
        gssm_sb = sb("gssm_sb", [P, INNER // P])
        ag_sb = sb("ag_sb", [P, 2])
        xg_sb = sb("xg_sb", [P, 4])
        cw_sb = sb("cw_sb", [P, CONV_T, TAPS])
        cb_sb = sb("cb_sb", [P, CONV_T])
        head_rows = sb("head_rows", [P, 4, SSM_HEADS])
        wdt_sb = S[:, 9, 0:KC * SSM_HEADS].rearrange("p (c h) -> p c h", c=KC)
        wr_sb = sb("wr_sb", [P, KC, EXPERTS])
        craw = sb("craw", [P, 2, 2, T + TAPS])
        work = sb("work", [P, 4, NB])
        tmp = sb("tmp", [P, 2, NB])
        cbm = sb("cbm", [P, 2, 384])
        stat = sb("stat", [P, 256])
        ss_x, rs_x = stat[:, 0:2], stat[:, 4:6]
        ss_h = stat[:, 8:40]
        mx, rc = stat[:, 40:42], stat[:, 42:44]
        nmx = stat[:, 192:196].rearrange("p (b t) -> p b t", b=2)
        sums = stat[:, 196:200].rearrange("p (b t) -> p b t", b=2)
        ss_m, rs_m = stat[:, 200:202], stat[:, 202:204]
        ss_y = stat[:, 49:57]
        ss_2 = stat[:, 57:59]
        ss_part = stat[:, 204:208]
        rs_2 = stat[:, 59:61]
        rs_for_act = stat[:, 208:210]
        npass_f, cmax = stat[:, 61:62], stat[:, 62:63]
        over = stat[:, 64:68]
        mx8 = stat[:, 72:88].rearrange("p (t k) -> p t k", t=TT)
        idxf = stat[:, 88:104].rearrange("p (t k) -> p t k", t=TT)
        e4 = stat[:, 104:112].rearrange("p (t k) -> p t k", t=TT)
        s4 = stat[:, 112:114]
        root_in, root_out = stat[:, 128:160], stat[:, 160:192]
        idx8 = sb("idx8", [P, TT, 8], U32)
        npass_i = sb("npass_i", [1, 1], I32)
        upto_r = sb("upto_r", [P, P], F32R)
        ones_r = sb("ones_r", [P, P], F32R)
        chosen_r = sb("chosen_r", [P, TT, EXPERTS], F32R)
        dtw = sb("dtw", [P, 6, TT * SSM_HEADS])
        dt_sb = dtw[:, 4].rearrange("p (t h) -> p t h", t=TT)
        a_sb = dtw[:, 5].rearrange("p (t h) -> p t h", t=TT)
        a_head = sb("a_head", [P, SSM_HEADS])
        decays = sb("decays", [P, 2, SSM_HEADS])
        rt = sb("rt", [P, 3, TT * EXPERTS])
        logits = rt[:, 0].rearrange("p (t e) -> p t e", t=TT)
        wts = rt[:, 1].rearrange("p (t e) -> p t e", t=TT)
        part = rt[:, 2].rearrange("p (t e) -> p t e", t=TT)
        chosen = chosen_r[:].bitcast(F32)

        g_sb, u_sb, sg_sb, gu_sb = (work[:, k] for k in range(4))
        act_sb, actT = tmp[:, 0], tmp[:, 1].rearrange("p (c j) -> p c j", c=4)
        yb, xgT = sig[:, 0], sig[:, 1].rearrange("p (c j) -> p c j", c=KC)
        spare = craw[:].rearrange("p a b t -> p (a b t)")
        pick = spare[:, 0:BLK]
        hot = spare[:, 64:64 + TT * BLK].rearrange("p (t j) -> p t j", t=TT)
        hot_w = spare[:, 192:192 + TT * 2 * BLK].rearrange("p (t r j) -> p t r j", t=TT, r=2)
        hot_wT = spare[:, 448:448 + 512].rearrange("p (h t j) -> p h t j", h=2, t=TT)
        tables = cbm[:].rearrange("p a n -> p (a n)")
        NPAD = PASSES * EXPERTS + 1
        place4 = tables[:, 0:TT * NPAD].rearrange("p (t i) -> p t i", t=TT)
        weight4 = tables[:, 260:260 + TT * PASSES * EXPERTS].rearrange("p (t i) -> p t i", t=TT)
        picks = tables[:, 520:520 + PASSES * EXPERTS]
        matches = work[:, 2, 0:TT * TOP_K * EXPERTS].rearrange("p (t k e) -> p t k e", t=TT, k=TOP_K)
        matched = work[:, 3, 0:TT * TOP_K * EXPERTS].rearrange("p (t k e) -> p t k e", t=TT, k=TOP_K)

        ps = ctx.enter_context(nc.psum_tensor("ps", [P, 8, NB], F32))
        GEMM_BANKS, EXP_BANK, MISC_BANKS = (0, 1, 2, 3), 7, (4, 5, 6)
        ACC, G_BANK, U_BANK, X_BANK, D_BANK = (0, 1, 2, 3), 4, 5, 6, 7

        gemm_taken = sem("gemm_taken")
        misc_ready, misc_taken = sem("misc_ready"), sem("misc_taken")
        exp_ready, exp_taken = sem("exp_ready"), sem("exp_taken")
        landed = [sem(f"half_landed{k}") for k in range(HALVES)]
        bias_landed = [sem(f"bias_landed{k}") for k in range(4)]
        hi_ready, lo_ready, lo_ready_pool = sem("rounded"), sem("rest_by_vector"), sem("rest_by_pool")
        unit_used = sem("quarter_used")
        SLOTS, LOADS = 8, 6
        ROUND = 4
        TURNS = ROUND * LOADS // SLOTS
        e_landed = [sem(f"expert_landed{k}") for k in range(SLOTS)]
        e_used = [sem(f"expert_used{k}") for k in range(SLOTS)]

        def place(r, k):
            return (r * LOADS + k) % SLOTS, (r * LOADS + k) // SLOTS

        MISC_END = MISC_AT["end"]
        GEMM_END = len(GEMM)

        def pool_rests(n):
            return n // QUARTERS

        def quarter(w):
            m = w // 2
            return halves[:, m % HALVES, 2 * (w % 2):2 * (w % 2) + 2], splits[:, w % SPLITS, 0], splits[:, w % SPLITS, 1]

        def weight_src(name, i):
            def rows(w, c0):
                return w.rearrange("(c p) n -> p c n", p=P)[:, :, c0:c0 + NB]
            if name in ("mk", "mv"):
                return rows(w_mem_kv, (0 if name == "mk" else D) + i * NB)
            if name in ("bc", "ba", "wo"):
                return rows({"bc": w_br_c, "ba": w_br_a, "wo": w_out}[name], i * NB)
            if name == "bb":
                return w_br_b[(i % 2) * D:(i % 2 + 1) * D].rearrange("(c p) n -> p c n", p=P)[
                    :, :, (i // 2) * NB:(i // 2 + 1) * NB]
            c0 = {"q": Q0, "k": K0, "v": V0, "z": Z0, "xbc": XBC0, "qx": QX0,
                  "ga": GATE0, "gb": GATE0 + D, "gc": GATE0 + 2 * D}[name]
            return rows(w_in, c0 + i * NB)

        def expert_src(k, e):
            w = (w_gate, w_up, w_gate, w_up, w_down, w_down)[k]
            half = (0, 0, 1, 1, 0, 1)[k]
            return w[e].rearrange("(h c p) n -> h p c n", h=2, p=P)[half]

        block = ctx.enter_context(nc.Block())

        @block.sync
        def _(sp):
            def load(m):
                name, i = BLOCKS[m // 2]
                if m >= HALVES:
                    done = 2 * (m - HALVES) + 2
                    sp.wait_ge(lo_ready, done - pool_rests(done))
                    if pool_rests(done):
                        sp.wait_ge(lo_ready_pool, pool_rests(done))
                sp.dma_start(halves[:, m % HALVES], weight_src(name, i)[:, 4 * (m % 2):4 * (m % 2) + 4])\
                    .then_inc(landed[m % HALVES], 16)

            def expert_load(e, k, slot=None):
                if slot is None:
                    slot = place(e, k)[0]
                sp.dma_start(eslots[slot], expert_src(k, e)).then_inc(e_landed[slot], 16)

            sp.dma_start(x_sb[:, 0], x[0, 0:P]).then_inc(sem("x_landed0"), 16)
            sp.dma_start(gain1, g_mix.partition_broadcast(P)).then_inc(sem("gain_landed"), 16)
            for m in range(2 * len(BLOCKS)):
                if m == 2 * BLOCK_AT[("xbc", 3)]:
                    sp.wait_ge(sem("rel_edge"), 2)
                    skewed = bass.AP(tensor=bias_dram.tensor, offset=0, ap=[[P * (SKEW + 1), A_HEADS], [SKEW + 1, P], [1, SKEW]])
                    sp.dma_start(skewed, rel_sb[:, 0:SKEW].unsqueeze(1).to_broadcast([A_HEADS, P, SKEW]))\
                        .then_inc(sem("rel_stored"), 16)
                if m == 2 * BLOCK_AT[("v", 0)]:
                    sp.wait_ge(misc_ready, ssm_end(N_UNITS - 1))
                    sp.dma_start(mem_sb, mem.rearrange("a (t p) d -> p (a t) d", p=P)).then_inc(sem("mem_landed"), 16)
                if m == 2 * BLOCK_AT[("gc", 0)]:
                    sp.wait_ge(unit_used, first("mv", 1) + 4)
                    expert_load(0, 0)
                    sp.wait_ge(misc_ready, values_end(A_HEADS + X_HEADS - 1))
                    expert_load(0, 1)
                if m == 2 * BLOCK_AT[("bc", 1)]:
                    sp.wait_ge(unit_used, first("ba", 1) + 4)
                    expert_load(0, 2)
                if m == 2 * BLOCK_AT[("wo", 1)]:
                    sp.wait_ge(unit_used, first("gc", 1) + 4)
                    sp.dma_start(x_sb, x.rearrange("a (t p) d -> p (a t) d", p=P)).then_inc(sem("x_again"), 16)
                    sp.dma_start(gain2, norm_ffn.partition_broadcast(P)).then_inc(sem("gain2_landed"), 16)
                    sp.wait_ge(sem("bias_rows_zero"), 1)
                    sp.dma_start(bias_d[0:EXPERTS, :], b_down).then_inc(sem("bias_rows_landed"), 16)
                load(m)
            sp.wait_ge(lo_ready, UNITS - pool_rests(UNITS))
            sp.wait_ge(lo_ready_pool, pool_rests(UNITS))
            expert_load(0, 3)
            expert_load(0, 4)
            sp.wait_ge(sem("bias_rows_zero"), 2)
            sp.dma_start(bias_gu[0:EXPERTS, 0:D], b_gate).then_inc(sem("bias_rows_landed"), 16)
            sp.dma_start(bias_gu[0:EXPERTS, D:2 * D], b_up).then_inc(sem("bias_rows_landed"), 16)
            sp.wait_ge(unit_used, UNITS)
            for k in range(5, SLOTS):
                expert_load(k // LOADS, k % LOADS)

            def round_loads(j, e0, skip=0):
                for n in range(skip, ROUND * LOADS):
                    slot, turn = place(0, n)
                    sp.wait_ge(e_used[slot], j * TURNS + turn)
                    expert_load(e0 + n // LOADS, n % LOADS, slot)

            round_loads(0, 0, SLOTS)
            with sp.Fori(1, EXPERTS // ROUND) as j:
                round_loads(j, j * ROUND)
            sp.wait_ge(sem("passes_known"), 1)
            n_pass = sp.value_load(npass_i[0:1, 0:1], min_val=1, max_val=PASSES)
            with sp.If(n_pass > 1):
                with sp.Fori(1, n_pass) as b:
                    with sp.Fori(0, EXPERTS // ROUND) as j:
                        round_loads(b * (EXPERTS // ROUND) + j, j * ROUND)
            for t in range(TT):
                for h in range(2):
                    sp.wait_ge(sem("y_ready"), 2 * t + h + 1)
                    cols = slice(h * NB, (h + 1) * NB)
                    sp.dma_start(out[0, t * P:(t + 1) * P, cols], x_sb[:, t, cols]).then_inc(sem("y_stored"), 16)
            sp.wait_ge(sem("y_stored"), 16 * 2 * TT)

        @block.gpsimd
        def _(pool):
            pool.memset(ones, 1.0).then_inc(sem("ones_set"), 1)
            pool.wait_ge(sem("ones_set"), 1)
            pool.affine_select(out=ident[:], in_=ones, compare_op=ALU.is_equal, fill=0.0, base=0,
                               pattern=[[-1, P]], channel_multiplier=1).then_inc(sem("masks"), 1)
            pool.affine_select(out=upto[:], in_=ones, compare_op=ALU.is_ge, fill=0.0, base=0,
                               pattern=[[1, P]], channel_multiplier=-1).then_inc(sem("masks"), 1)
            pool.affine_select(out=after[:], in_=ones, compare_op=ALU.is_ge, fill=0.0, base=-1,
                               pattern=[[-1, P]], channel_multiplier=1).then_inc(sem("masks"), 1)
            pool.iota(iota_i[:], pattern=[[1, BLK]], base=0, channel_multiplier=0).then_inc(sem("iota"), 1)
            pool.memset(craw[:], 0.0).then_inc(sem("craw_zero"), 1)
            pool.dma_start(rel_sb[:, 127:384], rel_rev).then_inc(sem("rel_landed"), 16)

            small = sem("small_landed")
            pool.dma_start(cw_sb[:], conv_w).then_inc(small, 16)
            pool.dma_start(cb_sb[:], conv_b).then_inc(small, 16)
            pool.dma_start(wdt_sb, w_dt.rearrange("(c p) n -> p c n", p=P)).then_inc(small, 16)
            pool.dma_start(gmem_sb[:], g_mem).then_inc(small, 16)
            pool.dma_start(gssm_sb[:], g_ssm).then_inc(small, 16)
            pool.dma_start(ag_sb[:], a_gains).then_inc(small, 16)
            pool.dma_start(xg_sb[:], x_gains).then_inc(small, 16)
            pool.dma_start(wr_sb[:], w_router.rearrange("(c p) n -> p c n", p=P)).then_inc(small, 16)
            for j, row in enumerate((dt_bias, a_log, d_skip, b_router)):
                pool.dma_start(head_rows[:, j], row.partition_broadcast(P)).then_inc(small, 16)
            for step in SCHED:
                kind = step[0]
                if kind == "split" and step[1] % QUARTERS == QUARTERS - 1:
                    w = step[1]
                    raw, hi, lo = quarter(w)
                    pool.wait_ge(hi_ready, w + 1)
                    pool.tensor_tensor(lo, raw, hi.bitcast(F32), ALU.subtract).then_inc(lo_ready_pool, 1)
                elif kind == "xdt":
                    half, part = step[1:]
                    hs, cs = slice(16 * half, 16 * half + 16), slice(D * half, D * (half + 1))
                    t = part // 2

                    def heads(v):
                        return v[:, cs].rearrange("p (h d) -> p h d", d=SSM_DIM)

                    def by_head(v):
                        return v[:, hs].unsqueeze(2).to_broadcast([P, 16, SSM_DIM])

                    if part == 0:
                        pool.wait_ge(misc_taken, MISC_AT[("xsT", 4 * half + 3)] + 1)
                        pool.wait_ge(sem("xs_first"), 4 * half + 4)
                        pool.wait_ge(sem("a_ready"), 1)
                    if part < 4 and part % 2 == 0:
                        ins = pool.tensor_tensor(heads(xdt[t]), heads(xs[t]), by_head(dt_sb[:, t]), ALU.mult)
                    elif part < 4:
                        pool.wait_ge(sem("xdt_ready"), 5 * half + part)
                        ins = pool.tensor_tensor(heads(xs[t]), heads(xs[t]), by_head(head_rows[:, 2]), ALU.mult)
                    else:
                        pool.wait_ge(exp_taken, 1)
                        pool.wait_ge(sem("xdt_ready"), 5 * half + 1)
                        ins = pool.tensor_tensor(heads(fx), heads(xdt[0]), by_head(decays[:, 0]), ALU.mult)
                    ins.then_inc(sem("xdt_ready"), 1)
                elif kind == "spread":
                    u, g, t, d = step[1:]
                    n = 2 * u + d
                    h0 = g * (SSM_HEADS // GROUPS) + 4 * d
                    if n >= 2:
                        pool.wait_ge(exp_ready, n)
                    pool.tensor_tensor(work[:, 2 + d].rearrange("p (h l) -> p h l", h=4),
                                       upto[:].unsqueeze(1).to_broadcast([P, 4, P]),
                                       a_sb[:, t, h0:h0 + 4].unsqueeze(2).to_broadcast([P, 4, P]),
                                       ALU.mult).then_inc(sem("steps_ready"), 1)
                elif kind == "clear":
                    pool.wait_ge(misc_ready, MISC_AT[("yT", 3)] + 2)
                    pool.memset(qz, 0.0).then_inc(sem("qz_zero"), 1)
                elif kind == "mergedT" and step[1] == 0:
                    pool.wait_ge(unit_used, first("ba", 1) + QUARTERS)
                    pool.memset(bias_d, 0.0).then_inc(sem("bias_rows_zero"), 1)
            pool.memset(hot_wT, 0.0).then_inc(sem("hot_wT_zero"), 1)
            pool.wait_ge(unit_used, UNITS)
            pool.memset(bias_gu, 0.0).then_inc(sem("bias_rows_zero"), 1)

        @block.scalar
        def _(act):
            roots = [0]

            def root(width):
                roots[0] += 1
                act.wait_ge(sem("variance"), roots[0])
                act.activation(root_out[:, 0:width], root_in[:, 0:width], ACT.Sqrt).then_inc(sem("root_ready"), 1)

            def exp_group(i):
                act.wait_ge(exp_ready, i + 1)

            def load_bias(h):
                src = bass.AP(tensor=bias_dram.tensor, offset=h * P * (SKEW + 1) + 127, ap=[[SKEW, P], [1, T]])
                act.dma_start(bias4[:, h % 4], src).then_inc(bias_landed[h % 4], 16)

            act.dma_start(x_sb[:, 1], x[0, P:T]).then_inc(sem("x_landed1"), 16)
            for t in range(TT):
                act.wait_ge(sem(f"x_landed{t}"), 16)
                act.activation(q_raw[:, t], x_sb[:, t], ACT.Square, accum_out=ss_x[:, t:t + 1])\
                    .then_inc(sem("row_squares"), 1)
            root(TT)
            n = 0
            br = 0
            n_gates = 0
            for step in SCHED:
                kind = step[0]
                if kind == "headnorm":
                    root(TT * (X_HEADS if step[1] in ("kx", "qx") else A_HEADS))
                elif kind == "ynorm":
                    root(N_UNITS)
                elif kind == "memnorm":
                    root(TT)
                elif kind == "split":
                    w = step[1]
                    raw, hi, lo = quarter(w)
                    if w % 2 == 0:
                        act.wait_ge(landed[w // 2 % HALVES], 16 * (w // 2 // HALVES + 1))
                    if w >= SPLITS:
                        act.wait_ge(unit_used, w - SPLITS + 1)
                    act.activation(hi, raw, ACT.Copy).then_inc(hi_ready, 1)
                elif kind in ("yT", "memT"):
                    pair, gain = (ybT, gssm_sb) if kind == "yT" else (memT, gmem_sb)
                    if step[1] == 0:
                        act.wait_ge(sem("small_landed"), 16 * 12)
                    for k in range(MISC_GROUPS[kind]):
                        n_misc = MISC_AT[step] + k
                        act.wait_ge(misc_ready, n_misc + 1)
                        for j in range(2):
                            c = 2 * (MISC_GROUPS[kind] * step[1] + k) + j
                            act.activation(pair[0][:, c], ps[:, MISC_BANKS[n_misc % 3], j * T:(j + 1) * T], ACT.Copy,
                                           scale=gain[:, c:c + 1]).then_inc(sem(kind + "_rounded"), 1)
                elif kind in ("hT", "mergedT"):
                    if kind == "hT":
                        act.wait_ge(sem("rows_scaled"), 2)
                    for k in range(MISC_GROUPS[kind]):
                        n_misc = MISC_AT[step] + k
                        c2 = k if kind == "hT" else 2 * step[1] + k
                        act.wait_ge(misc_ready, n_misc + 1)
                        act.activation((hT if kind == "hT" else mergedT)[0][:, 2 * c2:2 * c2 + 2],
                                       ps[:, MISC_BANKS[n_misc % 3], :].rearrange("p (c t) -> p c t", c=2), ACT.Copy)\
                            .then_inc(sem(kind + "_rounded"), 1)
                elif kind == "take" and step[1] == "wo":
                    i = step[2]
                    cols = slice(i * NB, (i + 1) * NB)
                    for h in range(2):
                        act.wait_ge(gemm_taken, GEMM_AT[("wo", i, h)] + 1)
                        act.wait_ge(sem("br_merged"), 12)
                        if i:
                            act.wait_ge(sem("out_squares"), h + 1)
                        act.activation(tmp[:, h], x_sb[:, h, cols], ACT.Square, accum_out=ss_part[:, 2 * i + h:2 * i + h + 1])\
                            .then_inc(sem("out_squares"), 1)
                elif kind == "take" and step[1:] != ("bc", 1):
                    name, i = step[1:]
                    cols = slice(i * NB, (i + 1) * NB)
                    if (name, i) == ("xbc", 0):
                        act.wait_ge(sem("rel_landed"), 16)
                        act.activation(rel_sb[:, 0:127], rel_sb[:, 127:128].to_broadcast([A_HEADS, 127]), ACT.Copy)\
                            .then_inc(sem("rel_edge"), 1)
                        act.activation(rel_sb[:, 384:512], rel_sb[:, 383:384].to_broadcast([A_HEADS, 128]), ACT.Copy)\
                            .then_inc(sem("rel_edge"), 1)
                    if name in GATES and n_gates:
                        act.wait_ge(sem("br_merged"), 2 * n_gates)
                    n_gates += name in GATES
                    for h in range(2):
                        act.wait_ge(unit_used, block_end(name, i))
                        src = ps[:, GEMM_BANKS[n % 4], :]
                        func = ACT.Copy
                        if name in ("q", "k", "v", "qx", "mk", "mv"):
                            dst = {"q": q_raw, "k": k_raw, "v": v_sb, "qx": qx_raw, "mk": kx_raw, "mv": vx}[name][:, h, cols]
                            if h == 0 and name == "mv" and i == 0:
                                act.wait_ge(misc_ready, values_end(A_HEADS - 1))
                        elif name == "xbc":
                            j = 2 * i + h
                            if j == 0:
                                act.wait_ge(sem("craw_zero"), 1)
                            if j >= 2:
                                act.wait_ge(sem("conv_done"), j - 1)
                            dst = craw[:, j % 2, :, TAPS - 1:TAPS - 1 + T]
                            src = src.rearrange("p (j t) -> p j t", j=2)
                        elif name == "z":
                            if i >= 2:
                                act.wait_ge(sem("gated"), 2 * (i - 2) + h + 1)
                            dst, func = zbuf[:, i % 2, h], ACT.Silu
                        elif name in GATES:
                            dst, func = sig[:, h], ACT.Sigmoid
                        else:
                            if br >= 2:
                                act.wait_ge(sem("br_merged"), br - 1)
                            dst = tmp[:, br % 2]
                            br += 1
                        act.activation(dst, src, func).then_inc(gemm_taken, 1)
                        n += 1
                elif kind == "square":
                    name = step[1]
                    src, last, order = {"q": (4, ("q", 1, 1), 0), "k": (9, ("k", 1, 1), 1), "qx": (12, ("qx", 1, 1), 2),
                                        "kx": (13, ("mk", 1, 1), 3)}[name]
                    act.wait_ge(gemm_taken, GEMM_AT[last] + 1)
                    if order:
                        act.wait_ge(sem("head_sums"), order)
                    if name == "q":
                        act.wait_ge(misc_ready, MISC_AT[("xsT", INNER // P // 2 - 1)] + 1)
                        act.wait_ge(sem("silu_out"), CONV_T // 2)
                    if name == "qx":
                        act.wait_ge(misc_ready, MISC_AT[("memT", 3)] + 1)
                    act.activation(squares[name], S[:, src], ACT.Square).then_inc(sem("head_squares"), 1)
                elif kind == "memsquare":
                    act.wait_ge(sem("mem_landed"), 16)
                    for t in range(TT):
                        act.activation(tmp[:].rearrange("p a n -> p (a n)"), mem_sb[:, t], ACT.Square,
                                       accum_out=ss_m[:, t:t + 1]).then_inc(sem("mem_squares"), 1)
                        act.wait_ge(sem("mem_squares"), t + 1)
                elif kind == "scores":
                    m, br_name, h = step[1:]
                    act.wait_ge(misc_taken, MISC_AT[step] + 1)
                    act.wait_ge(sem("maxima"), m + 1)
                    bounds = ((0, MEM), (MEM, 2 * MEM)) if br_name == "x" else ((0, P), (P, 3 * P))
                    for t, (lo, hi) in enumerate(bounds):
                        act.activation(work[:, m % 2, lo:hi], work[:, m % 2, lo:hi], ACT.Exp, bias=nmx[:, m % 2, t:t + 1],
                                       accum_out=sums[:, m % 2, t:t + 1]).then_inc(sem("exp_out"), 1)
                    if br_name == "a" and h + 4 < A_HEADS:
                        load_bias(h + 4)
                elif kind == "silu":
                    j = step[1]
                    act.wait_ge(sem("conv_done"), j + 1)
                    if 2 * j < INNER // P:
                        if j >= 2:
                            act.wait_ge(misc_ready, MISC_AT[("xsT", j - 2)] + 1)
                        dst = conv_out[:, j % 2]
                    else:
                        dst = bcT[:, 2 * j - INNER // P:2 * j - INNER // P + 2, :]
                    act.activation(dst, conv_acc[:, j % 2], ACT.Silu).then_inc(sem("silu_out"), 1)
                elif kind == "dt":
                    act.wait_ge(sem("dt_abs"), 1)
                    act.activation(dtw[:, 1], dtw[:, 1], ACT.Exp, scale=-1.0).then_inc(sem("dt_exp"), 1)
                    act.wait_ge(sem("dt_exp"), 1)
                    act.wait_ge(sem("dt_one"), 1)
                    act.activation(dtw[:, 3], dtw[:, 2], ACT.Ln).then_inc(sem("dt_ln"), 1)
                    act.activation(a_head[:], head_rows[:, 1], ACT.Exp).then_inc(sem("a_exp"), 1)
                elif kind == "decay":
                    exp_group(0)
                    act.activation(decays[:].rearrange("p a h -> p (a h)"), ps[:, EXP_BANK, 0:2 * SSM_HEADS],
                                   ACT.Exp).then_inc(exp_taken, 1)
                elif kind == "spread":
                    u, d = step[1], step[4]
                    exp_group(1 + 2 * u + d)
                    if u:
                        act.wait_ge(misc_ready, ssm_end(u - 1))
                    act.activation(work[:, d], ps[:, EXP_BANK, :], ACT.Exp).then_inc(exp_taken, 1)
                    if u == 0 and d == 0:
                        act.wait_ge(sem("rel_stored"), 16)
                        for h in range(4):
                            load_bias(h)
                elif kind == "ssm":
                    u, g, t = step[1:]
                    act.wait_ge(sem("gated"), u + 1)
                    if u:
                        act.wait_ge(sem("y_squares"), u)
                    act.activation(sq_junk, xs[t][:, g * GW:(g + 1) * GW], ACT.Square,
                                   accum_out=ss_y[:, t * GROUPS + g:t * GROUPS + g + 1]).then_inc(sem("y_squares"), 1)
            root(TT)
            act.wait_ge(sem("second_norm"), 1)
            act.wait_ge(misc_ready, MISC_AT["places"])
            for t in range(TT):
                act.activation(h2[:, t], h2[:, t], ACT.Copy, scale=rs_for_act[:, t:t + 1]).then_inc(sem("h2_ready"), 1)
            act.wait_ge(sem("top_shifted"), 1)
            act.activation(e4, e4, ACT.Exp).then_inc(sem("top_exp"), 1)
            act.wait_ge(sem("gather_ready"), 1)
            act.activation(xgT.rearrange("p c j -> p (c j)"), ps[:, X_BANK, :], ACT.Copy).then_inc(sem("xg_ready"), 1)
            act.wait_ge(sem("passes_known"), 1)
            n_pass = act.value_load(npass_i[0:1, 0:1], min_val=1, max_val=PASSES)
            with act.Fori(0, n_pass) as b:
                with act.Fori(0, EXPERTS) as e:
                    i = b * EXPERTS + e
                    act.wait_ge(sem("g_ready"), i + 1)
                    act.activation(sg_sb, g_sb, ACT.Sigmoid, scale=ALPHA).then_inc(sem("sg_ready"), 1)
                    act.wait_ge(sem("hot_wT_ready"), i + 1)
                    for h in range(2):
                        act.activation(hot_wT[64 * h:64 * h + 64, h],
                                       ps[64 * h:64 * h + 64, D_BANK, 0:T].rearrange("p (t j) -> p t j", t=TT),
                                       ACT.Copy).then_inc(sem("scatter_ready"), 1)
                    act.wait_ge(sem("actT_out"), i + 1)
                    act.activation(actT.rearrange("p c j -> p (c j)"), ps[:, G_BANK, :], ACT.Copy)\
                        .then_inc(sem("actT_ready"), 1)
                    act.wait_ge(sem("gather_ready"), i + 2)
                    act.activation(xgT.rearrange("p c j -> p (c j)"), ps[:, X_BANK, :], ACT.Copy)\
                        .then_inc(sem("xg_ready"), 1)

        @block.vector
        def _(dve):
            chain = [0]

            def link(ins):
                chain[0] += 1
                ins.then_inc(sem("vector_chain"), 1)
                dve.wait_ge(sem("vector_chain"), chain[0])

            misc = [0]
            roots = [0]

            def group():
                misc[0] += 1
                dve.wait_ge(misc_ready, misc[0])
                return MISC_BANKS[(misc[0] - 1) % 3]

            def rstd(dst, src, width):
                roots[0] += 1
                n = dst.shape[1]
                v, r = root_in[:, 0:n], root_out[:, 0:n]
                dve.tensor_scalar(v, src, 1.0 / width, EPS, ALU.mult, ALU.add).then_inc(sem("variance"), 1)
                dve.wait_ge(sem("root_ready"), roots[0])
                link(dve.reciprocal(dst, r))
                link(dve.tensor_tensor(r, dst, v, ALU.mult))
                link(dve.tensor_tensor(r, r, dst, ALU.mult))
                link(dve.tensor_scalar(r, r, -0.5, 1.5, ALU.mult, ALU.add))
                link(dve.tensor_tensor(dst, dst, r, ALU.mult))

            dve.wait_ge(sem("masks"), 3)
            dve.tensor_copy(upto_r[:], upto[:]).then_inc(sem("vector_side"), 1)
            dve.tensor_copy(ones_r[:], ones).then_inc(sem("vector_side"), 1)
            dve.wait_ge(sem("iota"), 1)
            link(dve.tensor_copy(iota_j[:], iota_i[:]))
            dve.tensor_copy(iota2[:], iota_j[:].unsqueeze(1).to_broadcast([P, 2, BLK])).then_inc(sem("vector_side"), 1)
            dve.tensor_scalar(steps_b[:], iota_j[:, 0:PASSES], float(BLK), None, ALU.mult).then_inc(sem("vector_side"), 1)
            dve.wait_ge(sem("row_squares"), 2)
            rstd(rs_x, ss_x, D)
            dve.wait_ge(sem("gain_landed"), 16)
            for t in range(TT):
                dve.scalar_tensor_tensor(out=xn[:, t], in0=x_sb[:, t], scalar=rs_x[:, t:t + 1], in1=gain1,
                                         op0=ALU.mult, op1=ALU.mult).then_inc(sem("rows_scaled"), 1)

            br = 0
            norms = 0
            for step in SCHED:
                kind = step[0]
                if kind in ("yT", "memT"):
                    pair, gain = (ybT, gssm_sb) if kind == "yT" else (memT, gmem_sb)
                    for k in range(MISC_GROUPS[kind]):
                        b = group()
                        dve.wait_ge(sem(kind + "_rounded"), 2 * (MISC_GROUPS[kind] * step[1] + k) + 2)
                        for j in range(2):
                            c = 2 * (MISC_GROUPS[kind] * step[1] + k) + j
                            ins = dve.scalar_tensor_tensor(out=pair[1][:, c], in0=ps[:, b, j * T:(j + 1) * T],
                                                           scalar=gain[:, c:c + 1], in1=pair[0][:, c].bitcast(F32),
                                                           op0=ALU.mult, op1=ALU.subtract)
                            if j == 0:
                                chain[0] += 1
                                ins.then_inc(sem("vector_chain"), 1)
                                dve.wait_ge(sem("vector_chain"), chain[0])
                            else:
                                ins.then_inc(misc_taken, 1)
                elif kind in ("hT", "mergedT"):
                    both = hT if kind == "hT" else mergedT
                    for k in range(MISC_GROUPS[kind]):
                        c2 = k if kind == "hT" else 2 * step[1] + k
                        b = group()
                        dve.wait_ge(sem(kind + "_rounded"), c2 + 1)
                        pair = slice(2 * c2, 2 * c2 + 2)
                        dve.tensor_tensor(both[1][:, pair], ps[:, b, :].rearrange("p (c t) -> p c t", c=2),
                                          both[0][:, pair].bitcast(F32), ALU.subtract).then_inc(misc_taken, 1)
                elif kind == "split":
                    w = step[1]
                    if w % QUARTERS != QUARTERS - 1:
                        raw, hi, lo = quarter(w)
                        dve.wait_ge(hi_ready, w + 1)
                        dve.tensor_tensor(lo, raw, hi.bitcast(F32), ALU.subtract).then_inc(lo_ready, 1)
                elif kind == "memnorm":
                    dve.wait_ge(sem("mem_squares"), TT)
                    rstd(rs_m, ss_m, D)
                    for t in range(TT):
                        dve.tensor_scalar(mem_sb[:, t], mem_sb[:, t], rs_m[:, t:t + 1], None, ALU.mult)\
                            .then_inc(sem("mem_scaled"), 1)
                elif kind == "headnorm":
                    raw, heads = {"kx": (kx_raw, X_HEADS), "qx": (qx_raw, X_HEADS),
                                  "q": (q_raw, A_HEADS), "k": (k_raw, A_HEADS)}[step[1]]
                    norms += 1
                    dve.wait_ge(sem("head_squares"), norms)
                    w = D // heads
                    ss = ss_h[:, 0:TT * heads]
                    dve.tensor_reduce(ss, squares[step[1]].rearrange("p (th d) -> p th d", d=w), AX, ALU.add)\
                        .then_inc(sem("head_sums"), 1)
                    dve.wait_ge(sem("head_sums"), norms)
                    rstd(ss, ss, w)
                    view = raw[:].rearrange("p t (h d) -> p (t h) d", d=w)
                    dve.tensor_tensor(view, view, ss.unsqueeze(2).to_broadcast([P, TT * heads, w]), ALU.mult)\
                        .then_inc(sem("head_normed"), 1)
                elif kind == "headT":
                    name = step[1]
                    if name == "q":
                        dve.wait_ge(sem("qz_zero"), 1)
                    for c2 in range(4):
                        b = group()
                        for j in range(2):
                            c = 2 * c2 + j
                            src = ps[:, b, j * T:(j + 1) * T]
                            if name == "kx":
                                last = dve.tensor_scalar(kxT[:, c], src, xg_sb[:, 2 + j:3 + j], None, ALU.mult)
                            elif name == "qx":
                                last = dve.tensor_scalar(qxT[:, c], src, xg_sb[:, j:j + 1], X_DIM ** -0.5,
                                                         ALU.mult, ALU.mult)
                            elif name == "k":
                                last = dve.tensor_scalar(kT[:, c], src, ag_sb[:, 1:2], None, ALU.mult)
                            else:
                                for r in range(2):
                                    rows = slice(64 * r, 64 * r + 64)
                                    last = dve.tensor_scalar(qz[rows, 2 * c + r], src[rows], ag_sb[rows, 0:1],
                                                             A_DIM ** -0.5, ALU.mult, ALU.mult)
                        last.then_inc(misc_taken, 1)
                elif kind == "scores":
                    m, br_name, h = step[1:]
                    b = group()
                    sc = work[:, m % 2]
                    if br_name == "x":
                        dve.tensor_copy(sc, ps[:, b, :]).then_inc(misc_taken, 1)
                        bounds = ((0, MEM), (MEM, 2 * MEM))
                    else:
                        bh = bias4[:, h % 4]
                        dve.wait_ge(bias_landed[h % 4], 16 * (h // 4 + 1))
                        link(dve.memset(bh[0:CHUNK, T - CHUNK:T], MASKED))
                        link(dve.tensor_tensor(sc[:, 0:P], ps[:, b, 0:P], bh[:, P:T], ALU.add))
                        dve.tensor_tensor(sc[:, P:3 * P], ps[:, b, P:3 * P], bh, ALU.add).then_inc(misc_taken, 1)
                        bounds = ((0, P), (P, 3 * P))
                    dve.wait_ge(misc_taken, misc[0])
                    for t, (lo, hi) in enumerate(bounds):
                        chain[0] += 1
                        dve.tensor_reduce(mx[:, t:t + 1], sc[:, lo:hi], AX, ALU.max).then_inc(sem("vector_chain"), 1)
                    dve.wait_ge(sem("vector_chain"), chain[0])
                    if m >= 2:
                        dve.wait_ge(sem("exp_out"), 2 * m - 2)
                    dve.tensor_scalar(nmx[:, m % 2], mx, -1.0, None, ALU.mult).then_inc(sem("maxima"), 1)
                elif kind == "soften":
                    m, br_name, h = step[1:]
                    dve.wait_ge(sem("exp_out"), 2 * m + 2)
                    sc = work[:, m % 2]
                    link(dve.reciprocal(rc, sums[:, m % 2]))
                    bounds = ((0, MEM), (MEM, 2 * MEM)) if br_name == "x" else ((0, P), (P, 3 * P))
                    for t, (lo, hi) in enumerate(bounds):
                        dve.tensor_scalar(sc[:, lo:hi], sc[:, lo:hi], rc[:, t:t + 1], None, ALU.mult)\
                            .then_inc(sem("probs"), 1)
                elif kind == "probsT":
                    m, br_name, h = step[1:]
                    b = group()
                    w = 512 if br_name == "x" else 384
                    dve.tensor_copy(work[:, 2 + m % 2, 0:w], ps[:, b, 0:w]).then_inc(misc_taken, 1)
                elif kind == "values":
                    m, br_name, h = step[1:]
                    b = group()
                    if br_name == "x":
                        src = ps[:, b, :].rearrange("p (c t) -> p c t", c=2)
                        hi, lo = ycT[0][:, 2 * h:2 * h + 2], ycT[1][:, 2 * h:2 * h + 2]
                    else:
                        rows = slice(64 * (h % 2), 64 * (h % 2) + 64)
                        src, hi, lo = ps[rows, b, 0:T], yaT[0][rows, h // 2], yaT[1][rows, h // 2]
                    link(dve.tensor_copy(hi, src))
                    dve.tensor_tensor(lo, src, hi.bitcast(F32), ALU.subtract).then_inc(misc_taken, 1)
                elif kind == "conv":
                    j = step[1]
                    dve.wait_ge(gemm_taken, GEMM_AT[("xbc", j // 2, j % 2)] + 1)
                    if j >= 2:
                        dve.wait_ge(sem("silu_out"), j - 1)
                    for tap in range(TAPS):
                        for i in range(2):
                            c = 2 * j + i
                            acc, src = conv_acc[:, j % 2, i], craw[:, j % 2, i, tap:tap + T]
                            if tap == 0:
                                ins = dve.tensor_scalar(acc, src, cw_sb[:, c, 0:1], cb_sb[:, c:c + 1], ALU.mult, ALU.add)
                            else:
                                ins = dve.scalar_tensor_tensor(out=acc, in0=src, scalar=cw_sb[:, c, tap:tap + 1],
                                                               in1=acc, op0=ALU.mult, op1=ALU.add)
                            if tap == TAPS - 1 and i == 1:
                                ins.then_inc(sem("conv_done"), 1)
                            else:
                                chain[0] += 1
                                ins.then_inc(sem("vector_chain"), 1)
                        dve.wait_ge(sem("vector_chain"), chain[0])
                elif kind == "xsT":
                    j = step[1]
                    b = group()
                    for t in range(TT):
                        last = dve.tensor_copy(xs[t][:, j * 256:(j + 1) * 256], ps[:, b, t * 256:(t + 1) * 256])
                        if t == 0:
                            last.then_inc(sem("xs_first"), 1)
                    last.then_inc(misc_taken, 1)
                elif kind == "take" and step[1:] == ("xbc", 0):
                    dve.wait_ge(sem("small_landed"), 16 * 12)
                    link(dve.tensor_copy(wdt_r[:, 0], wdt_sb))
                    dve.tensor_tensor(wdt_r[:, 1], wdt_sb, wdt_r[:, 0].bitcast(F32), ALU.subtract)\
                        .then_inc(sem("wdt_ready"), 1)
                elif kind == "dt":
                    b = group()
                    v = dtw[:, 0].rearrange("p (t h) -> p t h", t=TT)
                    dve.tensor_tensor(v, ps[:, b, 0:64].rearrange("p (t h) -> p t h", t=TT),
                                      head_rows[:, 0].unsqueeze(1).to_broadcast([P, TT, SSM_HEADS]), ALU.add)\
                        .then_inc(misc_taken, 1)
                    dve.wait_ge(misc_taken, misc[0])
                    dve.scalar_tensor_tensor(out=dtw[:, 1], in0=dtw[:, 0], scalar=-1.0, in1=dtw[:, 0],
                                             op0=ALU.mult, op1=ALU.max).then_inc(sem("dt_abs"), 1)
                    dve.wait_ge(sem("dt_exp"), 1)
                    dve.tensor_scalar(dtw[:, 2], dtw[:, 1], 1.0, None, ALU.add).then_inc(sem("dt_one"), 1)
                    dve.wait_ge(sem("dt_one"), 1)
                    link(dve.tensor_scalar(dtw[:, 4], dtw[:, 2], -1.0, 1e-30, ALU.add, ALU.max))
                    dve.wait_ge(sem("dt_ln"), 1)
                    link(dve.tensor_tensor(dtw[:, 3], dtw[:, 3], dtw[:, 1], ALU.mult))
                    link(dve.reciprocal(dtw[:, 5], dtw[:, 4]))
                    link(dve.tensor_tensor(dtw[:, 3], dtw[:, 3], dtw[:, 5], ALU.mult))
                    link(dve.tensor_scalar(dtw[:, 5], dtw[:, 4], 1e-20, None, ALU.is_lt))
                    link(dve.tensor_tensor(dtw[:, 5], dtw[:, 5], dtw[:, 1], ALU.mult))
                    link(dve.tensor_tensor(dtw[:, 3], dtw[:, 3], dtw[:, 5], ALU.add))
                    link(dve.scalar_tensor_tensor(out=dtw[:, 4], in0=dtw[:, 0], scalar=0.0, in1=dtw[:, 3],
                                                  op0=ALU.max, op1=ALU.add))
                    dve.wait_ge(sem("a_exp"), 1)
                    dve.scalar_tensor_tensor(out=a_sb, in0=dt_sb, scalar=-1.0,
                                             in1=a_head[:].unsqueeze(1).to_broadcast([P, TT, SSM_HEADS]),
                                             op0=ALU.mult, op1=ALU.mult).then_inc(sem("a_ready"), 1)
                elif kind == "cb":
                    g = step[1]
                    b = group()
                    chain[0] += 2
                    dve.tensor_tensor(cbm[:, g % 2, 0:P], ps[:, b, 0:P], upto[:], ALU.mult)\
                        .then_inc(sem("vector_chain"), 1)
                    dve.tensor_tensor(cbm[:, g % 2, P:2 * P], ps[:, b, 2 * P:3 * P], upto[:], ALU.mult)\
                        .then_inc(sem("vector_chain"), 1)
                    dve.tensor_copy(cbm[:, g % 2, 2 * P:3 * P], ps[:, b, P:2 * P]).then_inc(misc_taken, 1)
                    dve.wait_ge(sem("vector_chain"), chain[0])
                elif kind == "weigh":
                    u, g, t = step[1:]
                    for d in range(2):
                        dve.wait_ge(exp_taken, 1 + 2 * u + d + 1)
                        v = work[:, d].rearrange("p (h l) -> p h l", h=4)
                        dve.tensor_tensor(v, v, cbm[:, g % 2, t * P:(t + 1) * P].unsqueeze(1).to_broadcast([P, 4, P]),
                                          ALU.mult).then_inc(sem("weighed"), 1)
                elif kind == "ssm":
                    u, g, t = step[1:]
                    y = xs[t][:, g * GW:(g + 1) * GW]
                    if u == 0:
                        dve.wait_ge(sem("xdt_ready"), 10)
                    if t == 1:
                        b = group()
                        dve.tensor_tensor(y_off.rearrange("p (h d) -> p h d", d=SSM_DIM),
                                          ps[:, b, :].rearrange("p (h d) -> p h d", d=SSM_DIM),
                                          decays[:, 1, 8 * g:8 * g + 8].unsqueeze(2).to_broadcast([P, 8, SSM_DIM]),
                                          ALU.mult).then_inc(misc_taken, 1)
                        dve.wait_ge(misc_taken, misc[0])
                    b = group()
                    dve.tensor_tensor(y, ps[:, b, :], y, ALU.add).then_inc(misc_taken, 1)
                    dve.wait_ge(misc_taken, misc[0])
                    if t == 1:
                        link(dve.tensor_tensor(y, y, y_off, ALU.add))
                    dve.wait_ge(gemm_taken, GEMM_AT[("z", g, t)] + 1)
                    dve.tensor_tensor(y, y, zbuf[:, g % 2, t], ALU.mult).then_inc(sem("gated"), 1)
                elif kind == "ynorm":
                    dve.wait_ge(sem("y_squares"), N_UNITS)
                    rstd(ss_y, ss_y, GW)
                    for t in range(TT):
                        v = xs[t].rearrange("p (g d) -> p g d", d=GW)
                        dve.tensor_tensor(v, v, ss_y[:, t * GROUPS:(t + 1) * GROUPS].unsqueeze(2)
                                          .to_broadcast([P, GROUPS, GW]), ALU.mult).then_inc(sem("y_normed"), 1)
                elif kind == "take" and step[1] == "wo":
                    i = step[2]
                    cols = slice(i * NB, (i + 1) * NB)
                    dve.wait_ge(unit_used, block_end("wo", i))
                    dve.wait_ge(sem("x_again"), 16)
                    dve.wait_ge(sem("gain2_landed"), 16)
                    for h in range(2):
                        n = GEMM_AT[("wo", i, h)]
                        dve.tensor_tensor(x_sb[:, h, cols], x_sb[:, h, cols], ps[:, GEMM_BANKS[n % 4], :], ALU.add)\
                            .then_inc(gemm_taken, 1)
                        dve.wait_ge(gemm_taken, n + 1)
                        dve.tensor_tensor(h2[:, h, cols], x_sb[:, h, cols], gain2[:, cols], ALU.mult)\
                            .then_inc(sem("out_scaled"), 1)
                elif kind == "outT":
                    for c2 in range(2 * step[1], 2 * step[1] + 2):
                        b = group()
                        dve.tensor_copy(h2T[:, 2 * c2:2 * c2 + 2], ps[:, b, :].rearrange("p (c t) -> p c t", c=2))\
                            .then_inc(misc_taken, 1)
                elif kind == "merge":
                    name, i = step[1:]
                    for h in range(2):
                        cols = slice(i * NB, (i + 1) * NB)
                        src = tmp[:, br % 2]
                        if (name, i) == ("bc", 1):
                            n = GEMM_AT[(name, i, h)]
                            dve.wait_ge(unit_used, block_end(name, i))
                            dve.wait_ge(gemm_taken, GEMM_AT[("gc", 1, 1)] + 1)
                            dve.tensor_tensor(src, ps[:, GEMM_BANKS[n % 4], :], sig[:, h], ALU.mult)\
                                .then_inc(gemm_taken, 1)
                            dve.wait_ge(gemm_taken, n + 1)
                            dve.tensor_tensor(merged[:, h, cols], merged[:, h, cols], src, ALU.add)\
                                .then_inc(sem("br_merged"), 1)
                            br += 1
                            continue
                        dve.wait_ge(gemm_taken, GEMM_AT[(name, i, h)] + 1)
                        if name == "bb":
                            dve.tensor_tensor(merged[:, h, cols], src, sig[:, h], ALU.mult)\
                                .then_inc(sem("br_merged"), 1)
                        else:
                            link(dve.tensor_tensor(src, src, sig[:, h], ALU.mult))
                            dve.tensor_tensor(merged[:, h, cols], merged[:, h, cols], src, ALU.add)\
                                .then_inc(sem("br_merged"), 1)
                        br += 1

            dve.wait_ge(sem("out_squares"), 2 * TT)
            link(dve.tensor_tensor(ss_2, ss_part[:, 0:2], ss_part[:, 2:4], ALU.add))
            rstd(rs_2, ss_2, D)
            dve.tensor_copy(rs_for_act, rs_2).then_inc(sem("second_norm"), 1)
            dve.wait_ge(exp_ready, 2 + 2 * N_UNITS)
            for t in range(TT):
                dve.scalar_tensor_tensor(out=logits[:, t], in0=ps[:, EXP_BANK, t * EXPERTS:(t + 1) * EXPERTS],
                                         scalar=rs_2[:, t:t + 1], in1=head_rows[:, 3], op0=ALU.mult, op1=ALU.add)\
                    .then_inc(exp_taken, 1)
            dve.wait_ge(exp_taken, 1 + 2 * N_UNITS + TT)
            for t in range(TT):
                chain[0] += 1
                dve.max(mx8[:, t], logits[:, t]).then_inc(sem("vector_chain"), 1)
            dve.wait_ge(sem("vector_chain"), chain[0])
            dve.tensor_tensor(e4, mx8[:, :, 0:TOP_K], mx8[:, :, 0:1].to_broadcast([P, TT, TOP_K]), ALU.subtract)\
                .then_inc(sem("top_shifted"), 1)
            for t in range(TT):
                chain[0] += 1
                dve.max_index(idx8[:, t], mx8[:, t], logits[:, t]).then_inc(sem("vector_chain"), 1)
            dve.wait_ge(sem("vector_chain"), chain[0])
            link(dve.tensor_copy(idxf, idx8[:]))
            across = [P, TT, TOP_K, EXPERTS]
            link(dve.tensor_tensor(matches, iota_j[:, 0:EXPERTS].unsqueeze(1).unsqueeze(1).to_broadcast(across),
                                   idxf[:, :, 0:TOP_K].unsqueeze(3).to_broadcast(across), ALU.is_equal))
            link(dve.tensor_reduce(part, matches.rearrange("p t k e -> p t e k"), AX, ALU.add))
            dve.tensor_copy(chosen_r[:], part).then_inc(sem("chosen_ready"), 1)
            dve.wait_ge(sem("top_exp"), 1)
            link(dve.tensor_reduce(s4, e4, AX, ALU.add))
            link(dve.reciprocal(s4, s4))
            link(dve.tensor_tensor(e4, e4, s4.unsqueeze(2).to_broadcast([P, TT, TOP_K]), ALU.mult))
            link(dve.tensor_tensor(matched, matches, e4.unsqueeze(3).to_broadcast(across), ALU.mult))
            link(dve.tensor_reduce(wts, matched.rearrange("p t k e -> p t e k"), AX, ALU.add))

            def find(i):
                for t in range(TT):
                    dve.tensor_scalar(hot[:, t], iota_j[:], place4[:, t, bass.ds(i, 1)], None, ALU.is_equal)\
                        .then_inc(sem("hot_ready"), 1)

            b = group()
            dve.wait_ge(sem("chosen_ready"), 1)
            link(dve.tensor_tensor(part, ps[:, b, 0:64].rearrange("p (t e) -> p t e", t=TT), chosen, ALU.mult))
            dve.tensor_reduce(cmax, ps[:, b, 64:64 + EXPERTS], AX, ALU.max).then_inc(misc_taken, 1)
            for p in range(PASSES):
                cols = slice(p * EXPERTS, (p + 1) * EXPERTS)
                link(dve.tensor_scalar(place4[:, :, cols], part, -1.0 - BLK * p, None, ALU.add))
                if p == 0:
                    find(0)
            dve.wait_ge(misc_taken, misc[0])
            link(dve.tensor_scalar(over, steps_b[:], cmax, None, ALU.is_lt))
            link(dve.tensor_reduce(npass_f, over, AX, ALU.add))
            dve.tensor_copy(npass_i[:], npass_f[0:1, :]).then_inc(sem("passes_known"), 1)
            dve.memset(yb, 0.0).then_inc(sem("yb_ready"), 1)
            link(dve.memset(place4[:, :, PASSES * EXPERTS:NPAD], -1.0))
            for p in range(PASSES):
                cols = slice(p * EXPERTS, (p + 1) * EXPERTS)
                link(dve.tensor_copy(weight4[:, :, cols], wts))
                link(dve.tensor_copy(picks[:, cols], ident[:, 0:EXPERTS]))

            dve.wait_ge(sem("passes_known"), 1)
            n_pass = dve.value_load(npass_i[0:1, 0:1], min_val=1, max_val=PASSES)
            with dve.Fori(0, n_pass) as b_:
                with dve.Fori(0, EXPERTS // ROUND) as j_:
                    j = b_ * (EXPERTS // ROUND) + j_
                    for r in range(ROUND):
                        i = j * ROUND + r
                        (slot_g, turn_g), (slot_u, turn_u), (slot_d, turn_d) = place(r, 2), place(r, 3), place(r, 5)
                        dve.tensor_copy(pick, picks[:, bass.ds(i, 1)].to_broadcast([P, BLK]))\
                            .then_inc(sem("pick_ready"), 1)
                        for t in range(TT):
                            dve.tensor_scalar(hot_w[:, t], iota2[:], place4[:, t, bass.ds(i, 1)],
                                              weight4[:, t, bass.ds(i, 1)], ALU.is_equal, ALU.mult)\
                                .then_inc(sem("hot_w_ready"), 1)
                        dve.wait_ge(sem("gather_ready"), i + 1)
                        find(i + 1)
                        dve.wait_ge(e_used[slot_g], j * TURNS + turn_g + 1)
                        dve.tensor_scalar(g_sb, ps[:, G_BANK, :], LIMIT, None, ALU.min).then_inc(sem("g_ready"), 1)
                        dve.wait_ge(e_used[slot_u], j * TURNS + turn_u + 1)
                        dve.tensor_scalar(u_sb, ps[:, U_BANK, :], LIMIT, -LIMIT, ALU.min, ALU.max)\
                            .then_inc(sem("u_ready"), 1)
                        dve.wait_ge(sem("u_ready"), i + 1)
                        dve.wait_ge(sem("g_ready"), i + 1)
                        dve.scalar_tensor_tensor(out=gu_sb, in0=u_sb, scalar=1.0, in1=g_sb, op0=ALU.add, op1=ALU.mult)\
                            .then_inc(sem("gu_ready"), 1)
                        dve.wait_ge(sem("gu_ready"), i + 1)
                        dve.wait_ge(sem("sg_ready"), i + 1)
                        dve.tensor_tensor(act_sb, gu_sb, sg_sb, ALU.mult).then_inc(sem("act_ready"), 1)
                        dve.wait_ge(e_used[slot_d], j * TURNS + turn_d + 1)
                        dve.tensor_copy(yb, ps[:, D_BANK, :]).then_inc(sem("yb_ready"), 1)
            for t in range(TT):
                for h in range(2):
                    dve.wait_ge(sem("sums_ready"), 2 * t + h + 1)
                    cols = slice(h * NB, (h + 1) * NB)
                    dve.tensor_tensor(x_sb[:, t, cols], ps[:, ACC[2 * t + h], :], x_sb[:, t, cols], ALU.add)\
                        .then_inc(sem("y_ready"), 1)

        @block.tensor
        def _(pe):
            misc = [0]

            def group():
                n = misc[0]
                misc[0] += 1
                if n >= 3:
                    pe.wait_ge(misc_taken, n - 2)
                return MISC_BANKS[n % 3]

            def exp_bank(n):
                if n >= 1:
                    pe.wait_ge(exp_taken, n)
                return EXP_BANK

            def turn(dst, src):
                return pe.transpose(dst, src, ident[:])

            def by_columns(src, c2):
                b = group()
                for j in range(2):
                    for t in range(TT):
                        last = turn(ps[:, b, j * T + t * P:j * T + (t + 1) * P],
                                    src(t)[:, (2 * c2 + j) * P:(2 * c2 + j + 1) * P])
                last.then_inc(misc_ready, 1)

            def three_passes(out, lhs, rhs, start, stop):
                pe.matmul(out, lhs[0], rhs[0], start=start, stop=False, skip_group_check=True)
                pe.matmul(out, lhs[1], rhs[0], start=False, stop=False, skip_group_check=True)
                return pe.matmul(out, lhs[0], rhs[1], start=False, stop=stop, skip_group_check=True)

            pe.wait_ge(sem("masks"), 3)
            n = 0
            for step in SCHED:
                kind = step[0]
                if kind in ("memT", "hT"):
                    pe.wait_ge(sem("mem_scaled" if kind == "memT" else "rows_scaled"), 2)
                    src = mem_sb if kind == "memT" else xn
                    for c2 in range(4) if kind == "hT" else step[1:]:
                        by_columns(lambda t: src[:, t], c2)
                elif kind == "gemm":
                    name, i, q, w = step[1:]
                    raw, hi, lo = quarter(w)
                    pe.wait_ge(lo_ready_pool if q == QUARTERS - 1 else lo_ready, w // QUARTERS + 1
                               if q == QUARTERS - 1 else w + 1 - pool_rests(w))
                    opens = q == 0 and not (name == "bb" and i % 2)
                    closes = q == QUARTERS - 1 and not (name == "bb" and i % 2 == 0)
                    lhs = {"mk": memT, "mv": memT, "bc": ycT, "ba": yaT, "bb": ybT, "wo": mergedT}.get(name, hT)
                    needs = {("mk", 0, 0): ("memT", 3), ("bb", 0, 0): ("yT", 3),
                             ("bc", 0, 0): ("values", 19, "x", 3), ("ba", 0, 0): ("values", 15, "a", 15),
                             ("wo", 0, 0): ("mergedT", 0), ("wo", 0, 2): ("mergedT", 1)}.get((name, i, q))
                    if needs:
                        pe.wait_ge(misc_taken, MISC_AT[needs] + MISC_GROUPS[needs[0]])
                    if w < QUARTERS:
                        pe.wait_ge(misc_taken, MISC_AT[("hT",)] + q + 1)
                    if opens and n >= 4:
                        pe.wait_ge(gemm_taken, n - 2)
                    for h in range(2):
                        b = GEMM_BANKS[(n + h) % 4]
                        for c in range(2):
                            k = 2 * q + c
                            if name == "xbc":
                                for j in range(2):
                                    cols = slice((2 * h + j) * P, (2 * h + j + 1) * P)
                                    last = three_passes(ps[:, b, j * T:(j + 1) * T], (hi[:, c, cols], lo[:, c, cols]),
                                                        (hT[0][:, k], hT[1][:, k]), opens and c == 0 and j == 0,
                                                        closes and c == 1)
                            else:
                                kk = k + KC * (i % 2) if name == "bb" else k
                                tok = slice(h * P, (h + 1) * P)
                                last = three_passes(ps[:, b, :], (lhs[0][:, kk, tok], lhs[1][:, kk, tok]),
                                                    (hi[:, c], lo[:, c]), opens and c == 0, closes and c == 1)
                    last.then_inc(unit_used, 1)
                    if closes:
                        n += 2
                elif kind == "headT":
                    name = step[1]
                    raw, order = {"q": (q_raw, 1), "k": (k_raw, 2), "qx": (qx_raw, 3), "kx": (kx_raw, 4)}[name]
                    pe.wait_ge(sem("head_normed"), order)
                    for c2 in range(4):
                        by_columns(lambda t: raw[:, t], c2)
                elif kind == "scores":
                    m, br, h = step[1:]
                    b = group()
                    if h == 0:
                        pe.wait_ge(misc_taken, MISC_AT[("headT", "kx" if br == "x" else "k")] + 4)
                        pe.wait_ge(misc_taken, MISC_AT[("headT", "qx" if br == "x" else "q")] + 4)
                    for t in range(TT):
                        if br == "x":
                            for j in range(2):
                                last = pe.matmul(ps[:, b, t * MEM:(t + 1) * MEM], qxT[:, 2 * h + j, t * P:(t + 1) * P],
                                                 kxT[:, 2 * h + j], start=(j == 0), stop=(j == 1))
                        else:
                            last = pe.matmul(ps[:, b, t * P:t * P + (t + 1) * P], qz[:, h, t * P:(t + 1) * P],
                                             kT[:, h // 2, 0:(t + 1) * P], start=True, stop=True)
                    last.then_inc(misc_ready, 1)
                elif kind == "probsT":
                    m, br, h = step[1:]
                    b = group()
                    pe.wait_ge(sem("probs"), 2 * m + 2)
                    pr = work[:, m % 2]
                    if br == "x":
                        for k in range(2):
                            for t in range(TT):
                                last = turn(ps[:, b, k * T + t * P:k * T + (t + 1) * P],
                                            pr[:, t * MEM + k * P:t * MEM + (k + 1) * P])
                    else:
                        for j in range(3):
                            last = turn(ps[:, b, j * P:(j + 1) * P], pr[:, j * P:(j + 1) * P])
                    last.then_inc(misc_ready, 1)
                elif kind == "values":
                    m, br, h = step[1:]
                    b = group()
                    pe.wait_ge(misc_taken, MISC_AT[("probsT", m, br, h)] + 1)
                    pT = work[:, 2 + m % 2]
                    if br == "x":
                        pe.wait_ge(gemm_taken, GEMM_AT[("mv", 1, 1)] + 1)
                        for c in range(2):
                            for k in range(2):
                                last = pe.matmul(ps[:, b, c * T:(c + 1) * T],
                                                 vx[:, k, h * X_DIM + c * P:h * X_DIM + (c + 1) * P],
                                                 pT[:, k * T:(k + 1) * T], start=(k == 0), stop=(k == 1))
                    else:
                        pe.wait_ge(gemm_taken, GEMM_AT[("v", 1, 1)] + 1)
                        rows = slice(64 * (h % 2), 64 * (h % 2) + 64)
                        hc = slice(h * A_DIM, (h + 1) * A_DIM)
                        pe.matmul(ps[rows, b, 0:T], v_sb[:, 0, hc], pT[:, 0:T], start=True, stop=False)
                        last = pe.matmul(ps[rows, b, P:T], v_sb[:, 1, hc], pT[:, T:T + P], start=False, stop=True)
                    last.then_inc(misc_ready, 1)
                elif kind == "xsT":
                    j = step[1]
                    b = group()
                    pe.wait_ge(sem("silu_out"), j + 1)
                    for t in range(TT):
                        for c in range(2):
                            last = turn(ps[:, b, (2 * t + c) * P:(2 * t + c + 1) * P],
                                        conv_out[:, j % 2, c, t * P:(t + 1) * P])
                    last.then_inc(misc_ready, 1)
                elif kind == "dt":
                    b = group()
                    pe.wait_ge(sem("wdt_ready"), 1)
                    for t in range(TT):
                        for c in range(KC):
                            tok = slice(t * P, (t + 1) * P)
                            last = three_passes(ps[:, b, t * SSM_HEADS:(t + 1) * SSM_HEADS],
                                                (hT[0][:, c, tok], hT[1][:, c, tok]), (wdt_r[:, 0, c], wdt_r[:, 1, c]),
                                                c == 0, c == KC - 1)
                    last.then_inc(misc_ready, 1)
                elif kind == "decay":
                    b = exp_bank(0)
                    pe.wait_ge(sem("a_ready"), 1)
                    pe.matmul(ps[:, b, 0:SSM_HEADS], after[:], a_sb[:, 0], start=True, stop=True)
                    pe.matmul(ps[:, b, SSM_HEADS:2 * SSM_HEADS], upto[:], a_sb[:, 1], start=True, stop=True)\
                        .then_inc(exp_ready, 1)
                elif kind == "cb":
                    g = step[1]
                    b = group()
                    pe.wait_ge(sem("silu_out"), CONV_T // 2)
                    pe.matmul(ps[:, b, 0:T], bcT[:, g, 0:P], bcT[:, GROUPS + g], start=True, stop=True)
                    pe.matmul(ps[:, b, T:T + P], bcT[:, g, P:T], bcT[:, GROUPS + g, P:T], start=True, stop=True)\
                        .then_inc(misc_ready, 1)
                elif kind == "spread":
                    u, g, t, d = step[1:]
                    n_exp = 1 + 2 * u + d
                    b = exp_bank(n_exp)
                    pe.wait_ge(sem("steps_ready"), n_exp)
                    pe.matmul(ps[:, b, :], after[:], work[:, 2 + d], start=True, stop=True).then_inc(exp_ready, 1)
                elif kind == "ssm":
                    u, g, t = step[1:]
                    if t == 1:
                        b = group()
                        pe.matmul(ps[:, b, :], cbm[:, g % 2, 2 * P:3 * P], fx[:, g * GW:(g + 1) * GW],
                                  start=True, stop=True).then_inc(misc_ready, 1)
                    b = group()
                    pe.wait_ge(sem("weighed"), 2 * u + 2)
                    pe.wait_ge(sem("xdt_ready"), 10)
                    for r in range(8):
                        hc = slice(g * GW + r * SSM_DIM, g * GW + (r + 1) * SSM_DIM)
                        last = pe.matmul(ps[:, b, r * SSM_DIM:(r + 1) * SSM_DIM],
                                         work[:, r // 4, (r % 4) * P:(r % 4 + 1) * P], xdt[t][:, hc],
                                         start=True, stop=True)
                    last.then_inc(misc_ready, 1)
                elif kind == "yT":
                    pe.wait_ge(sem("y_normed"), TT)
                    for c2 in range(2 * step[1], 2 * step[1] + 2):
                        by_columns(lambda t: xs[t], c2)
                elif kind == "outT":
                    pe.wait_ge(sem("out_scaled"), 2 * step[1] + 2)
                    for c2 in range(2 * step[1], 2 * step[1] + 2):
                        by_columns(lambda t: h2[:, t], c2)
                elif kind == "logits":
                    pe.wait_ge(misc_taken, MISC_AT[("outT", step[1])] + 2)
                    pe.wait_ge(exp_taken, 1 + 2 * N_UNITS)
                    for t in range(TT):
                        for c in range(4 * step[1], 4 * step[1] + 4):
                            last = pe.matmul(ps[:, EXP_BANK, t * EXPERTS:(t + 1) * EXPERTS],
                                             h2T[:, c, t * P:(t + 1) * P], wr_sb[:, c], start=(c == 0 and t == 0),
                                             stop=(c == KC - 1), skip_group_check=True)
                    if step[1] == 1:
                        last.then_inc(exp_ready, 1)
                elif kind == "mergedT":
                    pe.wait_ge(sem("br_merged"), 10 + 2 * step[1])
                    for c2 in range(2 * step[1], 2 * step[1] + 2):
                        by_columns(lambda t: merged[:, t], c2)

            pe.wait_ge(sem("chosen_ready"), 1)
            b = group()
            pe.matmul(ps[:, b, 0:EXPERTS], upto_r[:], chosen_r[:, 0], start=True, stop=True)
            pe.matmul(ps[:, b, EXPERTS:2 * EXPERTS], upto_r[:], chosen_r[:, 1], start=True, stop=False)
            pe.matmul(ps[:, b, EXPERTS:2 * EXPERTS], ones_r[:], chosen_r[:, 0], start=False, stop=True)
            for t in range(TT):
                last = pe.matmul(ps[:, b, 64:64 + EXPERTS], ones_r[:], chosen_r[:, t], start=(t == 0), stop=(t == 1))
            last.then_inc(misc_ready, 1)
            pe.wait_ge(gemm_taken, GEMM_END)
            for bank in ACC:
                pe.matmul(ps[:, bank, 0:1], ident[:], after[:, P - 1:P], start=True, stop=False, skip_group_check=True)

            def gather():
                for c in range(KC):
                    for t in range(TT):
                        last = pe.matmul(ps[:, X_BANK, c * BLK:(c + 1) * BLK], h2[:, t, c * P:(c + 1) * P], hot[:, t],
                                         start=(t == 0), stop=(t == TT - 1))
                last.then_inc(sem("gather_ready"), 1)

            def scatter(n, signal=None):
                pe.wait_ge(sem("yb_ready"), n + 1)
                for t in range(TT):
                    for h in range(2):
                        last = pe.matmul(ps[:, ACC[2 * t + h], :], hot_wT[:, h, t], yb, start=False, stop=False,
                                         skip_group_check=True)
                        if signal is not None:
                            last.then_inc(signal, 1)

            pe.wait_ge(sem("hot_ready"), TT)
            pe.wait_ge(sem("hot_wT_zero"), 1)
            pe.wait_ge(sem("h2_ready"), TT)
            pe.wait_ge(misc_taken, MISC_END)
            gather()
            pe.wait_ge(sem("bias_rows_landed"), 48)
            pe.wait_ge(exp_taken, 1 + 2 * N_UNITS + TT)
            pe.wait_ge(sem("passes_known"), 1)
            n_pass = pe.value_load(npass_i[0:1, 0:1], min_val=1, max_val=PASSES)
            with pe.Fori(0, n_pass) as b_:
                with pe.Fori(0, EXPERTS // ROUND) as j_:
                    j = b_ * (EXPERTS // ROUND) + j_
                    for r in range(ROUND):
                        i = j * ROUND + r
                        pe.wait_ge(sem("pick_ready"), i + 1)
                        pe.wait_ge(sem("xg_ready"), i + 1)
                        for k in range(4):
                            bank, (slot, turns) = (G_BANK, U_BANK)[k % 2], place(r, k)
                            pe.wait_ge(e_landed[slot], (j * TURNS + turns + 1) * 16)
                            for c in range(KC // 2):
                                for h in range(2):
                                    last = pe.matmul(ps[64 * h:64 * h + 64, bank, :], xgT[:, k // 2 * 4 + c],
                                                     eslots[slot][:, c, h * NB:(h + 1) * NB], start=(k < 2 and c == 0),
                                                     stop=(k >= 2 and c == 3), skip_group_check=True)
                            last.then_inc(e_used[slot], 1)
                            if k < 2:
                                for h in range(2):
                                    cols = slice(k * D + h * NB, k * D + (h + 1) * NB)
                                    pe.matmul(ps[64 * h:64 * h + 64, bank, :], pick, bias_gu[:, cols],
                                              start=False, stop=False, skip_group_check=True)
                        scatter(i)
                        pe.wait_ge(sem("hot_w_ready"), i * TT + TT)
                        for t in range(TT):
                            last = turn(ps[:, D_BANK, t * P:(t + 1) * P], hot_w[:, t].rearrange("p r j -> p (r j)"))
                        last.then_inc(sem("hot_wT_ready"), 1)
                        pe.wait_ge(sem("act_ready"), i + 1)
                        for c in range(4):
                            last = turn(ps[:, G_BANK, c * P:(c + 1) * P], act_sb[:, c * P:(c + 1) * P])
                        last.then_inc(sem("actT_out"), 1)
                        pe.wait_ge(sem("hot_ready"), i * TT + 2 * TT)
                        gather()
                        pe.wait_ge(sem("actT_ready"), i + 1)
                        pe.wait_ge(sem("scatter_ready"), i * 2 + 2)
                        for h in range(2):
                            pe.matmul(ps[64 * h:64 * h + 64, D_BANK, :], pick, bias_d[:, h * NB:(h + 1) * NB],
                                      start=True, stop=False, skip_group_check=True)
                        for k in range(2):
                            slot, turns = place(r, 4 + k)
                            pe.wait_ge(e_landed[slot], (j * TURNS + turns + 1) * 16)
                            for c in range(4):
                                for h in range(2):
                                    last = pe.matmul(ps[64 * h:64 * h + 64, D_BANK, :], actT[:, c, 64 * k:64 * k + 64],
                                                     eslots[slot][:, c, h * NB:(h + 1) * NB],
                                                     start=False, stop=(k == 1 and c == 3), skip_group_check=True)
                            last.then_inc(e_used[slot], 1)
            scatter(n_pass * EXPERTS, sem("sums_ready"))


def kernel(**inputs):
    import numpy as np
    import concourse.bacc as bacc
    from concourse.bass_utils import run_bass_kernel_spmd

    src = {k: np.asarray(v) for k, v in inputs.items()}
    one = {k: v[0] for k, v in src.items() if k not in ("x", "mem")}

    def columns(v):
        return np.ascontiguousarray(v.reshape(-1, P).T)

    args = {
        "x": src["x"], "mem": src["mem"], "g_mix": one["norm_mix"], "w_in": one["w_in"],
        "w_dt": np.ascontiguousarray(one["w_in"][:, DT0:DT0 + SSM_HEADS]),
        "a_gains": np.stack([np.concatenate([one["a_q_gain"]] * 2), np.concatenate([one["a_k_gain"]] * 2)], 1),
        "rel_rev": np.ascontiguousarray(one["a_rel_bias"][:, ::-1]),
        "conv_w": np.ascontiguousarray(one["conv_w"].reshape(TAPS, CONV_T, P).transpose(2, 1, 0)),
        "conv_b": columns(one["conv_b"]), "dt_bias": one["dt_bias"], "a_log": one["a_log"], "d_skip": one["d_skip"],
        "g_ssm": columns(one["ssm_norm"]), "g_mem": columns(one["norm_mem"]), "w_mem_kv": one["w_mem_kv"],
        "x_gains": np.concatenate([columns(one["x_q_gain"]), columns(one["x_k_gain"])], 1),
        "w_br_a": one["w_br_a"], "w_br_b": one["w_br_b"], "w_br_c": one["w_br_c"], "w_out": one["w_out"],
        "norm_ffn": one["norm_ffn"], "w_router": one["w_router"], "b_router": one["b_router"],
        "w_gate": one["w_gate"], "b_gate": one["b_gate"], "w_up": one["w_up"], "b_up": one["b_up"],
        "w_down": one["w_down"], "b_down": one["b_down"],
    }
    nc = bacc.Bacc("TRN2", target_bir_lowering=False, num_devices=1)
    arrays, aps = {}, []
    for name, a in args.items():
        a = np.ascontiguousarray(a)
        arrays["in_" + name] = a
        aps.append(nc.dram_tensor("in_" + name, a.shape, mybir.dt.from_np(a.dtype), kind="ExternalInput").ap())
    aps.append(nc.dram_tensor("bias_rows", (A_HEADS, P * (SKEW + 1)), F32).ap())
    aps.append(nc.dram_tensor("out_0", (1, T, D), F32, kind="ExternalOutput").ap())
    hybrid_block_kernel(nc, *aps)
    r = run_bass_kernel_spmd(nc, [arrays], core_ids=[0])
    return r.results[0]["out_0"]
```
